# Optimizing a Trainium2 kernel written in Bass

```python
import math
import jax, jax.numpy as jnp
from jax import lax
import numpy as np

D_MODEL = 1024
BATCH = 1
SEQ = 512
DEPTH = 1

D_MIX = D_MODEL
DA_HEADS = 4
DA_HEAD_DIM = 64
DA_V_DIM = 2 * DA_HEAD_DIM
DA_WIDTH = DA_HEADS * DA_V_DIM
RW_HEAD = 64
RW_WIDTH = D_MIX - DA_WIDTH
RW_HEADS = RW_WIDTH // RW_HEAD
DECAY_LORA = 64
AAA_LORA = 64
GATE_LORA = 128
DA_COLS = 3 * DA_WIDTH
RW_COLS = 3 * RW_WIDTH + DECAY_LORA + AAA_LORA + GATE_LORA
IN_COLS = DA_COLS + RW_COLS
ROPE_THETA = 10000.0
Q_BLOCK = 128
N_EXPERTS = 32
TOP_K = 4
D_FF = D_MODEL
SWIGLU_ALPHA = 1.702
SWIGLU_LIMIT = 7.0
MOE_BLOCK = 128
NORM_EPS = 1e-5
GN_EPS = 64e-5

kernel_name = "hybrid_diffattn_rwkv7_moe"

F32 = jnp.float32

def rmsnorm(x, w):
    x32 = x.astype(F32)
    y = x32 * lax.rsqrt(jnp.mean(x32 * x32, axis=-1, keepdims=True) + NORM_EPS)
    return (y * w.astype(F32)).astype(x.dtype)

def rope_tables(positions):
    inv = ROPE_THETA ** (-jnp.arange(0, DA_HEAD_DIM, 2, dtype=F32) / DA_HEAD_DIM)
    ang = positions.astype(F32)[..., None] * inv
    return jnp.cos(ang), jnp.sin(ang)

def apply_rope(x, cos, sin):
    c = cos[:, :, None, None, :]
    s = sin[:, :, None, None, :]
    x1, x2 = jnp.split(x.astype(F32), 2, axis=-1)
    return jnp.concatenate([x1 * c - x2 * s, x2 * c + x1 * s], axis=-1).astype(x.dtype)

def diff_attention(q, k, v, lam, lam_init, subln_w):
    B, S = q.shape[0], q.shape[1]
    nb = S // Q_BLOCK
    scale = DA_HEAD_DIM ** -0.5
    kt = jnp.transpose(k, (0, 2, 3, 1, 4))
    vt = jnp.transpose(v, (0, 2, 1, 3))
    qb = q.reshape(B, nb, Q_BLOCK, DA_HEADS, 2, DA_HEAD_DIM).transpose(1, 0, 3, 4, 2, 5)
    key_pos = jnp.arange(S)

    def block(args):
        qi, i = args
        s = jnp.einsum('bhcqd,bhckd->bhcqk', qi, kt, preferred_element_type=F32) * scale
        qpos = i * Q_BLOCK + jnp.arange(Q_BLOCK)
        s = jnp.where(key_pos[None, :] <= qpos[:, None], s, -jnp.inf)
        p = jax.nn.softmax(s, axis=-1)
        a = p[:, :, 0] - lam * p[:, :, 1]
        return jnp.einsum('bhqk,bhkd->bhqd', a.astype(vt.dtype), vt)

    o = lax.map(block, (qb, jnp.arange(nb)))
    o = o.transpose(1, 0, 3, 2, 4).reshape(B, S, DA_HEADS, DA_V_DIM)
    o = rmsnorm(o, subln_w) * (1.0 - lam_init)
    return o.reshape(B, S, DA_WIDTH)

def rwkv7_scan(r, w, k, v, kk, a):
    B, S_len, H, N = r.shape

    def step(st, inp):
        r_t, w_t, k_t, v_t, kk_t, a_t = inp
        sa = jnp.einsum('bhvk,bhk->bhv', st, kk_t)
        st = (st * w_t[:, :, None, :]
              - sa[..., None] * (kk_t * a_t)[:, :, None, :]
              + v_t[..., None] * k_t[:, :, None, :])
        y = jnp.einsum('bhvk,bhk->bhv', st, r_t)
        return st, y

    xs = tuple(jnp.moveaxis(t.astype(F32), 1, 0) for t in (r, w, k, v, kk, a))
    st0 = jnp.zeros((B, H, N, N), F32)
    _, y = lax.scan(step, st0, xs)
    return jnp.moveaxis(y, 0, 1)

def rwkv7_group(p, mu, w0, w2, a0, a2, g2, k_k, k_a, r_k, lnx_w, lnx_b):
    B, S = p.shape[0], p.shape[1]
    prev = jnp.pad(p, ((0, 0), (1, 0), (0, 0)))[:, :-1]
    p = p + mu * (prev - p)
    c0, c1, c2 = RW_WIDTH, 2 * RW_WIDTH, 3 * RW_WIDTH
    c3, c4 = c2 + DECAY_LORA, c2 + DECAY_LORA + AAA_LORA
    r, k, v, wd, ad, gd = jnp.split(p, [c0, c1, c2, c3, c4], axis=-1)
    wlog = -jax.nn.softplus(-(w0 + jnp.tanh(wd) @ w2).astype(F32)) - 0.5
    decay = jnp.exp(-jnp.exp(wlog))
    a = jax.nn.sigmoid((a0 + ad @ a2).astype(F32))
    g = jax.nn.sigmoid(gd) @ g2
    heads = lambda t: t.reshape(B, S, RW_HEADS, RW_HEAD)
    kk = heads((k * k_k).astype(F32))
    kk = kk / jnp.maximum(jnp.sqrt(jnp.sum(kk * kk, axis=-1, keepdims=True)), 1e-12)
    k = k.astype(F32) * (1.0 + (a - 1.0) * k_a.astype(F32))
    rh, kh, vh, ah = heads(r.astype(F32)), heads(k), heads(v.astype(F32)), heads(a)
    y = rwkv7_scan(rh, heads(decay), kh, vh, kk, ah)
    mean = jnp.mean(y, axis=-1, keepdims=True)
    var = jnp.mean(jnp.square(y - mean), axis=-1, keepdims=True)
    yn = ((y - mean) * lax.rsqrt(var + GN_EPS)).reshape(B, S, RW_WIDTH)
    yn = yn * lnx_w.astype(F32) + lnx_b.astype(F32)
    bonus = jnp.sum(rh * kh * r_k.astype(F32), axis=-1, keepdims=True) * vh
    out = (yn + bonus.reshape(B, S, RW_WIDTH)) * g.astype(F32)
    return out.astype(p.dtype)

def moe_ffn(h, router_w, router_b, mlp1_w, mlp1_b, mlp2_w, mlp2_b):
    B, S, D = h.shape
    T = B * S
    xf = h.reshape(T, D)
    logits = (xf @ router_w + router_b).astype(F32)
    top_val, top_idx = lax.top_k(logits, TOP_K)
    gates = jax.nn.softmax(top_val, axis=-1)
    M = T * TOP_K
    e_flat = top_idx.reshape(M)
    tok_flat = jnp.arange(M, dtype=jnp.int32) // TOP_K
    gate_flat = gates.reshape(M)
    order = jnp.argsort(e_flat)
    e_s, tok_s, gate_s = e_flat[order], tok_flat[order], gate_flat[order]
    counts = jnp.bincount(e_flat, length=N_EXPERTS)
    start = jnp.cumsum(counts) - counts
    padded = (counts + MOE_BLOCK - 1) // MOE_BLOCK * MOE_BLOCK
    pend = jnp.cumsum(padded)
    pstart = pend - padded
    dest = pstart[e_s] + (jnp.arange(M) - start[e_s])
    P = M + N_EXPERTS * MOE_BLOCK
    row_tok = jnp.full((P,), T, jnp.int32).at[dest].set(tok_s)
    row_gate = jnp.zeros((P,), F32).at[dest].set(gate_s)
    nblk = P // MOE_BLOCK
    blk_expert = jnp.minimum(jnp.searchsorted(pend, jnp.arange(nblk) * MOE_BLOCK, side='right'), N_EXPERTS - 1)
    x_pad = jnp.concatenate([xf, jnp.zeros((1, D), xf.dtype)], axis=0)

    def block(args):
        toks, e = args
        xb = x_pad[toks]
        gu = xb @ mlp1_w[e] + mlp1_b[e]
        gate, up = gu[..., ::2], gu[..., 1::2]
        gate = jnp.minimum(gate, SWIGLU_LIMIT)
        up = jnp.clip(up, -SWIGLU_LIMIT, SWIGLU_LIMIT)
        act = (up + 1.0) * gate * jax.nn.sigmoid(SWIGLU_ALPHA * gate)
        return act @ mlp2_w[e] + mlp2_b[e]

    y = lax.map(block, (row_tok.reshape(nblk, MOE_BLOCK), blk_expert)).reshape(P, D)
    y = (y.astype(F32) * row_gate[:, None]).astype(h.dtype)
    out = jnp.zeros((T + 1, D), h.dtype).at[row_tok].add(y)[:T]
    return out.reshape(B, S, D)

def setup_inputs(seed: int = 0) -> dict:
    key = jax.random.key(seed)
    ks = jax.random.split(key, 32)
    L = DEPTH
    nrm = lambda k, shape, scale: jax.random.normal(k, shape, F32) * scale
    uni = lambda k, shape, lo, hi: jax.random.uniform(k, shape, F32, lo, hi)
    return {
        'x': nrm(ks[0], (BATCH, SEQ, D_MODEL), 1.0),
        'positions': jnp.broadcast_to(jnp.arange(SEQ, dtype=jnp.int32), (BATCH, SEQ)),
        'attn_norm_w': 1.0 + nrm(ks[1], (L, D_MODEL), 0.02),
        'w_in': nrm(ks[2], (L, D_MODEL, IN_COLS), D_MODEL ** -0.5),
        'shift_mu': uni(ks[3], (L, RW_COLS), 0.0, 1.0),
        'lambda_q1': nrm(ks[4], (L, DA_HEAD_DIM), 0.1),
        'lambda_k1': nrm(ks[5], (L, DA_HEAD_DIM), 0.1),
        'lambda_q2': nrm(ks[6], (L, DA_HEAD_DIM), 0.1),
        'lambda_k2': nrm(ks[7], (L, DA_HEAD_DIM), 0.1),
        'subln_w': 1.0 + nrm(ks[8], (L, DA_V_DIM), 0.02),
        'rw_w0': uni(ks[9], (L, RW_WIDTH), -6.0, 0.0),
        'rw_w2': nrm(ks[10], (L, DECAY_LORA, RW_WIDTH), 0.1 * DECAY_LORA ** -0.5),
        'rw_a0': nrm(ks[11], (L, RW_WIDTH), 0.5),
        'rw_a2': nrm(ks[12], (L, AAA_LORA, RW_WIDTH), AAA_LORA ** -0.5),
        'rw_g2': nrm(ks[13], (L, GATE_LORA, RW_WIDTH), GATE_LORA ** -0.5),
        'rw_k_k': 0.85 + nrm(ks[14], (L, RW_WIDTH), 0.02),
        'rw_k_a': 1.0 + nrm(ks[15], (L, RW_WIDTH), 0.02),
        'rw_r_k': nrm(ks[16], (L, RW_HEADS, RW_HEAD), 0.1),
        'rw_lnx_w': 1.0 + nrm(ks[17], (L, RW_WIDTH), 0.02),
        'rw_lnx_b': nrm(ks[18], (L, RW_WIDTH), 0.01),
        'w_out': nrm(ks[19], (L, D_MIX, D_MODEL), D_MIX ** -0.5),
        'ffn_norm_w': 1.0 + nrm(ks[20], (L, D_MODEL), 0.02),
        'router_w': nrm(ks[21], (L, D_MODEL, N_EXPERTS), D_MODEL ** -0.5),
        'router_b': nrm(ks[22], (L, N_EXPERTS), 0.01),
        'mlp1_w': nrm(ks[23], (L, N_EXPERTS, D_MODEL, 2 * D_FF), D_MODEL ** -0.5),
        'mlp1_b': nrm(ks[24], (L, N_EXPERTS, 2 * D_FF), 0.01),
        'mlp2_w': nrm(ks[25], (L, N_EXPERTS, D_FF, D_MODEL), D_FF ** -0.5),
        'mlp2_b': nrm(ks[26], (L, N_EXPERTS, D_MODEL), 0.01),
        'final_norm_w': 1.0 + nrm(ks[27], (D_MODEL,), 0.02),
    }

def reference(x, positions, attn_norm_w, w_in, shift_mu, lambda_q1, lambda_k1, lambda_q2, lambda_k2,
              subln_w, rw_w0, rw_w2, rw_a0, rw_a2, rw_g2, rw_k_k, rw_k_a, rw_r_k, rw_lnx_w, rw_lnx_b,
              w_out, ffn_norm_w, router_w, router_b, mlp1_w, mlp1_b, mlp2_w, mlp2_b, final_norm_w):
    B, S = x.shape[0], x.shape[1]
    cos, sin = rope_tables(positions)
    for l in range(DEPTH):
        h = rmsnorm(x, attn_norm_w[l])
        p = h @ w_in[l]
        q, k, v, p_rw = jnp.split(p, [DA_WIDTH, 2 * DA_WIDTH, 3 * DA_WIDTH], axis=-1)
        q = apply_rope(q.reshape(B, S, DA_HEADS, 2, DA_HEAD_DIM), cos, sin)
        k = apply_rope(k.reshape(B, S, DA_HEADS, 2, DA_HEAD_DIM), cos, sin)
        v = v.reshape(B, S, DA_HEADS, DA_V_DIM)
        lam_init = 0.8 - 0.6 * math.exp(-0.3 * l)
        lam = (jnp.exp(jnp.sum(lambda_q1[l].astype(F32) * lambda_k1[l].astype(F32)))
               - jnp.exp(jnp.sum(lambda_q2[l].astype(F32) * lambda_k2[l].astype(F32))) + lam_init)
        o_da = diff_attention(q, k, v, lam, lam_init, subln_w[l])
        o_rw = rwkv7_group(p_rw, shift_mu[l], rw_w0[l], rw_w2[l], rw_a0[l], rw_a2[l], rw_g2[l],
                           rw_k_k[l], rw_k_a[l], rw_r_k[l], rw_lnx_w[l], rw_lnx_b[l])
        x = x + jnp.concatenate([o_da, o_rw.astype(o_da.dtype)], axis=-1) @ w_out[l]
        h = rmsnorm(x, ffn_norm_w[l])
        x = x + moe_ffn(h, router_w[l], router_b[l], mlp1_w[l], mlp1_b[l], mlp2_w[l], mlp2_b[l])
    return rmsnorm(x, final_norm_w)


_drawn_inputs = setup_inputs


def setup_inputs(seed=0):
    import zlib

    import numpy as np

    out = dict(_drawn_inputs(seed))
    spreads = {}
    factors = {'rw_w2': 4.49,
     'rw_k_k': 3.197,
     'rw_k_a': 3.497,
     'rw_lnx_w': 3.203,
     'rw_lnx_b': 4.143,
     'mlp1_b': 8.0,
     'mlp2_b': 8.0,
     'final_norm_w': 3.118}
    for name, (base, spread) in spreads.items():
        noise = np.random.default_rng([zlib.crc32(name.encode()), seed]).standard_normal(out[name].shape)
        drawn = base * np.exp(spread * noise) if base else spread * noise
        out[name] = __import__('jax').numpy.asarray(drawn.astype(out[name].dtype))
    for name, factor in factors.items():
        out[name] = (out[name] * factor).astype(out[name].dtype)
    return out
```

```python
from contextlib import ExitStack

import numpy as np

import concourse.bass as bass
from concourse import mybir

F32 = mybir.dt.float32
F32R = mybir.dt.float32r
I32 = mybir.dt.int32
U32 = mybir.dt.uint32
ALU = mybir.AluOpType
ACT = mybir.ActivationFunctionType
AX = mybir.AxisListType

P = 128
D = 1024
S = 512
NT = S // P
KT = D // P
IN_TILES = 26
HEADS = 4
CH = 64
NCH = S // CH
LEVELS = (2, 4, 8, 16, 32)
NORM_EPS = 1e-5
GN_EPS = 64e-5
LAM_INIT = 0.8 - 0.6 * 1.0
E_HALF = float(np.exp(-0.5))
EXPERTS = 32
TURNS = EXPERTS + 1
PIECES = 12
RAW = 6
RING = 4
ROUNDS = S // P
BIG = float(1 << 20)
NPAR = 10
NEG = -1e30


def constant_tables():
    p = np.arange(P)[:, None]
    c = np.arange(P)[None, :]
    same = p // CH == c // CH
    m1 = (same & (p < c)).astype(np.float32)
    m2 = (same & (p <= c)).astype(np.float32)
    level = [((p // (2 * b) == c // (2 * b)) & ((p // b) % 2 == 1) & ((c // b) % 2 == 0)) for b in LEVELS]
    t = np.arange(S)[None, :]
    inv = (np.float32(10000.0) ** (-np.arange(0, 64, 2, dtype=np.float32) / np.float32(64))).astype(np.float32)
    parts = {
        "ident": p == c,
        "mask_b": np.concatenate([m1, -m2], 1),
        "mask_k": np.concatenate([m1, m2], 1),
        "level1": (p // 2 == c // 2) & (p % 2 == 0) & (c % 2 == 1),
        "levels": np.concatenate(level, 1),
        "stack": p % CH == np.arange(CH)[None, :],
        "heads": same,
        "swap": p == (c ^ 32),
        "causal": np.where(np.arange(S)[None, :] - 3 * P > p, NEG, 0.0),
        "reset": np.broadcast_to(t % CH != 0, (P, S)),
        "before": p < c,
        "ones": np.ones((P, P)),
        "slot": np.broadcast_to(c, (P, P)),
        "token": np.arange(NT)[None, :] * P + p,
        "experts": np.broadcast_to(np.arange(EXPERTS)[None, :], (P, EXPERTS)),
        "pick": ((p % EXPERTS) == np.arange(TURNS)[None, :]) & (p < 2 * EXPERTS),
        "inv": inv[np.arange(P) % 32][:, None],
        "sign": np.where(np.arange(P)[:, None] % 64 < 32, -1.0, 1.0),
        "eps": np.full((P, 1), NORM_EPS),
        "gn_eps": np.full((P, 1), GN_EPS),
    }
    at, out, n = {}, [], 0
    for name, a in parts.items():
        a = np.asarray(a, np.float32)
        at[name] = (n, n + a.shape[1])
        n += a.shape[1]
        out.append(a)
    return np.ascontiguousarray(np.concatenate(out, 1)), at


class Steps:

    def __init__(self, sem, names):
        self.sem, self.names, self.next = sem, list(names), 0

    def step(self, name):
        assert self.names[self.next] == name, (self.names[self.next], name)
        self.next += 1
        return 1

    def reached(self, j, name):
        return j * len(self.names) + (self.names.index(name) + 2)

    def turn_before(self, j):
        return j * len(self.names) + 1


def build_program(nc, d, out):
    _, at = constant_tables()
    with ExitStack() as top:
        def sb(stack, name, shape, dt=F32):
            return stack.enter_context(nc.sbuf_tensor(name, shape, dt))

        def sem(name):
            return top.enter_context(nc.semaphore(name))

        psum = top.enter_context(nc.psum_tensor("psum", [P, 8, 512], F32))
        cst = sb(top, "cst", [P, d["cst"].shape[1]])
        cols = sb(top, "cols", [P, d["cols"].shape[1]])
        x = sb(top, "x", [P, NT, D])
        stat = sb(top, "stat", [P, 64])

        def con(name, a=0, b=None):
            lo, hi = at[name]
            return cst[:, lo + a:(lo + b if b is not None else hi)]

        ident = con("ident")

        def bank(n, a=0, b=512, rows=slice(0, P)):
            return psum[rows, n, a:b]

        h2_dram = nc.dram_tensor("h2_rows", (S, D), F32, kind="Internal").ap()
        y_dram = nc.dram_tensor("expert_rows", (4 * S, D), F32, kind="Internal").ap()
        rank = sb(top, "rank", [P, NT, TURNS])
        info = sb(top, "info", [P, NT, TURNS, 4])
        flags = sb(top, "flags", [P, ROUNDS], I32)

        with ExitStack() as mixer:
            o_t = sb(mixer, "o_t", [P, 2 * HEADS, S])
            with ExitStack() as st:
                pall = sb(st, "pall", [P, IN_TILES, S + 1])
                cosb = sb(st, "cosb", [P, S])
                sinb = sb(st, "sinb", [P, S])
                g = dict(cst=cst, cols=cols, x=x, stat=stat, pall=pall, cosb=cosb, sinb=sinb, o_t=o_t)
                project(nc, d, sb, sem, g, con, ident, psum, bank)
                mix(nc, d, sb, sem, st, g, con, ident, psum, bank)
            output_and_route(nc, d, sb, sem, mixer, dict(x=x, stat=stat, o_t=o_t, rank=rank, info=info, flags=flags,
                                                         h2_dram=h2_dram), con, ident, psum, bank)
        with ExitStack() as st:
            experts(nc, d, sb, sem, st, dict(stat=stat, rank=rank, info=info, flags=flags, h2_dram=h2_dram, y_dram=y_dram),
                    con, ident, psum, bank)
        with ExitStack() as st:
            combine(nc, d, sb, sem, st, dict(x=x, stat=stat, y_dram=y_dram), con, out)


def project(nc, d, sb, sem, g, con, ident, psum, bank):
    cst, cols, x, stat, pall, cosb, sinb = (g[k] for k in ("cst", "cols", "x", "stat", "pall", "cosb", "sinb"))
    s_cst, s_cols, s_lam, s_pos = sem("cst_loaded"), sem("cols_loaded"), sem("lam_loaded"), sem("pos_loaded")
    s_x = [sem(f"x_loaded{t}") for t in range(NT)]
    s_w = [sem(f"w_in_loaded{u}") for u in range(2)]
    s_sq, s_sd, s_rstd, s_xn = sem("x_squared"), sem("x_deviation"), sem("x_rstd"), sem("x_normed")
    s_xt, s_hh, s_hl = sem("x_turned"), sem("h_hi"), sem("h_lo")
    s_whi, s_wlo, s_prod, s_out = sem("w_hi"), sem("w_lo"), sem("projected"), sem("p_copied")
    s_zero, s_rope, s_lam1, s_ang = sem("p_zeroed"), sem("rope_steps"), sem("lam_steps"), sem("angles_done")
    s_trig, s_lex = sem("trig_done"), sem("lam_exp")
    with ExitStack() as st:
        xn = sb(st, "xn", [P, NT, D])
        h_hi = sb(st, "h_hi_sb", [P, KT, S], F32R)
        h_lo = sb(st, "h_lo_sb", [P, KT, S], F32R)
        w_raw = sb(st, "w_raw", [P, 2, KT, P])
        w_hi = sb(st, "w_hi_sb", [P, 2, KT, P], F32R)
        w_lo = sb(st, "w_lo_sb", [P, 2, KT, P], F32R)
        posi = sb(st, "posi", [P, S], I32)
        ang = sb(st, "ang", [P, S])
        turns = sb(st, "turns", [P, S])
        lam = sb(st, "lam", [P, 4, 64])
        lamp = sb(st, "lamp", [P, 64])
        w_v = d["w_in"][0].rearrange("(k p) n -> p k n", p=P)
        x_v = d["x"][0].rearrange("(t p) c -> p t c", p=P)
        block = st.enter_context(nc.Block())

        @block.sync
        def _(sp):
            for t in range(NT):
                sp.dma_start(x[:, t, :], x_v[:, t, :]).then_inc(s_x[t], 16)
            with sp.Fori(0, IN_TILES // 2) as i:
                for u in range(2):
                    sp.wait_ge(s_wlo, i * 2 + (u + 1))
                    sp.dma_start(w_raw[:, u], w_v[:, :, bass.ds(i * 256 + u * P, P)]).then_inc(s_w[u], 16)

        @block.gpsimd
        def _(pool):
            nc.gpsimd.dma_start(cst[:], d["cst"]).then_inc(s_cst, 16)
            nc.gpsimd.dma_start(cols[:], d["cols"]).then_inc(s_cols, 16)
            nc.gpsimd.dma_start(posi[:], d["positions"].to_broadcast([P, S])).then_inc(s_pos, 16)
            nc.gpsimd.dma_start(lam[:].rearrange("p a b -> p (a b)"), d["lam"].to_broadcast([P, 256])).then_inc(s_lam, 16)
            nc.gpsimd.memset(pall[:, :, 0:1], 0.0).then_inc(s_zero, 1)
            pool.wait_ge(s_zero, 1)

        @block.scalar
        def _(act):
            for t in range(NT):
                act.wait_ge(s_x[t], 16)
                last = nc.scalar.activation(xn[:, t, :], x[:, t, :], ACT.Square, accum_out=stat[:, t:t + 1])
            last.then_inc(s_sq, 1)
            act.wait_ge(s_sq, 1)
            act.wait_ge(s_cst, 16)
            nc.scalar.activation(stat[:, 4:8], stat[:, 0:4], ACT.Sqrt, bias=con("eps"), scale=1.0 / D).then_inc(s_sd, 1)
            act.wait_ge(s_cols, 16)

            def split(i, u):
                act.wait_ge(s_w[u], i * 16 + 16)
                act.wait_ge(s_prod, i * 2 + (u + 1))
                nc.scalar.activation(w_hi[:, u], w_raw[:, u], ACT.Copy).then_inc(s_whi, 1)

            def copy_out(n, u):
                act.wait_ge(s_prod, n + 3)
                nc.scalar.activation(pall[:, bass.ds(n, 1), 1:S + 1].rearrange("p a s -> p (a s)"), bank(u), ACT.Copy).then_inc(s_out, 1)

            split(0, 0)
            split(0, 1)
            for k in range(KT):
                act.wait_ge(s_xt, k + 1)
                nc.scalar.activation(h_hi[:, k, :], bank(k), ACT.Copy, scale=cols[:, k:k + 1]).then_inc(s_hh, 1)
            with act.Fori(1, IN_TILES // 2) as i:
                for u in range(2):
                    split(i, u)
                    copy_out(i * 2 + (u - 2), u)
            for u in range(2):
                copy_out(IN_TILES - 2 + u, u)
            act.wait_ge(s_ang, 2)
            nc.scalar.activation(cosb[:], ang[:], ACT.Sin)
            nc.scalar.activation(sinb[:], turns[:], ACT.Sin).then_inc(s_trig, 1)
            act.wait_ge(s_lam1, 2)
            nc.scalar.activation(stat[:, 18:20], stat[:, 16:18], ACT.Exp).then_inc(s_lex, 1)

        @block.vector
        def _(dve):
            nc.vector.memset(stat[:, 63:64], 0.0).then_inc(s_wlo, 2)
            dve.wait_ge(s_sd, 1)
            nc.vector.reciprocal(stat[:, 8:12], stat[:, 4:8]).then_inc(s_rstd, 1)
            dve.wait_ge(s_rstd, 1)
            for t in range(NT):
                nc.vector.tensor_scalar(xn[:, t, :], x[:, t, :], stat[:, 8 + t:9 + t], None, ALU.mult).then_inc(s_xn, 1)

            def split(i, u):
                dve.wait_ge(s_whi, i * 2 + (u + 1))
                nc.vector.tensor_tensor(w_lo[:, u], w_raw[:, u], w_hi[:, u].bitcast(F32), ALU.subtract).then_inc(s_wlo, 1)

            split(0, 0)
            split(0, 1)
            for k in range(KT):
                dve.wait_ge(s_hh, k + 1)
                nc.vector.scalar_tensor_tensor(h_lo[:, k, :], bank(k), cols[:, k:k + 1], h_hi[:, k, :].bitcast(F32),
                                               ALU.mult, ALU.subtract).then_inc(s_hl, 1)
            with dve.Fori(1, IN_TILES // 2) as i:
                for u in range(2):
                    split(i, u)
            dve.wait_ge(s_pos, 16)
            step = 0

            def chain(ins):
                nonlocal step
                step += 1
                ins.then_inc(s_rope, 1)
                dve.wait_ge(s_rope, step)

            two_pi = 2 * np.pi
            c1 = 6.28125
            c2 = float(np.float32(two_pi - c1) - np.float32(two_pi - c1) % np.float32(2.0 ** -20))
            c3 = float(two_pi - c1 - c2)
            chain(nc.vector.tensor_copy(cosb[:], posi[:]))
            chain(nc.vector.tensor_scalar(sinb[:], cosb[:], con("inv"), None, ALU.mult))
            for dst, shift in ((ang, 0.25), (turns, 0.0)):
                chain(nc.vector.tensor_scalar(cosb[:], sinb[:], float(1 / two_pi), shift, ALU.mult, ALU.add))
                chain(nc.vector.tensor_scalar(cosb[:], cosb[:], 12582912.0, None, ALU.add))
                chain(nc.vector.tensor_scalar(cosb[:], cosb[:], 12582912.0, None, ALU.subtract))
                chain(nc.vector.scalar_tensor_tensor(dst[:], cosb[:], -c1, sinb[:], ALU.mult, ALU.add))
                chain(nc.vector.scalar_tensor_tensor(dst[:], cosb[:], -c2, dst[:], ALU.mult, ALU.add))
                chain(nc.vector.scalar_tensor_tensor(dst[:], cosb[:], -c3, dst[:], ALU.mult, ALU.add))
                if shift:
                    chain(nc.vector.tensor_scalar(dst[:], dst[:], float(np.pi / 2), None, ALU.add))
                chain(nc.vector.tensor_scalar(dst[:], dst[:], 3.1415925, -3.1415925, ALU.min, ALU.max))
                nc.vector.memset(stat[:, 62:63], 0.0).then_inc(s_ang, 1)
            dve.wait_ge(s_lam, 16)
            for n in range(2):
                if n:
                    dve.wait_ge(s_lam1, n)
                nc.vector.tensor_tensor_reduce(lamp[:], lam[:, 2 * n, :], lam[:, 2 * n + 1, :], 1.0, 0.0, ALU.mult, ALU.add,
                                               stat[:, 16 + n:17 + n]).then_inc(s_lam1, 1)
            dve.wait_ge(s_lex, 1)
            chain(nc.vector.tensor_tensor(stat[:, 20:21], stat[:, 19:20], stat[:, 18:19], ALU.subtract))
            chain(nc.vector.tensor_scalar(stat[:, 21:22], stat[:, 20:21], -LAM_INIT, None, ALU.add))
            dve.wait_ge(s_trig, 1)
            chain(nc.vector.tensor_scalar(sinb[:], sinb[:], con("sign"), None, ALU.mult))

        @block.tensor
        def _(pe):
            pe.wait_ge(s_cst, 16)
            pe.wait_ge(s_xn, NT)
            for k in range(KT):
                for t in range(NT):
                    last = nc.tensor.transpose(bank(k, t * P, t * P + P), xn[:, t, k * P:(k + 1) * P], ident)
                if k == 0:
                    pe.sem_inc(s_prod, 2)
                last.then_inc(s_xt, 1)
            pe.wait_ge(s_hl, KT)

            def tile(n, i, u):
                pe.wait_ge(s_wlo, n + 3)
                for k in range(KT):
                    pairs = ((w_hi, h_hi), (w_hi, h_lo), (w_lo, h_hi))
                    for m, (w, h) in enumerate(pairs):
                        last = nc.tensor.matmul(bank(u), w[:, u, k, :], h[:, k, :], start=k == 0 and m == 0,
                                                stop=k == KT - 1 and m == 2)
                last.then_inc(s_prod, 1)

            for u in range(2):
                tile(u, 0, u)
            with pe.Fori(1, IN_TILES // 2) as i:
                for u in range(2):
                    pe.wait_ge(s_out, i * 2 + (u - 1))
                    tile(i * 2 + u, i, u)


MIX_PE = (["rope_swap", "v_turn"] + [f"{a}{i}" for i in range(NT) for a in ("score", "a_turn", "o")] + ["o_turn"]
          + ["lora", "kk_sum", "bonus", "t_kappa", "t_beta", "t_khat", "t_v"]
          + ["mb0", "mk0", "mb1", "mk1", "x_turn0", "x_turn1"]
          + [f"{a}{lv}_{h}" for lv in range(5) for a in ("t", "x") for h in range(2)]
          + ["akv", "wu0", "wu1", "q", "chunk"] + [f"z{c}" for c in range(1, 7)] + ["y", "y_turn"])
MIX_ACT = (["v_copy", "params", "v_major"] + [f"{a}{i}" for i in range(NT) for a in ("exp", "a_major")] + ["o_ss", "o_sd"]
           + ["sig", "exps", "kk_sq", "kk_norm", "e_kappa", "e_beta", "e_khat", "e_v", "x_major0", "x_major1",
              "e_akv", "e_wu0", "e_wu1", "y_sd"])
MIX_DVE = (["qc", "qs", "q", "kc", "ks", "k"]
           + [f"{a}{i}" for i in range(NT) for a in ("masked", "max", "rl", "nl", "p2", "a")]
           + ["o_rs", "o_n", "o_out", "shift", "mix_", "lsum", "lprev", "kk0", "kk_max", "kk_inv", "kk",
              "kappa", "b", "beta", "am", "kmod", "khat", "rhat", "rk", "bon"]
           + [f"{a}{h}" for h in range(2) for a in ("emb", "emk", "x1a", "x1b")]
           + [f"{a}{lv}_{h}" for lv in range(5) for a in ("et", "ex") for h in range(2)]
           + ["eg", "eh", "e_q"] + [f"z{c}" for c in range(1, 8)]
           + ["y_sum", "y_mean", "y_c", "y_sq", "y_var", "y_rs", "y_n", "ot1", "ot2", "ot3"])


def mix(nc, d, sb, sem, st, g, con, ident, psum, bank):
    cols, stat, pall, cosb, sinb, o_t = (g[k] for k in ("cols", "stat", "pall", "cosb", "sinb", "o_t"))
    PE = Steps(sem("mix_tensor_steps"), MIX_PE)
    AC = Steps(sem("mix_scalar_steps"), MIX_ACT)
    DV = Steps(sem("mix_vector_steps"), MIX_DVE)
    s_lora, s_set, s_set2, s_gp = sem("lora_loaded"), sem("mix_set"), sem("mix_set2"), sem("mix_zeroed")
    lw = sb(st, "lora_w", [P, 2, S])
    wa = sb(st, "wa", [P, S])
    sg = sb(st, "sg", [P, S])
    par = sb(st, "par", [P, NPAR])
    lj = sb(st, "lj", [P, 2, P])
    rkv = sb(st, "rkv", [P, 3, S])
    w3 = sb(st, "w3", [P, 3, S])
    r_, k_, v_ = rkv[:, 0, :], rkv[:, 1, :], rkv[:, 2, :]
    lsum, lprev, kk = w3[:, 0, :], w3[:, 1, :], w3[:, 2, :]
    sg_w = sb(st, "sg_w", [P, S])
    gate = sb(st, "gate", [P, S])
    aa = sb(st, "aa", [P, S])
    pe_ = sb(st, "p_end", [P, S])
    pi_ = sb(st, "p_inv", [P, S])
    pp_ = sb(st, "p_prev", [P, S])
    sq = sb(st, "sq", [P, S])
    beta = sb(st, "beta", [P, S])
    khat = sb(st, "khat", [P, S])
    kr = sb(st, "kr", [P, NT, 2, P])
    ab = sb(st, "ab", [P, 2, NT, 2, P])
    ak = sb(st, "ak", [P, 2, NT, 2, P])
    xx = sb(st, "xx", [P, 2, NT, 2, P])
    t1 = sb(st, "t1", [P, 2, NT, P])
    bn = sb(st, "bn", [P, NT, P])
    kh = sb(st, "kh", [P, NT, P])
    vt = sb(st, "vt", [P, NT, P])
    rh = sb(st, "rh", [P, 2, NT, P])
    wu = sb(st, "wu", [P, 2, NT, P])
    gt = sb(st, "gt", [P, NCH, P])
    zz = sb(st, "zz", [P, NCH, CH])
    hp = t1[:, 0].rearrange("p t c -> p (t c)").rearrange("p (n k) -> p n k", k=CH)
    qt = t1[:, 1]
    yc, ysq, yn = pe_, pi_, pp_
    vf = sb(st, "vf", [P, S])
    vm = sb(st, "vm", [P, NT, P])
    qr = sb(st, "qr", [P, S])
    kro = sb(st, "kro", [P, S])
    sc = sb(st, "sc", [P, 2, S])
    am, at_ = beta, khat
    on = vf
    ast = sb(st, "ast", [P, 48])
    pg = pall[:, 0:24, :].rearrange("p (g j) t -> p g j t", j=HEADS)

    def tile_of(group, j, shift=1):
        return pg[:, group, bass.ds(j, 1), shift:shift + S].rearrange("p a s -> p (a s)")

    block = st.enter_context(nc.Block())

    @block.sync
    def _(sp):
        sp.dma_start(lw[:, 0, :], d["w2a2"]).then_inc(s_lora, 16)
        sp.dma_start(lw[:, 1, :], d["g2"]).then_inc(s_lora, 16)

    @block.gpsimd
    def _(pool):
        nc.gpsimd.memset(gt[:], 0.0)
        nc.gpsimd.memset(zz[:, 0, :], 0.0).then_inc(s_gp, 1)
        pool.wait_ge(s_gp, 1)

    @block.scalar
    def _(act):
        act.wait_ge(s_set, 2)
        nc.scalar.activation(wa[0:64], sq[0:64], ACT.Tanh)
        nc.scalar.activation(wa[64:128], sq[64:128], ACT.Copy)
        nc.scalar.activation(sg[:], aa[:], ACT.Sigmoid).then_inc(AC.sem, 1)
        act.wait_ge(s_lora, 32)
        with act.Fori(0, HEADS) as j:
            act.wait_ge(DV.sem, DV.turn_before(j))
            act.wait_ge(PE.sem, PE.turn_before(j))
            act.wait_ge(AC.sem, AC.turn_before(j))
            nc.scalar.activation(vf[:], tile_of(2, j), ACT.Copy).then_inc(AC.sem, AC.step("v_copy"))
            base = KT + 2
            nc.scalar.activation(par[:], cols[:, bass.ds(j * NPAR + base, NPAR)], ACT.Copy)
            nc.scalar.activation(lj[:], lw[:, :, bass.ds(j * P, P)], ACT.Copy).then_inc(AC.sem, AC.step("params"))
            act.wait_ge(PE.sem, PE.reached(j, "v_turn"))
            nc.scalar.activation(vm[:].rearrange("p a b -> p (a b)"), bank(2), ACT.Copy).then_inc(AC.sem, AC.step("v_major"))
            for i in range(NT):
                n = (i + 1) * P
                act.wait_ge(DV.sem, DV.reached(j, f"max{i}"))
                for c in range(2):
                    last = nc.scalar.activation(sc[:, c, 0:n], sc[:, c, 0:n], ACT.Exp, bias=ast[:, 2 * i + c:2 * i + c + 1],
                                                accum_out=ast[:, 8 + 2 * i + c:9 + 2 * i + c])
                last.then_inc(AC.sem, AC.step(f"exp{i}"))
                act.wait_ge(PE.sem, PE.reached(j, f"a_turn{i}"))
                nc.scalar.activation(at_[:, 0:n], bank(2, 0, n), ACT.Copy).then_inc(AC.sem, AC.step(f"a_major{i}"))
            act.wait_ge(PE.sem, PE.reached(j, f"o{NT - 1}"))
            act.wait_ge(DV.sem, DV.reached(j, f"a{NT - 1}"))
            for i in range(NT):
                last = nc.scalar.activation(sc[:, 0, i * P:(i + 1) * P], bank(3, i * P, i * P + P), ACT.Square,
                                            accum_out=ast[:, 24 + i:25 + i])
            last.then_inc(AC.sem, AC.step("o_ss"))
            act.wait_ge(AC.sem, AC.reached(j, "o_ss"))
            nc.scalar.activation(ast[:, 28:32], ast[:, 24:28], ACT.Sqrt, bias=con("eps"), scale=1.0 / P).then_inc(AC.sem, AC.step("o_sd"))
            act.wait_ge(PE.sem, PE.reached(j, "lora"))
            nc.scalar.activation(sg_w[:], bank(4), ACT.Sigmoid, bias=par[:, 3:4])
            nc.scalar.activation(aa[:], bank(5), ACT.Sigmoid, bias=par[:, 4:5])
            nc.scalar.activation(gate[:], bank(6), ACT.Copy).then_inc(AC.sem, AC.step("sig"))
            act.wait_ge(DV.sem, DV.reached(j, "lprev"))
            nc.scalar.activation(pe_[:], lsum, ACT.Exp, scale=-E_HALF)
            nc.scalar.activation(pi_[:], lsum, ACT.Exp, scale=E_HALF)
            nc.scalar.activation(pp_[:], lprev, ACT.Exp, scale=-E_HALF).then_inc(AC.sem, AC.step("exps"))
            act.wait_ge(DV.sem, DV.reached(j, "kk0"))
            nc.scalar.activation(sq[:], kk, ACT.Square).then_inc(AC.sem, AC.step("kk_sq"))
            act.wait_ge(PE.sem, PE.reached(j, "kk_sum"))
            nc.scalar.activation(sq[:], bank(7), ACT.Sqrt).then_inc(AC.sem, AC.step("kk_norm"))
            act.wait_ge(PE.sem, PE.reached(j, "t_kappa"))
            for h in range(2):
                last = nc.scalar.activation(rh[:, h, :, 0:64], bank(4).rearrange("p (t h c) -> p t h c", h=2, c=64)[:, :, h, :], ACT.Copy)
            last.then_inc(AC.sem, AC.step("e_kappa"))
            act.wait_ge(PE.sem, PE.reached(j, "t_beta"))
            nc.scalar.activation(bn[:].rearrange("p a b -> p (a b)"), bank(5), ACT.Copy, scale=-1.0).then_inc(AC.sem, AC.step("e_beta"))
            act.wait_ge(PE.sem, PE.reached(j, "t_khat"))
            nc.scalar.activation(kh[:].rearrange("p a b -> p (a b)"), bank(6), ACT.Copy).then_inc(AC.sem, AC.step("e_khat"))
            act.wait_ge(PE.sem, PE.reached(j, "t_v"))
            nc.scalar.activation(vt[:].rearrange("p a b -> p (a b)"), bank(7), ACT.Copy).then_inc(AC.sem, AC.step("e_v"))
            for h in range(2):
                act.wait_ge(PE.sem, PE.reached(j, f"x_turn{h}"))
                nc.scalar.activation(xx[:, h, :, 0, :], bank(4 + h).rearrange("p (t c) -> p t c", c=P), ACT.Copy).then_inc(
                    AC.sem, AC.step(f"x_major{h}"))
            act.wait_ge(PE.sem, PE.reached(j, "akv"))
            nc.scalar.activation(rh[:, :, :, 64:128].rearrange("p h t c -> p (h t) c"),
                                 bank(4).rearrange("p (u c) -> p u c", c=64), ACT.Copy).then_inc(AC.sem, AC.step("e_akv"))
            for h in range(2):
                act.wait_ge(PE.sem, PE.reached(j, f"wu{h}"))
                nc.scalar.activation(wu[:, h].rearrange("p t c -> p (t c)"), bank(5 + h), ACT.Copy).then_inc(AC.sem, AC.step(f"e_wu{h}"))
            act.wait_ge(DV.sem, DV.reached(j, "y_var"))
            nc.scalar.activation(ast[:, 40:48], ast[:, 32:40], ACT.Sqrt, bias=con("gn_eps"), scale=1.0 / CH).then_inc(AC.sem, AC.step("y_sd"))

    @block.vector
    def _(dve):
        for n, dst in ((0, sq), (1, aa)):
            t = 24 + n
            nc.vector.tensor_tensor(w3[:, n, :], pall[:, t, 0:S], pall[:, t, 1:S + 1], ALU.subtract).then_inc(s_set2, 1)
            dve.wait_ge(s_set2, n + 1)
            nc.vector.scalar_tensor_tensor(dst[:], w3[:, n, :], cols[:, KT + n:KT + n + 1], pall[:, t, 1:S + 1],
                                           ALU.mult, ALU.add).then_inc(s_set, 1)
        dve.wait_ge(s_set, 2)
        nc.vector.memset(ast[:, 0:1], 0.0).then_inc(DV.sem, 1)
        with dve.Fori(0, HEADS) as j:
            dve.wait_ge(DV.sem, DV.turn_before(j))
            dve.wait_ge(PE.sem, PE.turn_before(j))
            dve.wait_ge(AC.sem, AC.turn_before(j))

            def own(name):
                dve.wait_ge(DV.sem, DV.reached(j, name))

            for n, (a, group, dst) in enumerate((("q", 0, qr), ("k", 1, kro))):
                nc.vector.tensor_tensor(dst[:], tile_of(group, j), cosb[:], ALU.mult).then_inc(DV.sem, DV.step(a + "c"))
                if n == 0:
                    dve.wait_ge(PE.sem, PE.reached(j, "rope_swap"))
                nc.vector.tensor_tensor(sc[:, n, :], bank(n), sinb[:], ALU.mult).then_inc(DV.sem, DV.step(a + "s"))
                own(a + "s")
                nc.vector.tensor_tensor(dst[:], dst[:], sc[:, n, :], ALU.add).then_inc(DV.sem, DV.step(a))
            for i in range(NT):
                n = (i + 1) * P
                dve.wait_ge(PE.sem, PE.reached(j, f"score{i}"))
                own(f"a{i - 1}" if i else "k")
                mask = con("causal", (NT - 1 - i) * P, S)
                nc.vector.scalar_tensor_tensor(sc[:, :, 0:n], psum[:, 0:2, 0:n], 0.125,
                                               mask.rearrange("p (a n) -> p a n", a=1).to_broadcast([P, 2, n]),
                                               ALU.mult, ALU.add).then_inc(DV.sem, DV.step(f"masked{i}"))
                own(f"masked{i}")
                nc.vector.tensor_reduce(ast[:, 2 * i:2 * i + 2], sc[:, :, 0:n], AX.X, ALU.max, negate=True).then_inc(
                    DV.sem, DV.step(f"max{i}"))
                dve.wait_ge(AC.sem, AC.reached(j, f"exp{i}"))
                nc.vector.reciprocal(ast[:, 16:18], ast[:, 8 + 2 * i:10 + 2 * i]).then_inc(DV.sem, DV.step(f"rl{i}"))
                own(f"rl{i}")
                nc.vector.tensor_tensor(ast[:, 18:19], ast[:, 17:18], stat[:, 21:22], ALU.mult).then_inc(DV.sem, DV.step(f"nl{i}"))
                own(f"nl{i}")
                nc.vector.tensor_scalar(sc[:, 1, 0:n], sc[:, 1, 0:n], ast[:, 18:19], None, ALU.mult).then_inc(DV.sem, DV.step(f"p2{i}"))
                own(f"p2{i}")
                if i:
                    dve.wait_ge(PE.sem, PE.reached(j, f"a_turn{i - 1}"))
                nc.vector.scalar_tensor_tensor(am[:, 0:n], sc[:, 0, 0:n], ast[:, 16:17], sc[:, 1, 0:n], ALU.mult,
                                               ALU.add).then_inc(DV.sem, DV.step(f"a{i}"))
            dve.wait_ge(AC.sem, AC.reached(j, "o_sd"))
            nc.vector.reciprocal(ast[:, 20:24], ast[:, 28:32]).then_inc(DV.sem, DV.step("o_rs"))
            own("o_rs")
            for i in range(NT):
                last = nc.vector.tensor_scalar(on[:, i * P:(i + 1) * P], bank(3, i * P, i * P + P), ast[:, 20 + i:21 + i],
                                               1.0 - LAM_INIT, ALU.mult, ALU.mult)
            last.then_inc(DV.sem, DV.step("o_n"))
            dve.wait_ge(PE.sem, PE.reached(j, "o_turn"))
            nc.vector.tensor_scalar(o_t[:, bass.ds(j, 1), :].rearrange("p a s -> p (a s)"), bank(2),
                                    cols[:, KT + 2 + HEADS * NPAR:KT + 3 + HEADS * NPAR], None, ALU.mult).then_inc(DV.sem, DV.step("o_out"))
            nc.vector.tensor_tensor(w3[:], pg[:, 3:6, bass.ds(j, 1), 0:S].rearrange("p g a s -> p g (a s)"),
                                    pg[:, 3:6, bass.ds(j, 1), 1:S + 1].rearrange("p g a s -> p g (a s)"),
                                    ALU.subtract).then_inc(DV.sem, DV.step("shift"))
            own("shift")
            for n in range(3):
                last = nc.vector.scalar_tensor_tensor(rkv[:, n, :], w3[:, n, :], par[:, n:n + 1], tile_of(3 + n, j),
                                                      ALU.mult, ALU.add)
            last.then_inc(DV.sem, DV.step("mix_"))
            own("mix_")
            dve.wait_ge(AC.sem, AC.reached(j, "sig"))
            nc.vector.tensor_tensor_scan(lsum, con("reset"), sg_w[:], 0.0, ALU.mult, ALU.add).then_inc(DV.sem, DV.step("lsum"))
            own("lsum")
            nc.vector.tensor_tensor(lprev, lsum, sg_w[:], ALU.subtract).then_inc(DV.sem, DV.step("lprev"))
            nc.vector.tensor_scalar(kk, k_, par[:, 5:6], None, ALU.mult).then_inc(DV.sem, DV.step("kk0"))
            dve.wait_ge(AC.sem, AC.reached(j, "kk_norm"))
            nc.vector.tensor_scalar(sq[:], sq[:], 1e-12, None, ALU.max).then_inc(DV.sem, DV.step("kk_max"))
            own("kk_max")
            nc.vector.reciprocal(sq[:], sq[:]).then_inc(DV.sem, DV.step("kk_inv"))
            own("kk_inv")
            nc.vector.tensor_tensor(kk, kk, sq[:], ALU.mult).then_inc(DV.sem, DV.step("kk"))
            own("kk")

            def tiles(a):
                return a.rearrange("p (t c) -> p t c", c=P)

            nc.vector.tensor_tensor(kr[:, :, 0, :], tiles(kk), tiles(pp_[:]), ALU.mult).then_inc(DV.sem, DV.step("kappa"))
            nc.vector.tensor_tensor(sq[:], kk, aa[:], ALU.mult).then_inc(DV.sem, DV.step("b"))
            own("b")
            nc.vector.tensor_tensor(beta[:], sq[:], pi_[:], ALU.mult).then_inc(DV.sem, DV.step("beta"))
            nc.vector.tensor_scalar(aa[:], aa[:], 1.0, par[:, 6:7], ALU.subtract, ALU.mult).then_inc(DV.sem, DV.step("am"))
            own("am")
            nc.vector.scalar_tensor_tensor(k_, aa[:], 1.0, k_, ALU.add, ALU.mult).then_inc(DV.sem, DV.step("kmod"))
            own("kmod")
            nc.vector.tensor_tensor(khat[:], k_, pi_[:], ALU.mult).then_inc(DV.sem, DV.step("khat"))
            nc.vector.tensor_tensor(kr[:, :, 1, :], tiles(r_), tiles(pe_[:]), ALU.mult).then_inc(DV.sem, DV.step("rhat"))
            own("rhat")
            nc.vector.scalar_tensor_tensor(r_, r_, par[:, 7:8], k_, ALU.mult, ALU.mult).then_inc(DV.sem, DV.step("rk"))
            dve.wait_ge(PE.sem, PE.reached(j, "bonus"))
            nc.vector.tensor_tensor(r_, bank(7), v_, ALU.mult).then_inc(DV.sem, DV.step("bon"))
            for h in range(2):
                for a, b0, dst, msk in (("b", 0, ab, "mask_b"), ("k", 2, ak, "mask_k")):
                    dve.wait_ge(PE.sem, PE.reached(j, f"m{a}{h}"))
                    nc.vector.tensor_tensor(dst[:, h].rearrange("p t a c -> p t (a c)"),
                                            psum[:, b0:b0 + 2, :].rearrange("p b (t c) -> p (b t) c", c=2 * P),
                                            con(msk).rearrange("p (a n) -> p a n", a=1).to_broadcast([P, NT, 2 * P]),
                                            ALU.mult).then_inc(DV.sem, DV.step(f"em{a}{h}"))
                own(f"emk{h}")
                nc.vector.tensor_tensor(t1[:, h], ab[:, h, :, 0, :],
                                        con("level1").rearrange("p (a n) -> p a n", a=1).to_broadcast([P, NT, P]),
                                        ALU.mult).then_inc(DV.sem, DV.step(f"x1a{h}"))
                own(f"x1a{h}")
                nc.vector.tensor_tensor(xx[:, h, :, 1, :], ident.rearrange("p (a n) -> p a n", a=1).to_broadcast([P, NT, P]),
                                        t1[:, h], ALU.subtract).then_inc(DV.sem, DV.step(f"x1b{h}"))
            for lv in range(5):
                for h in range(2):
                    dve.wait_ge(PE.sem, PE.reached(j, f"t{lv}_{h}"))
                    nc.vector.tensor_tensor(t1[:, h], bank(4 + h).rearrange("p (t c) -> p t c", c=P),
                                            con("levels", lv * P, lv * P + P).rearrange("p (a n) -> p a n", a=1).to_broadcast([P, NT, P]),
                                            ALU.mult).then_inc(DV.sem, DV.step(f"et{lv}_{h}"))
                for h in range(2):
                    dve.wait_ge(PE.sem, PE.reached(j, f"x{lv}_{h}"))
                    src = psum[:, 2 * h:2 * h + 2, :].rearrange("p b (t a c) -> p (b t) a c", a=2, c=P)
                    if lv < 4:
                        nc.vector.tensor_tensor(xx[:, h], xx[:, h], src, ALU.subtract).then_inc(DV.sem, DV.step(f"ex{lv}_{h}"))
                    else:
                        nc.vector.tensor_tensor(xx[:, h, :, 1, :], xx[:, h, :, 1, :], src[:, :, 1, :], ALU.subtract).then_inc(
                            DV.sem, DV.step(f"ex{lv}_{h}"))
            dve.wait_ge(s_gp, 1)
            dve.wait_ge(PE.sem, PE.reached(j, "chunk"))
            for h in range(2):
                rows = slice(64 * h, 64 * h + 64)
                last = nc.vector.tensor_tensor(
                    gt[rows, :, 64 * h:64 * h + 64].rearrange("p (t c) k -> p c t k", c=2),
                    psum[rows, 0:2, 0:256].rearrange("p c (t k) -> p c t k", k=64),
                    con("stack")[rows].rearrange("p (a b k) -> p a b k", a=1, b=1).to_broadcast([64, 2, NT, 64]), ALU.add)
            last.then_inc(DV.sem, DV.step("eg"))
            decay_end = pe_[:].rearrange("p (t c k) -> p c t k", c=2, k=64)[:, :, :, 63:64]
            nc.vector.tensor_tensor(hp[:].rearrange("p (t c) k -> p c t k", c=2),
                                    psum[:, 0:2, 256:512].rearrange("p c (t k) -> p c t k", k=64),
                                    decay_end.to_broadcast([P, 2, NT, 64]), ALU.mult).then_inc(DV.sem, DV.step("eh"))
            dve.wait_ge(PE.sem, PE.reached(j, "q"))
            nc.vector.tensor_tensor(qt[:], bank(3).rearrange("p (t c) -> p t c", c=P), kr[:, :, 1, :], ALU.add).then_inc(
                DV.sem, DV.step("e_q"))
            own("eh")
            nc.vector.tensor_copy(zz[:, 1, :], hp[:, 0, :]).then_inc(DV.sem, DV.step("z1"))
            for c in range(1, 7):
                dve.wait_ge(PE.sem, PE.reached(j, f"z{c}"))
                nc.vector.scalar_tensor_tensor(zz[:, c + 1, :], bank(2, c * 64, c * 64 + 64), pe_[:, 64 * c + 63:64 * c + 64],
                                               hp[:, c, :], ALU.mult, ALU.add).then_inc(DV.sem, DV.step(f"z{c + 1}"))
            own("z7")
            dve.wait_ge(PE.sem, PE.reached(j, "y"))
            yb = psum[:, 6:8, 0:256].rearrange("p h (t v) -> p h t v", v=64)
            y4 = yc[:].rearrange("p (h t v) -> p h t v", h=2, v=64)
            nc.vector.tensor_reduce(ast[:, 32:40], yb, AX.X, ALU.add).then_inc(DV.sem, DV.step("y_sum"))
            own("y_sum")
            nc.vector.tensor_scalar(ast[:, 40:48], ast[:, 32:40], -1.0 / CH, None, ALU.mult).then_inc(DV.sem, DV.step("y_mean"))
            own("y_mean")

            def per_head(a):
                return a.rearrange("p (h t v) -> p h t v", h=2, v=1).to_broadcast([P, 2, NT, 64])

            nc.vector.tensor_tensor(y4, yb, per_head(ast[:, 40:48]), ALU.add).then_inc(DV.sem, DV.step("y_c"))
            own("y_c")
            nc.vector.tensor_tensor(ysq[:], yc[:], yc[:], ALU.mult).then_inc(DV.sem, DV.step("y_sq"))
            own("y_sq")
            nc.vector.tensor_reduce(ast[:, 32:40], ysq[:].rearrange("p (u v) -> p u v", v=64), AX.X, ALU.add).then_inc(
                DV.sem, DV.step("y_var"))
            dve.wait_ge(AC.sem, AC.reached(j, "y_sd"))
            nc.vector.reciprocal(ast[:, 32:40], ast[:, 40:48]).then_inc(DV.sem, DV.step("y_rs"))
            own("y_rs")
            nc.vector.tensor_tensor(yn[:].rearrange("p (t h v) -> p h t v", h=2, v=64), y4, per_head(ast[:, 32:40]),
                                    ALU.mult).then_inc(DV.sem, DV.step("y_n"))
            dve.wait_ge(PE.sem, PE.reached(j, "y_turn"))
            nc.vector.tensor_scalar(kk, bank(4), par[:, 8:9], par[:, 9:10], ALU.mult, ALU.add).then_inc(DV.sem, DV.step("ot1"))
            own("ot1")
            nc.vector.tensor_tensor(kk, kk, r_, ALU.add).then_inc(DV.sem, DV.step("ot2"))
            own("ot2")
            nc.vector.tensor_tensor(o_t[:, bass.ds(j + HEADS, 1), :].rearrange("p a s -> p (a s)"), kk, gate[:], ALU.mult).then_inc(
                DV.sem, DV.step("ot3"))

    @block.tensor
    def _(pe):
        pe.wait_ge(AC.sem, 1)
        pe.sem_inc(PE.sem, 1)
        with pe.Fori(0, HEADS) as j:
            pe.wait_ge(DV.sem, DV.turn_before(j))
            pe.wait_ge(AC.sem, AC.turn_before(j))

            def dv(name):
                pe.wait_ge(DV.sem, DV.reached(j, name))

            def ac(name):
                pe.wait_ge(AC.sem, AC.reached(j, name))

            nc.tensor.matmul(bank(0), con("swap"), tile_of(0, j), start=True, stop=True)
            nc.tensor.matmul(bank(1), con("swap"), tile_of(1, j), start=True, stop=True).then_inc(PE.sem, PE.step("rope_swap"))
            ac("v_copy")
            for t in range(NT):
                last = nc.tensor.transpose(bank(2, t * P, t * P + P), vf[:, t * P:(t + 1) * P], ident)
            last.then_inc(PE.sem, PE.step("v_turn"))
            dv("k")
            ac("v_major")
            for i in range(NT):
                n = (i + 1) * P
                if i:
                    dv(f"masked{i - 1}")
                for c in range(2):
                    rows = slice(64 * c, 64 * c + 64)
                    last = nc.tensor.matmul(bank(c, 0, n), qr[rows, i * P:(i + 1) * P], kro[rows, 0:n], start=True, stop=True)
                last.then_inc(PE.sem, PE.step(f"score{i}"))
                dv(f"a{i}")
                if i:
                    ac(f"a_major{i - 1}")
                for b in range(i + 1):
                    last = nc.tensor.transpose(bank(2, b * P, b * P + P), am[:, b * P:(b + 1) * P], ident)
                last.then_inc(PE.sem, PE.step(f"a_turn{i}"))
                ac(f"a_major{i}")
                for b in range(i + 1):
                    last = nc.tensor.matmul(bank(3, i * P, i * P + P), at_[:, b * P:(b + 1) * P], vm[:, b, :], start=b == 0, stop=b == i)
                last.then_inc(PE.sem, PE.step(f"o{i}"))
            dv("o_n")
            for t in range(NT):
                last = nc.tensor.transpose(bank(2, t * P, t * P + P), on[:, t * P:(t + 1) * P], ident)
            last.then_inc(PE.sem, PE.step("o_turn"))
            ac("params")
            nc.tensor.matmul(bank(4), lj[0:64, 0, :], wa[0:64, :], start=True, stop=True)
            nc.tensor.matmul(bank(5), lj[64:128, 0, :], wa[64:128, :], start=True, stop=True)
            nc.tensor.matmul(bank(6), lj[:, 1, :], sg[:], start=True, stop=True).then_inc(PE.sem, PE.step("lora"))
            ac("kk_sq")
            nc.tensor.matmul(bank(7), con("heads"), sq[:], start=True, stop=True).then_inc(PE.sem, PE.step("kk_sum"))
            dv("rk")
            nc.tensor.matmul(bank(7), con("heads"), r_, start=True, stop=True).then_inc(PE.sem, PE.step("bonus"))
            for name, b, src in (("t_kappa", 4, lambda t: kr[:, t, 0, :]), ("t_beta", 5, lambda t: beta[:, t * P:(t + 1) * P]),
                                 ("t_khat", 6, lambda t: khat[:, t * P:(t + 1) * P]), ("t_v", 7, lambda t: v_[:, t * P:(t + 1) * P])):
                if name == "t_v":
                    dv("bon")
                for t in range(NT):
                    last = nc.tensor.transpose(bank(b, t * P, t * P + P), src(t), ident)
                last.then_inc(PE.sem, PE.step(name))
            dv("o_out")
            for h in range(2):
                rows = slice(64 * h, 64 * h + 64)
                for a, b0, src in (("b", 0, beta), ("k", 2, khat)):
                    if h:
                        dv(f"em{a}0")
                    for t in range(NT):
                        c0 = (t % 2) * 2 * P
                        last = nc.tensor.matmul(bank(b0 + t // 2, c0, c0 + 2 * P), src[rows, t * P:(t + 1) * P],
                                                kr[rows, t, :, :].rearrange("p a c -> p (a c)"), start=True, stop=True)
                    last.then_inc(PE.sem, PE.step(f"m{a}{h}"))
            ac("e_v")
            for h in range(2):
                dv(f"x1b{h}")
                for t in range(NT):
                    last = nc.tensor.transpose(bank(4 + h, t * P, t * P + P), xx[:, h, t, 1, :], ident)
                last.then_inc(PE.sem, PE.step(f"x_turn{h}"))
            for lv in range(5):
                for h in range(2):
                    if lv == 0:
                        ac(f"x_major{h}")
                    else:
                        dv(f"ex{lv - 1}_{h}")
                    for t in range(NT):
                        last = nc.tensor.matmul(bank(4 + h, t * P, t * P + P), ab[:, h, t, 0, :], xx[:, h, t, 0, :], start=True, stop=True)
                    last.then_inc(PE.sem, PE.step(f"t{lv}_{h}"))
                for h in range(2):
                    dv(f"et{lv}_{h}")
                    for t in range(NT):
                        b, c0 = 2 * h + t // 2, (t % 2) * 2 * P
                        if lv < 4:
                            nc.tensor.matmul(bank(b, c0, c0 + P), xx[:, h, t, 1, :], t1[:, h, t, :], start=True, stop=True)
                        last = nc.tensor.matmul(bank(b, c0 + P, c0 + 2 * P), t1[:, h, t, :], xx[:, h, t, 1, :], start=True, stop=True)
                    last.then_inc(PE.sem, PE.step(f"x{lv}_{h}"))
            dv("ex4_1")
            for h in range(2):
                for t in range(NT):
                    u = h * NT + t
                    last = nc.tensor.matmul(bank(4, u * 64, u * 64 + 64), ak[:, h, t, 0, :], vt[:, t, 64 * h:64 * h + 64], start=True, stop=True)
            last.then_inc(PE.sem, PE.step("akv"))
            ac("e_akv")
            for h in range(2):
                for t in range(NT):
                    last = nc.tensor.matmul(bank(5 + h, t * P, t * P + P), xx[:, h, t, 1, :], rh[:, h, t, :], start=True, stop=True)
                last.then_inc(PE.sem, PE.step(f"wu{h}"))
            ac("e_wu1")
            for h in range(2):
                for t in range(NT):
                    last = nc.tensor.matmul(bank(3, t * P, t * P + P, slice(64 * h, 64 * h + 64)), wu[:, h, t, 0:64], ab[:, h, t, 1, :],
                                            start=True, stop=True)
            last.then_inc(PE.sem, PE.step("q"))
            for c in range(2):
                tok = slice(64 * c, 64 * c + 64)
                for h in range(2):
                    hs, rows = slice(64 * h, 64 * h + 64), slice(64 * h, 64 * h + 64)
                    for t in range(NT):
                        nc.tensor.matmul(bank(c, t * 64, t * 64 + 64, rows), wu[tok, h, t, 0:64], bn[tok, t, hs], start=True, stop=True)
                        o = bank(c, 256 + t * 64, 320 + t * 64, rows)
                        nc.tensor.matmul(o, kh[tok, t, hs], vt[tok, t, hs], start=True, stop=False)
                        last = nc.tensor.matmul(o, bn[tok, t, hs], wu[tok, h, t, 64:128], start=False, stop=True)
            last.then_inc(PE.sem, PE.step("chunk"))
            for c in range(1, 7):
                dv(f"z{c}")
                nc.tensor.matmul(bank(2, c * 64, c * 64 + 64), gt[:, c, :], zz[:, c, :], start=True, stop=True).then_inc(
                    PE.sem, PE.step(f"z{c}"))
            dv("z7")
            for h in range(2):
                rows = slice(64 * h, 64 * h + 64)
                for t in range(NT):
                    o = bank(6 + h, t * 64, t * 64 + 64)
                    nc.tensor.matmul(o, ak[:, h, t, 1, :], vt[:, t, rows], start=True, stop=False)
                    nc.tensor.matmul(o, ab[:, h, t, 1, :], wu[:, h, t, 64:128], start=False, stop=False)
                    for c in range(2):
                        tok = slice(64 * c, 64 * c + 64)
                        last = nc.tensor.matmul(bank(6 + h, t * 64, t * 64 + 64, tok), qt[rows, t, tok], zz[rows, 2 * t + c, :],
                                                start=False, stop=True)
            last.then_inc(PE.sem, PE.step("y"))
            dv("y_n")
            for t in range(NT):
                last = nc.tensor.transpose(bank(4, t * P, t * P + P), yn[:, t * P:(t + 1) * P], ident)
            last.then_inc(PE.sem, PE.step("y_turn"))


def output_and_route(nc, d, sb, sem, st, g, con, ident, psum, bank):
    x, stat, o_t, rank, info, flags = (g[k] for k in ("x", "stat", "o_t", "rank", "info", "flags"))
    s_w = [sem(f"w_out_loaded{k}") for k in range(KT)]
    s_rw, s_fw, s_oh, s_ol = sem("router_loaded"), sem("ffn_norm_loaded"), sem("o_hi"), sem("o_lo")
    s_wh, s_wl, s_acc, s_x2, s_ss = sem("w_out_hi"), sem("w_out_lo"), sem("out_projected"), sem("x2_ready"), sem("x2_squared")
    s_sd, s_rs, s_h2, s_store = sem("x2_deviation"), sem("x2_rstd"), sem("h2_ready"), sem("h2_stored")
    s_turn, s_h2t, s_log, s_rt = sem("h2_turned"), sem("h2t_ready"), sem("logits_ready"), sem("route_steps")
    s_exp, s_mask, s_rank = sem("gate_exp"), sem("choice_mask"), sem("ranks_ready")
    wo = sb(st, "wo_raw", [P, KT, D])
    wh = sb(st, "wo_hi", [P, KT, D], F32R)
    wl = sb(st, "wo_lo", [P, KT, D], F32R)
    oh = sb(st, "o_hi_sb", [P, KT, S], F32R)
    ol = sb(st, "o_lo_sb", [P, KT, S], F32R)
    h2 = wo[:, 0:4, :]
    h2t = wo[:, 4:8, :].rearrange("p a (b s) -> p (a b) s", s=S)
    fw = sb(st, "fw", [P, D])
    rw = sb(st, "rw", [P, KT, EXPERTS])
    rb = sb(st, "rb", [1, EXPERTS])
    lg = sb(st, "lg", [P, NT, EXPERTS])
    top8 = sb(st, "top8", [P, NT, 8])
    idx8 = sb(st, "idx8", [P, NT, 8], U32)
    idxf = sb(st, "idxf", [P, NT, 8])
    one = sb(st, "one_hot", [P, 4, NT, EXPERTS])
    mask = sb(st, "mask", [P, NT, EXPERTS])
    which = sb(st, "which", [P, NT, EXPERTS])
    eg = sb(st, "eg", [P, NT, EXPERTS])
    r1 = sb(st, "r1", [P, 32])
    w_v = d["w_out"][0].rearrange("(k p) n -> p k n", p=P)
    block = st.enter_context(nc.Block())

    def flat(t):
        return psum[:, 2 * t:2 * t + 2, :].rearrange("p b n -> p (b n)")

    @block.sync
    def _(sp):
        for k in range(KT):
            sp.dma_start(wo[:, k, :], w_v[:, k, :]).then_inc(s_w[k], 16)
        for t in range(NT):
            sp.wait_ge(s_h2, t + 1)
            sp.dma_start(g["h2_dram"][t * P:(t + 1) * P, :], h2[:, t, :]).then_inc(s_store, 16)
        sp.wait_ge(s_store, 16 * NT)

    @block.gpsimd
    def _(pool):
        nc.gpsimd.dma_start(fw[:], d["ffn_norm_w"].to_broadcast([P, D])).then_inc(s_fw, 16)
        nc.gpsimd.dma_start(rw[:], d["router_w"][0].rearrange("(k p) e -> p k e", p=P)).then_inc(s_rw, 16)
        nc.gpsimd.dma_start(rb[:], d["router_b"]).then_inc(s_rw, 16)
        pool.wait_ge(s_fw, 16)

    @block.scalar
    def _(act):
        nc.scalar.activation(oh[:], o_t[:], ACT.Copy).then_inc(s_oh, 1)
        for k in range(KT):
            act.wait_ge(s_w[k], 16)
            nc.scalar.activation(wh[:, k, :], wo[:, k, :], ACT.Copy).then_inc(s_wh, 1)
        for t in range(NT):
            act.wait_ge(s_wl, KT)
            act.wait_ge(s_x2, t + 1)
            last = nc.scalar.activation(h2[:, t, :], x[:, t, :], ACT.Square, accum_out=stat[:, 24 + t:25 + t])
        last.then_inc(s_ss, 1)
        act.wait_ge(s_ss, 1)
        nc.scalar.activation(stat[:, 28:32], stat[:, 24:28], ACT.Sqrt, bias=con("eps"), scale=1.0 / D).then_inc(s_sd, 1)
        for t in range(NT):
            act.wait_ge(s_turn, t + 1)
            nc.scalar.activation(h2t[:, :, t * P:(t + 1) * P], flat(t).rearrange("p (k c) -> p k c", c=P), ACT.Copy).then_inc(s_h2t, 1)
        act.wait_ge(s_rt, 9)
        for t in range(NT):
            last = nc.scalar.activation(eg[:, t, :], lg[:, t, :], ACT.Exp, bias=r1[:, t:t + 1])
        last.then_inc(s_exp, 1)

    @block.vector
    def _(dve):
        dve.wait_ge(s_oh, 1)
        nc.vector.tensor_tensor(ol[:], o_t[:], oh[:].bitcast(F32), ALU.subtract).then_inc(s_ol, 1)
        for k in range(KT):
            dve.wait_ge(s_wh, k + 1)
            nc.vector.tensor_tensor(wl[:, k, :], wo[:, k, :], wh[:, k, :].bitcast(F32), ALU.subtract).then_inc(s_wl, 1)
        for t in range(NT):
            dve.wait_ge(s_acc, t + 1)
            nc.vector.tensor_tensor(x[:, t, :], flat(t), x[:, t, :], ALU.add).then_inc(s_x2, 1)
        nc.vector.memset(info[:], 0.0)
        nc.vector.memset(rank[:], -1e6)
        dve.wait_ge(s_sd, 1)
        nc.vector.reciprocal(stat[:, 32:36], stat[:, 28:32]).then_inc(s_rs, 1)
        dve.wait_ge(s_rs, 1)
        dve.wait_ge(s_fw, 16)
        for t in range(NT):
            nc.vector.scalar_tensor_tensor(h2[:, t, :], x[:, t, :], stat[:, 32 + t:33 + t], fw[:], ALU.mult, ALU.mult).then_inc(s_h2, 1)
        n = 0

        def chain(ins):
            nonlocal n
            n += 1
            ins.then_inc(s_rt, 1)
            dve.wait_ge(s_rt, n)

        dve.wait_ge(s_log, 1)
        chain(nc.vector.tensor_copy(lg[:], bank(0, 0, NT * EXPERTS).rearrange("p (t e) -> p t e", e=EXPERTS)))
        for t in range(NT):
            nc.vector.max(top8[:, t, :], lg[:, t, :]).then_inc(s_rt, 1)
        n += NT
        dve.wait_ge(s_rt, n)
        for t in range(NT - 1):
            nc.vector.max_index(idx8[:, t, :], top8[:, t, :], lg[:, t, :]).then_inc(s_rt, 1)
        n += NT - 1
        nc.vector.max_index(idx8[:, NT - 1, :], top8[:, NT - 1, :], lg[:, NT - 1, :])
        chain(nc.vector.tensor_scalar(r1[:, 0:4], top8[:, :, 0], -1.0, None, ALU.mult))
        chain(nc.vector.tensor_copy(idxf[:], idx8[:]))
        for j in range(4):
            last = nc.vector.tensor_tensor(one[:, j], con("experts").rearrange("p (a e) -> p a e", a=1).to_broadcast([P, NT, EXPERTS]),
                                           idxf[:, :, j:j + 1].to_broadcast([P, NT, EXPERTS]), ALU.is_equal)
        chain(last)
        chain(nc.vector.tensor_tensor(mask[:], one[:, 0], one[:, 1], ALU.add))
        chain(nc.vector.tensor_tensor(mask[:], mask[:], one[:, 2], ALU.add))
        chain(nc.vector.tensor_tensor(mask[:], mask[:], one[:, 3], ALU.add))
        nc.vector.memset(r1[:, 31:32], 0.0).then_inc(s_mask, 1)
        chain(nc.vector.scalar_tensor_tensor(which[:], one[:, 2], 2.0, one[:, 1], ALU.mult, ALU.add))
        chain(nc.vector.scalar_tensor_tensor(which[:], one[:, 3], 3.0, which[:], ALU.mult, ALU.add))
        dve.wait_ge(s_exp, 1)
        chain(nc.vector.tensor_tensor(eg[:], eg[:], mask[:], ALU.mult))
        chain(nc.vector.tensor_reduce(r1[:, 4:8], eg[:], AX.X, ALU.add))
        chain(nc.vector.reciprocal(r1[:, 8:12], r1[:, 4:8]))
        nc.vector.tensor_tensor(info[:, :, 0:EXPERTS, 2], eg[:], r1[:, 8:12].rearrange("p (t a) -> p t a", a=1).to_broadcast([P, NT, EXPERTS]),
                                ALU.mult)
        chain(nc.vector.tensor_scalar(r1[:, 12:16], con("token"), 4.0, -BIG, ALU.mult, ALU.add))
        nc.vector.tensor_tensor(info[:, :, 0:EXPERTS, 1], which[:], r1[:, 12:16].rearrange("p (t a) -> p t a", a=1).to_broadcast([P, NT, EXPERTS]),
                                ALU.add)
        chain(nc.vector.tensor_scalar(r1[:, 16:20], con("token"), -BIG, None, ALU.add))
        nc.vector.tensor_copy(info[:, :, 0:EXPERTS, 0], r1[:, 16:20].rearrange("p (t a) -> p t a", a=1).to_broadcast([P, NT, EXPERTS]))
        chain(nc.vector.tensor_scalar(which[:], mask[:], 1e6, -1e6, ALU.mult, ALU.add))
        dve.wait_ge(s_rank, 1)
        nc.vector.tensor_tensor(rank[:, :, 0:EXPERTS], which[:], bank(1, 0, NT * EXPERTS).rearrange("p (t e) -> p t e", e=EXPERTS), ALU.add)
        chain(nc.vector.tensor_reduce(r1[:, 20:21], bank(1, NT * EXPERTS, (NT + 1) * EXPERTS), AX.X, ALU.max))
        for r in range(ROUNDS):
            last = nc.vector.tensor_scalar(flags[:, r:r + 1], r1[:, 20:21], float(P * r) if r else -1.0, None, ALU.is_gt)
        chain(last)

    @block.tensor
    def _(pe):
        pe.wait_ge(s_ol, 1)
        for k in range(KT):
            pe.wait_ge(s_wl, k + 1)
            for t in range(NT):
                for c in range(2):
                    for m, (o, w) in enumerate(((oh, wh), (oh, wl), (ol, wh))):
                        last = nc.tensor.matmul(bank(2 * t + c), o[:, k, t * P:(t + 1) * P], w[:, k, c * 512:(c + 1) * 512],
                                                start=k == 0 and m == 0, stop=k == KT - 1 and m == 2)
                if k == KT - 1:
                    last.then_inc(s_acc, 1)
        for t in range(NT):
            pe.wait_ge(s_h2, t + 1)
            for k in range(KT):
                last = nc.tensor.transpose(bank(2 * t + k // 4, (k % 4) * P, (k % 4) * P + P), h2[:, t, k * P:(k + 1) * P], ident)
            last.then_inc(s_turn, 1)
        pe.wait_ge(s_h2t, NT)
        pe.wait_ge(s_rw, 32)
        for t in range(NT):
            o = bank(0, t * EXPERTS, (t + 1) * EXPERTS)
            for k in range(KT):
                nc.tensor.matmul(o, h2t[:, k, t * P:(t + 1) * P], rw[:, k, :], start=k == 0, stop=False)
            last = nc.tensor.matmul(o, con("ones")[0:1, :], rb[:], start=False, stop=True)
        last.then_inc(s_log, 1)
        pe.wait_ge(s_mask, 1)
        for t in range(NT):
            o = bank(1, t * EXPERTS, (t + 1) * EXPERTS)
            for u in range(t):
                nc.tensor.matmul(o, con("ones"), mask[:, u, :], start=u == 0, stop=False)
            nc.tensor.matmul(o, con("before"), mask[:, t, :], start=t == 0, stop=True)
        for u in range(NT):
            last = nc.tensor.matmul(bank(1, NT * EXPERTS, (NT + 1) * EXPERTS), con("ones"), mask[:, u, :], start=u == 0, stop=u == NT - 1)
        last.then_inc(s_rank, 1)


def experts(nc, d, sb, sem, st, g, con, ident, psum, bank):
    rank, info, flags = g["rank"], g["info"], g["flags"]
    raw = sb(st, "w_pieces", [P, RAW, 2, D])
    hi = sb(st, "w_pieces_hi", [P, RING, 2, D], F32R)
    lo = sb(st, "w_pieces_lo", [P, RING, 2, D], F32R)
    xg = sb(st, "xg", [P, D])
    xh = sb(st, "xh", [P, KT, P], F32R)
    xl = sb(st, "xl", [P, KT, P], F32R)
    ah = sb(st, "ah", [P, KT, P], F32R)
    al = sb(st, "al", [P, KT, P], F32R)
    gg = sb(st, "gg", [P, 512])
    uu = sb(st, "uu", [P, 512])
    sg = sb(st, "sig", [P, 512])
    av = sb(st, "av", [P, 512])
    ys = sb(st, "ys", [P, D])
    sel = sb(st, "sel", [P, NT, P])
    pick = sb(st, "pick_e", [P, P], F32R)
    bias = sb(st, "bias", [P, 3 * D], F32R)
    next_i = sb(st, "next_i", [P, 2], I32)
    next_g = sb(st, "next_g", [P, 1])
    this_i = sb(st, "this_i", [P, 1], I32)
    this_g = sb(st, "this_g", [P, 1])
    s_raw = [sem(f"piece_loaded{p}") for p in range(PIECES)]
    s_hi, s_lo, s_used = sem("piece_hi"), sem("piece_lo"), sem("piece_used")
    s_bl, s_bh, s_bias, s_z = sem("bias_loaded"), sem("bias_hi"), sem("bias_split"), sem("zeroed")
    s_sel, s_imm, s_idx, s_copy, s_pick = sem("selected"), sem("index_summed"), sem("index_ready"), sem("index_moved"), sem("bias_row_picked")
    s_gath, s_tx, s_xh, s_xl = sem("rows_gathered"), sem("rows_turned"), sem("x_hi"), sem("x_lo")
    s_g, s_u, s_sig, s_act = sem("gate_clipped"), sem("up_steps"), sem("gate_sigmoid"), sem("act_ready")
    s_ta, s_ah, s_al, s_y, s_scat = sem("act_turned"), sem("act_hi"), sem("act_lo"), sem("y_ready"), sem("rows_scattered")
    s_round, s_stored, s_part = sem("round_moved"), sem("rows_stored"), sem("dma_about_to_start")
    block = st.enter_context(nc.Block())

    def rounds(eng, run):
        with eng.Fori(0, ROUNDS) as r:
            flag = eng.value_load(flags[0:1, bass.ds(r, 1)])
            with eng.If(flag == 1):
                run(r)

    @block.sync
    def _(sp):
        for rows in (slice(0, 32), slice(32, 64)):
            for w, c0, n in (("mlp1_b", 0, 2 * D), ("mlp2_b", 2 * D, D)):
                sp.dma_start(raw[rows].rearrange("p a b n -> p (a b n)")[:, c0:c0 + n], d[w][0]).then_inc(s_bl, 16)
        sp.wait_ge(s_bias, 1)

        def run(r):
            with sp.Fori(0, EXPERTS) as e:
                for p in range(PIECES):
                    sp.wait_ge(s_lo, (r * EXPERTS + e) * PIECES + (p + 1))
                    half, k = p // 4, p % 4
                    src = (d["mlp1_w"][0][bass.ds(e, 1), k * 256:(k + 1) * 256, half * D:(half + 1) * D] if half < 2
                           else d["mlp2_w"][0][bass.ds(e, 1), k * 256:(k + 1) * 256, :])
                    sp.dma_start(raw[:, p % RAW], src.rearrange("e (r p) n -> p (e r) n", p=P)).then_inc(s_raw[p], 16)

        rounds(sp, run)

    @block.gpsimd
    def _(pool):
        nc.gpsimd.memset(xg[:], 0.0).then_inc(s_z, 1)
        pool.wait_ge(s_z, 1)
        nc.gpsimd.memset(bias[64:128, :].bitcast(F32), 0.0).then_inc(s_z, 1)
        pool.wait_ge(s_z, 2)
        pool.sem_inc(s_stored, 1)

        def part_waits():
            pool.sem_inc(s_part, 1)

        def gather(m):
            pool.wait_ge(s_idx, m + 1)
            pool.wait_ge(s_tx, m * 2 + 1)
            part_waits()
            nc.gpsimd.indirect_dma_start(xg[:], None, g["h2_dram"], bass.IndirectOffsetOnAxis(next_i[:, 0:1], 0),
                                         bounds_check=S - 1, oob_is_err=False).then_inc(s_gath, 16)

        def scatter(turn):
            pool.wait_ge(s_copy, turn + 1)
            pool.wait_ge(s_y, turn + 2)
            part_waits()
            nc.gpsimd.indirect_dma_start(g["y_dram"], bass.IndirectOffsetOnAxis(this_i[:, 0:1], 0), ys[:], None,
                                         bounds_check=4 * S - 1, oob_is_err=False).then_inc(s_scat, 16)
            pool.wait_ge(s_scat, turn * 16 + 16)
            pool.sem_inc(s_stored, 1)

        def run(r):
            gather(r * TURNS)
            gather(r * TURNS + 1)
            with pool.Fori(1, EXPERTS) as e:
                scatter(r * EXPERTS + (e - 1))
                gather(r * TURNS + (e + 1))
            scatter(r * EXPERTS + (EXPERTS - 1))

        rounds(pool, run)

    @block.scalar
    def _(act):
        act.wait_ge(s_bl, 64)
        flat = raw[:].rearrange("p a b n -> p (a b n)")
        nc.scalar.activation(bias[0:32, :], flat[0:32, 0:3 * D], ACT.Copy)
        nc.scalar.activation(hi[:].rearrange("p a b n -> p (a b n)")[32:64, 0:3 * D], flat[32:64, 0:3 * D], ACT.Copy).then_inc(s_bh, 1)
        act.wait_ge(s_bias, 1)
        act.sem_inc(s_y, 1)

        def split(turn, p):
            act.wait_ge(s_raw[p], turn * 16 + 16)
            act.wait_ge(s_used, turn * PIECES + (p + 1))
            nc.scalar.activation(hi[:, p % RING], raw[:, p % RAW], ACT.Copy).then_inc(s_hi, 1)

        def x_hi(m, q):
            act.wait_ge(s_tx, m * 2 + (q + 2))
            nc.scalar.activation(xh[:, 4 * q:4 * q + 4, :].rearrange("p a b -> p (a b)"), bank(7), ACT.Copy).then_inc(s_xh, 1)

        def sigmoid(turn, h):
            act.wait_ge(s_g, turn * 2 + (h + 1))
            nc.scalar.activation(sg[:], gg[:], ACT.Sigmoid, scale=1.702).then_inc(s_sig, 1)

        def a_hi(turn, h):
            act.wait_ge(s_ta, turn * 2 + (h + 2))
            nc.scalar.activation(ah[:, 4 * h:4 * h + 4, :].rearrange("p a b -> p (a b)"), bank(6), ACT.Copy).then_inc(s_ah, 1)

        def y_out(turn):
            act.wait_ge(s_used, turn * PIECES + (PIECES + RING))
            act.wait_ge(s_copy, turn + 1)
            act.wait_ge(s_stored, turn + 1)
            nc.scalar.activation(ys[:], psum[:, 4:6, :].rearrange("p b n -> p (b n)"), ACT.Copy, scale=this_g[:, 0:1]).then_inc(s_y, 1)

        def body(r, e, first):
            turn = r * EXPERTS + e
            for p in range(PIECES):
                split(turn, p)
                if p == 2 and not first:
                    y_out(r * EXPERTS + (e - 1))
                if p == 6:
                    sigmoid(turn, 0)
                if p == 8:
                    a_hi(turn, 0)
                if p == 9:
                    sigmoid(turn, 1)
                if p == 10:
                    a_hi(turn, 1)
                    x_hi(r * TURNS + (e + 1), 0)
                if p == 11:
                    x_hi(r * TURNS + (e + 1), 1)

        def run(r):
            for q in range(2):
                x_hi(r * TURNS, q)
            body(r, 0, True)
            with act.Fori(1, EXPERTS) as e:
                body(r, e, False)
            y_out(r * EXPERTS + (EXPERTS - 1))

        rounds(act, run)

    @block.vector
    def _(dve):
        dve.wait_ge(s_bh, 1)
        hi_flat, raw_flat = (a[:].rearrange("p a b n -> p (a b n)") for a in (hi, raw))
        nc.vector.tensor_tensor(bias[32:64, :], raw_flat[32:64, 0:3 * D], hi_flat[32:64, 0:3 * D].bitcast(F32), ALU.subtract).then_inc(s_bias, 1)
        dve.wait_ge(s_bias, 1)
        dve.sem_inc(s_lo, RAW)
        dve.sem_inc(s_round, 1)
        dve.sem_inc(s_xl, 1)
        dve.sem_inc(s_act, 1)
        dve.sem_inc(s_al, 1)

        def split(turn, p):
            dve.wait_ge(s_hi, turn * PIECES + (p + 1))
            nc.vector.tensor_tensor(lo[:, p % RING], raw[:, p % RAW], hi[:, p % RING].bitcast(F32), ALU.subtract).then_inc(s_lo, 1)

        def select(m, e):
            dve.wait_ge(s_imm, m + 1)
            nc.vector.tensor_tensor(sel[:], con("slot").rearrange("p (a n) -> p a n", a=1).to_broadcast([P, NT, P]),
                                    rank[:, :, bass.ds(e, 1)].to_broadcast([P, NT, P]), ALU.is_equal).then_inc(s_sel, 1)

        def indices(m):
            dve.wait_ge(s_imm, m + 2)
            dve.wait_ge(s_tx, m * 2 + 1)
            nc.vector.tensor_scalar(next_i[:], bank(4, 0, 2), BIG, None, ALU.add)
            nc.vector.tensor_copy(next_g[:], bank(4, 2, 3)).then_inc(s_idx, 1)

        def move_indices(turn, m):
            dve.wait_ge(s_stored, turn + 1)
            dve.wait_ge(s_idx, m + 1)
            nc.vector.tensor_copy(this_i[:], next_i[:, 1:2])
            nc.vector.tensor_copy(this_g[:], next_g[:]).then_inc(s_copy, 1)

        def pick_bias(e, used):
            dve.wait_ge(s_used, used)
            nc.vector.tensor_copy(pick[:], con("pick")[:, bass.ds(e, 1)].to_broadcast([P, P])).then_inc(s_pick, 1)

        def x_lo(m, q):
            dve.wait_ge(s_xh, m * 2 + (q + 1))
            x4 = xh[:, 4 * q:4 * q + 4, :].rearrange("p a b -> p (a b)")
            nc.vector.tensor_tensor(xl[:, 4 * q:4 * q + 4, :].rearrange("p a b -> p (a b)"), bank(7), x4.bitcast(F32),
                                    ALU.subtract).then_inc(s_xl, 1)

        def a_lo(turn, h):
            dve.wait_ge(s_ah, turn * 2 + (h + 1))
            a4 = ah[:, 4 * h:4 * h + 4, :].rearrange("p a b -> p (a b)")
            nc.vector.tensor_tensor(al[:, 4 * h:4 * h + 4, :].rearrange("p a b -> p (a b)"), bank(6), a4.bitcast(F32),
                                    ALU.subtract).then_inc(s_al, 1)

        def swiglu(turn, h):
            dve.wait_ge(s_used, turn * PIECES + (4 * h + 4 + RING))
            pair = psum[:, 2 * h:2 * h + 2, :].rearrange("p b (n two) -> p (b n) two", two=2)
            nc.vector.tensor_scalar(gg[:], pair[:, :, 0], 7.0, None, ALU.min).then_inc(s_g, 1)
            nc.vector.tensor_scalar(uu[:], pair[:, :, 1], 7.0, -7.0, ALU.min, ALU.max).then_inc(s_u, 1)
            dve.wait_ge(s_g, turn * 2 + (h + 1))
            dve.wait_ge(s_u, turn * 4 + (2 * h + 1))
            nc.vector.scalar_tensor_tensor(uu[:], uu[:], 1.0, gg[:], ALU.add, ALU.mult).then_inc(s_u, 1)
            dve.wait_ge(s_u, turn * 4 + (2 * h + 2))
            dve.wait_ge(s_sig, turn * 2 + (h + 1))
            dve.wait_ge(s_ta, turn * 2 + (h + 1))
            nc.vector.tensor_tensor(av[:], uu[:], sg[:], ALU.mult).then_inc(s_act, 1)

        def body(r, e):
            turn = r * EXPERTS + e
            m = r * TURNS + (e + 1)
            for p in range(PIECES):
                split(turn, p)
                if p == 1:
                    select(m, e + 1)
                if p == 6:
                    swiglu(turn, 0)
                if p == 7:
                    move_indices(turn, r * TURNS + e)
                    dve.wait_ge(s_copy, turn + 1)
                    indices(m)
                if p == 8:
                    a_lo(turn, 0)
                if p == 9:
                    swiglu(turn, 1)
                if p == 10:
                    a_lo(turn, 1)
                    x_lo(m, 0)
                if p == 11:
                    x_lo(m, 1)
                    pick_bias(e + 1, turn * PIECES + (9 + RING))

        def run(r):
            dve.wait_ge(s_round, r + 1)
            select(r * TURNS, 0)
            indices(r * TURNS)
            pick_bias(0, r * (EXPERTS * PIECES) + RING)
            for q in range(2):
                x_lo(r * TURNS, q)
            body(r, 0)
            with dve.Fori(1, EXPERTS) as e:
                body(r, e)
            nc.vector.tensor_scalar(rank[:], rank[:], float(-P), None, ALU.add).then_inc(s_round, 1)

        rounds(dve, run)

    @block.tensor
    def _(pe):
        pe.wait_ge(s_z, 2)
        pe.wait_ge(s_bias, 1)
        pe.sem_inc(s_used, RING)
        pe.sem_inc(s_imm, 1)
        pe.sem_inc(s_tx, 1)
        pe.sem_inc(s_ta, 1)

        def index_sum(m, e, turn):
            pe.wait_ge(s_sel, m + 1)
            pe.wait_ge(s_y, turn + 1)
            for t in range(NT):
                last = nc.tensor.matmul(bank(4, 0, 4), sel[:, t, :], info[:, t, bass.ds(e, 1), :].rearrange("p a c -> p (a c)"),
                                        start=t == 0, stop=t == NT - 1)
            last.then_inc(s_imm, 1)

        def turn_x(m, q):
            if q == 0:
                pe.wait_ge(s_gath, m * 16 + 16)
            pe.wait_ge(s_xl, m * 2 + (q + 1))
            for k in range(4):
                last = nc.tensor.transpose(bank(7, k * P, k * P + P), xg[:, (4 * q + k) * P:(4 * q + k + 1) * P], ident)
            last.then_inc(s_tx, 1)

        def turn_a(turn, h):
            pe.wait_ge(s_act, turn * 2 + (h + 2))
            pe.wait_ge(s_al, turn * 2 + (h + 1))
            for k in range(4):
                last = nc.tensor.transpose(bank(6, k * P, k * P + P), av[:, k * P:(k + 1) * P], ident)
            last.then_inc(s_ta, 1)

        def piece(turn, p, ops, b0, k0, first, last_piece):
            if first:
                for c in range(2):
                    nc.tensor.matmul(bank(b0 + c), pick[:], bias[:, (b0 + c) * 512:(b0 + c + 1) * 512], start=True, stop=False)
            pe.wait_ge(s_lo, turn * PIECES + (p + 1 + RAW))
            for r2 in range(2):
                for c in range(2):
                    w = [a[:, p % RING, r2, c * 512:(c + 1) * 512] for a in (hi, lo)]
                    a = [o[:, k0 + r2, :] for o in ops]
                    nc.tensor.matmul(bank(b0 + c), a[0], w[0], start=False, stop=False)
                    nc.tensor.matmul(bank(b0 + c), a[0], w[1], start=False, stop=False)
                    last = nc.tensor.matmul(bank(b0 + c), a[1], w[0], start=False, stop=last_piece and r2 == 1)
            last.then_inc(s_used, 1)

        def body(r, e):
            turn = r * EXPERTS + e
            m = r * TURNS + (e + 1)
            pe.wait_ge(s_xl, m * 2 + 1)
            pe.wait_ge(s_pick, m)
            pe.wait_ge(s_act, turn * 2 + 1)
            for p in range(8):
                piece(turn, p, (xh, xl), 2 * (p // 4), 2 * (p % 4), p % 4 == 0, p % 4 == 3)
                if p == 1:
                    index_sum(m, e + 1, turn)
                if p == 6:
                    turn_a(turn, 0)
            pe.wait_ge(s_al, turn * 2 + 2)
            pe.wait_ge(s_idx, m + 1)
            piece(turn, 8, (ah, al), 4, 0, True, False)
            turn_x(m, 0)
            piece(turn, 9, (ah, al), 4, 2, False, False)
            turn_a(turn, 1)
            pe.wait_ge(s_al, turn * 2 + 3)
            piece(turn, 10, (ah, al), 4, 4, False, False)
            turn_x(m, 1)
            piece(turn, 11, (ah, al), 4, 6, False, True)

        def run(r):
            index_sum(r * TURNS, 0, r * EXPERTS)
            turn_x(r * TURNS, 0)
            turn_x(r * TURNS, 1)
            body(r, 0)
            with pe.Fori(1, EXPERTS) as e:
                body(r, e)

        rounds(pe, run)


def combine(nc, d, sb, sem, st, g, con, out):
    x, stat, y_dram = g["x"], g["stat"], g["y_dram"]
    y4 = sb(st, "y4", [P, NT, 4, D])
    sqr = sb(st, "sqr", [P, D])
    fw = sb(st, "final_w", [P, D])
    s_y = [sem(f"y_loaded{t}") for t in range(NT)]
    s_fw, s_add, s_ss, s_sd, s_rs, s_o, s_out = (sem(n) for n in ("final_w_loaded", "rows_added", "x3_squared", "x3_deviation",
                                                                  "x3_rstd", "out_ready", "out_stored"))
    block = st.enter_context(nc.Block())

    @block.sync
    def _(sp):
        for t in range(NT):
            sp.dma_start(y4[:, t], y_dram[t * 4 * P:(t + 1) * 4 * P, :].rearrange("(p j) n -> p j n", j=4)).then_inc(s_y[t], 16)
        for t in range(NT):
            sp.wait_ge(s_o, t + 1)
            sp.dma_start(out[0, t * P:(t + 1) * P, :], x[:, t, :]).then_inc(s_out, 16)
        sp.wait_ge(s_out, 16 * NT)

    @block.gpsimd
    def _(pool):
        nc.gpsimd.dma_start(fw[:], d["final_norm_w"].to_broadcast([P, D])).then_inc(s_fw, 16)

    @block.scalar
    def _(act):
        for t in range(NT):
            act.wait_ge(s_add, 4 * t + 4)
            nc.scalar.activation(sqr[:], x[:, t, :], ACT.Square, accum_out=stat[:, 40 + t:41 + t]).then_inc(s_ss, 1)
            act.wait_ge(s_ss, t + 1)
            nc.scalar.activation(stat[:, 44 + t:45 + t], stat[:, 40 + t:41 + t], ACT.Sqrt, bias=con("eps"), scale=1.0 / D).then_inc(s_sd, 1)

    @block.vector
    def _(dve):
        dve.wait_ge(s_fw, 16)

        def finish(t):
            dve.wait_ge(s_sd, t + 1)
            nc.vector.reciprocal(stat[:, 48 + t:49 + t], stat[:, 44 + t:45 + t]).then_inc(s_rs, 1)
            dve.wait_ge(s_rs, t + 1)
            nc.vector.scalar_tensor_tensor(x[:, t, :], x[:, t, :], stat[:, 48 + t:49 + t], fw[:], ALU.mult, ALU.mult).then_inc(s_o, 1)

        for t in range(NT):
            dve.wait_ge(s_y[t], 16)
            for j in range(4):
                if j:
                    dve.wait_ge(s_add, 4 * t + j)
                nc.vector.tensor_tensor(x[:, t, :], x[:, t, :], y4[:, t, j, :], ALU.add).then_inc(s_add, 1)
            if t:
                finish(t - 1)
        finish(NT - 1)


def kernel(x, positions, attn_norm_w, w_in, shift_mu, lambda_q1, lambda_k1, lambda_q2, lambda_k2, subln_w, rw_w0, rw_w2,
           rw_a0, rw_a2, rw_g2, rw_k_k, rw_k_a, rw_r_k, rw_lnx_w, rw_lnx_b, w_out, ffn_norm_w, router_w, router_b,
           mlp1_w, mlp1_b, mlp2_w, mlp2_b, final_norm_w):
    import concourse.bacc as bacc
    from concourse.bass_utils import run_bass_kernel_spmd as run

    def col(a):
        return np.asarray(a).reshape(-1, P).T

    mu = col(shift_mu)
    per_pair = [mu[:, 0:4], mu[:, 4:8], mu[:, 8:12]] + [col(a) for a in (rw_w0, rw_a0, rw_k_k, rw_k_a, rw_r_k, rw_lnx_w, rw_lnx_b)]
    pairs = np.stack(per_pair, 2).reshape(P, HEADS * NPAR)
    tables, _ = constant_tables()
    arrays = {
        "x": x, "positions": positions, "w_in": w_in, "w_out": w_out, "router_w": router_w, "router_b": router_b,
        "mlp1_w": mlp1_w, "mlp1_b": mlp1_b, "mlp2_w": mlp2_w, "mlp2_b": mlp2_b, "ffn_norm_w": ffn_norm_w,
        "final_norm_w": np.asarray(final_norm_w).reshape(1, D),
        "cols": np.concatenate([col(attn_norm_w), mu[:, 12:14], pairs, col(subln_w)], 1),
        "lam": np.concatenate([np.asarray(a) for a in (lambda_q1, lambda_k1, lambda_q2, lambda_k2)], 1),
        "w2a2": np.concatenate([np.asarray(rw_w2)[0], np.asarray(rw_a2)[0]], 0), "g2": np.asarray(rw_g2)[0],
        "cst": tables,
    }
    nc = bacc.Bacc("TRN2", target_bir_lowering=False, num_devices=1)
    feed, d = {}, {}
    for name, a in arrays.items():
        a = np.ascontiguousarray(a)
        feed[f"in_{name}"] = a
        d[name] = nc.dram_tensor(f"in_{name}", a.shape, mybir.dt.from_np(a.dtype), kind="ExternalInput").ap()
    out = nc.dram_tensor("out_0", (1, S, D), F32, kind="ExternalOutput").ap()
    build_program(nc, d, out)
    return run(nc, [feed], core_ids=[0]).results[0]["out_0"]
```

```python
from contextlib import ExitStack

import numpy as np

import concourse.bass as bass
from concourse import mybir

F32 = mybir.dt.float32
F32R = mybir.dt.float32r
I32 = mybir.dt.int32
U32 = mybir.dt.uint32
ALU = mybir.AluOpType
ACT = mybir.ActivationFunctionType
AX = mybir.AxisListType

P = 128
D = 1024
S = 512
NT = S // P
KT = D // P
IN_TILES = 26
HEADS = 4
CH = 64
NCH = S // CH
LEVELS = (2, 4, 8, 16, 32)
NORM_EPS = 1e-5
GN_EPS = 64e-5
LAM_INIT = 0.8 - 0.6 * 1.0
E_HALF = float(np.exp(-0.5))
EXPERTS = 32
TURNS = EXPERTS + 1
PIECES = 12
RAW = 6
RING = 4
ROUNDS = S // P
BIG = float(1 << 20)
NPAR = 10
NEG = -1e30


def constant_tables():
    p = np.arange(P)[:, None]
    c = np.arange(P)[None, :]
    same = p // CH == c // CH
    m1 = (same & (p < c)).astype(np.float32)
    m2 = (same & (p <= c)).astype(np.float32)
    level = [((p // (2 * b) == c // (2 * b)) & ((p // b) % 2 == 1) & ((c // b) % 2 == 0)) for b in LEVELS]
    t = np.arange(S)[None, :]
    inv = (np.float32(10000.0) ** (-np.arange(0, 64, 2, dtype=np.float32) / np.float32(64))).astype(np.float32)
    parts = {
        "ident": p == c,
        "mask_b": np.concatenate([m1, -m2], 1),
        "mask_k": np.concatenate([m1, m2], 1),
        "level1": (p // 2 == c // 2) & (p % 2 == 0) & (c % 2 == 1),
        "levels": np.concatenate(level, 1),
        "stack": p % CH == np.arange(CH)[None, :],
        "heads": same,
        "swap": p == (c ^ 32),
        "causal": np.where(np.arange(S)[None, :] - 3 * P > p, NEG, 0.0),
        "reset": np.broadcast_to(t % CH != 0, (P, S)),
        "before": p < c,
        "ones": np.ones((P, P)),
        "slot": np.broadcast_to(c, (P, P)),
        "token": np.arange(NT)[None, :] * P + p,
        "experts": np.broadcast_to(np.arange(EXPERTS)[None, :], (P, EXPERTS)),
        "pick": ((p % EXPERTS) == np.arange(TURNS)[None, :]) & (p < 2 * EXPERTS),
        "inv": inv[np.arange(P) % 32][:, None],
        "sign": np.where(np.arange(P)[:, None] % 64 < 32, -1.0, 1.0),
        "eps": np.full((P, 1), NORM_EPS),
        "gn_eps": np.full((P, 1), GN_EPS),
    }
    at, out, n = {}, [], 0
    for name, a in parts.items():
        a = np.asarray(a, np.float32)
        at[name] = (n, n + a.shape[1])
        n += a.shape[1]
        out.append(a)
    return np.ascontiguousarray(np.concatenate(out, 1)), at


class Steps:

    def __init__(self, sem, names):
        self.sem, self.names, self.next = sem, list(names), 0

    def step(self, name):
        assert self.names[self.next] == name, (self.names[self.next], name)
        self.next += 1
        return 1

    def reached(self, j, name):
        return j * len(self.names) + (len(self.names) + self.names.index(name) + 2)

    def before(self, j, name):
        return j * len(self.names) + (self.names.index(name) + 2)

    def ahead(self):
        return len(self.names) + 1


def build_program(nc, d, out):
    _, at = constant_tables()
    with ExitStack() as top:
        def sb(stack, name, shape, dt=F32):
            return stack.enter_context(nc.sbuf_tensor(name, shape, dt))

        def sem(name):
            return top.enter_context(nc.semaphore(name))

        psum = top.enter_context(nc.psum_tensor("psum", [P, 8, 512], F32))
        cst = sb(top, "cst", [P, d["cst"].shape[1]])
        cols = sb(top, "cols", [P, d["cols"].shape[1]])
        x = sb(top, "x", [P, NT, D])
        stat = sb(top, "stat", [P, 64])

        def con(name, a=0, b=None):
            lo, hi = at[name]
            return cst[:, lo + a:(lo + b if b is not None else hi)]

        ident = con("ident")

        def bank(n, a=0, b=512, rows=slice(0, P)):
            return psum[rows, n, a:b]

        h2_dram = nc.dram_tensor("h2_rows", (S, D), F32, kind="Internal").ap()
        y_dram = nc.dram_tensor("expert_rows", (4 * S, D), F32, kind="Internal").ap()
        rank = sb(top, "rank", [P, NT, TURNS])
        info = sb(top, "info", [P, NT, TURNS, 4])
        flags = sb(top, "flags", [P, ROUNDS], I32)

        with ExitStack() as mixer:
            o_t = sb(mixer, "o_t", [P, 2 * HEADS, S])
            with ExitStack() as st:
                pall = sb(st, "pall", [P, IN_TILES, S + 1])
                cosb = sb(st, "cosb", [P, S])
                sinb = sb(st, "sinb", [P, S])
                g = dict(cst=cst, cols=cols, x=x, stat=stat, pall=pall, cosb=cosb, sinb=sinb, o_t=o_t)
                project(nc, d, sb, sem, g, con, ident, psum, bank)
                mix(nc, d, sb, sem, st, g, con, ident, psum, bank)
            output_and_route(nc, d, sb, sem, mixer, dict(x=x, stat=stat, o_t=o_t, rank=rank, info=info, flags=flags,
                                                         h2_dram=h2_dram), con, ident, psum, bank)
        with ExitStack() as st:
            experts(nc, d, sb, sem, st, dict(stat=stat, rank=rank, info=info, flags=flags, h2_dram=h2_dram, y_dram=y_dram),
                    con, ident, psum, bank)
        with ExitStack() as st:
            combine(nc, d, sb, sem, st, dict(x=x, stat=stat, y_dram=y_dram), con, out)


def project(nc, d, sb, sem, g, con, ident, psum, bank):
    cst, cols, x, stat, pall, cosb, sinb = (g[k] for k in ("cst", "cols", "x", "stat", "pall", "cosb", "sinb"))
    s_cst, s_cols, s_lam, s_pos = sem("cst_loaded"), sem("cols_loaded"), sem("lam_loaded"), sem("pos_loaded")
    s_x = [sem(f"x_loaded{t}") for t in range(NT)]
    s_w = [sem(f"w_in_loaded{u}") for u in range(2)]
    s_sq, s_sd, s_rstd, s_xn = sem("x_squared"), sem("x_deviation"), sem("x_rstd"), sem("x_normed")
    s_xt, s_hh, s_hl = sem("x_turned"), sem("h_hi"), sem("h_lo")
    s_whi, s_wlo, s_prod, s_out = sem("w_hi"), sem("w_lo"), sem("projected"), sem("p_copied")
    s_zero, s_rope, s_lam1, s_ang = sem("p_zeroed"), sem("rope_steps"), sem("lam_steps"), sem("angles_done")
    s_trig, s_lex = sem("trig_done"), sem("lam_exp")
    with ExitStack() as st:
        xn = sb(st, "xn", [P, NT, D])
        h_hi = sb(st, "h_hi_sb", [P, KT, S], F32R)
        h_lo = sb(st, "h_lo_sb", [P, KT, S], F32R)
        w_raw = sb(st, "w_raw", [P, 2, KT, P])
        w_hi = sb(st, "w_hi_sb", [P, 2, KT, P], F32R)
        w_lo = sb(st, "w_lo_sb", [P, 2, KT, P], F32R)
        posi = sb(st, "posi", [P, S], I32)
        ang = sb(st, "ang", [P, S])
        turns = sb(st, "turns", [P, S])
        lam = sb(st, "lam", [P, 4, 64])
        lamp = sb(st, "lamp", [P, 64])
        w_v = d["w_in"][0].rearrange("(k p) n -> p k n", p=P)
        x_v = d["x"][0].rearrange("(t p) c -> p t c", p=P)
        block = st.enter_context(nc.Block())

        @block.sync
        def _(sp):
            for t in range(NT):
                sp.dma_start(x[:, t, :], x_v[:, t, :]).then_inc(s_x[t], 16)
            with sp.Fori(0, IN_TILES // 2) as i:
                for u in range(2):
                    sp.wait_ge(s_wlo, i * 2 + (u + 1))
                    sp.dma_start(w_raw[:, u], w_v[:, :, bass.ds(i * 256 + u * P, P)]).then_inc(s_w[u], 16)

        @block.gpsimd
        def _(pool):
            nc.gpsimd.dma_start(cst[:], d["cst"]).then_inc(s_cst, 16)
            nc.gpsimd.dma_start(cols[:], d["cols"]).then_inc(s_cols, 16)
            nc.gpsimd.dma_start(posi[:], d["positions"].to_broadcast([P, S])).then_inc(s_pos, 16)
            nc.gpsimd.dma_start(lam[:].rearrange("p a b -> p (a b)"), d["lam"].to_broadcast([P, 256])).then_inc(s_lam, 16)
            nc.gpsimd.memset(pall[:, :, 0:1], 0.0).then_inc(s_zero, 1)
            pool.wait_ge(s_zero, 1)

        @block.scalar
        def _(act):
            for t in range(NT):
                act.wait_ge(s_x[t], 16)
                last = nc.scalar.activation(xn[:, t, :], x[:, t, :], ACT.Square, accum_out=stat[:, t:t + 1])
            last.then_inc(s_sq, 1)
            act.wait_ge(s_sq, 1)
            act.wait_ge(s_cst, 16)
            nc.scalar.activation(stat[:, 4:8], stat[:, 0:4], ACT.Sqrt, bias=con("eps"), scale=1.0 / D).then_inc(s_sd, 1)
            act.wait_ge(s_cols, 16)

            def split(i, u):
                act.wait_ge(s_w[u], i * 16 + 16)
                act.wait_ge(s_prod, i * 2 + (u + 1))
                nc.scalar.activation(w_hi[:, u], w_raw[:, u], ACT.Copy).then_inc(s_whi, 1)

            def copy_out(n, u):
                act.wait_ge(s_prod, n + 3)
                nc.scalar.activation(pall[:, bass.ds(n, 1), 1:S + 1].rearrange("p a s -> p (a s)"), bank(u), ACT.Copy).then_inc(s_out, 1)

            split(0, 0)
            split(0, 1)
            for k in range(KT):
                act.wait_ge(s_xt, k + 1)
                nc.scalar.activation(h_hi[:, k, :], bank(k), ACT.Copy, scale=cols[:, k:k + 1]).then_inc(s_hh, 1)
            with act.Fori(1, IN_TILES // 2) as i:
                for u in range(2):
                    split(i, u)
                    copy_out(i * 2 + (u - 2), u)
            for u in range(2):
                copy_out(IN_TILES - 2 + u, u)
            act.wait_ge(s_ang, 2)
            nc.scalar.activation(cosb[:], ang[:], ACT.Sin)
            nc.scalar.activation(sinb[:], turns[:], ACT.Sin).then_inc(s_trig, 1)
            act.wait_ge(s_lam1, 2)
            nc.scalar.activation(stat[:, 18:20], stat[:, 16:18], ACT.Exp).then_inc(s_lex, 1)

        @block.vector
        def _(dve):
            nc.vector.memset(stat[:, 63:64], 0.0).then_inc(s_wlo, 2)
            dve.wait_ge(s_sd, 1)
            nc.vector.reciprocal(stat[:, 8:12], stat[:, 4:8]).then_inc(s_rstd, 1)
            dve.wait_ge(s_rstd, 1)
            for t in range(NT):
                nc.vector.tensor_scalar(xn[:, t, :], x[:, t, :], stat[:, 8 + t:9 + t], None, ALU.mult).then_inc(s_xn, 1)

            def split(i, u):
                dve.wait_ge(s_whi, i * 2 + (u + 1))
                nc.vector.tensor_tensor(w_lo[:, u], w_raw[:, u], w_hi[:, u].bitcast(F32), ALU.subtract).then_inc(s_wlo, 1)

            split(0, 0)
            split(0, 1)
            for k in range(KT):
                dve.wait_ge(s_hh, k + 1)
                nc.vector.scalar_tensor_tensor(h_lo[:, k, :], bank(k), cols[:, k:k + 1], h_hi[:, k, :].bitcast(F32),
                                               ALU.mult, ALU.subtract).then_inc(s_hl, 1)
            with dve.Fori(1, IN_TILES // 2) as i:
                for u in range(2):
                    split(i, u)
            dve.wait_ge(s_pos, 16)
            step = 0

            def chain(ins):
                nonlocal step
                step += 1
                ins.then_inc(s_rope, 1)
                dve.wait_ge(s_rope, step)

            two_pi = 2 * np.pi
            c1 = 6.28125
            c2 = float(np.float32(two_pi - c1) - np.float32(two_pi - c1) % np.float32(2.0 ** -20))
            c3 = float(two_pi - c1 - c2)
            chain(nc.vector.tensor_copy(cosb[:], posi[:]))
            chain(nc.vector.tensor_scalar(sinb[:], cosb[:], con("inv"), None, ALU.mult))
            for dst, shift in ((ang, 0.25), (turns, 0.0)):
                chain(nc.vector.tensor_scalar(cosb[:], sinb[:], float(1 / two_pi), shift, ALU.mult, ALU.add))
                chain(nc.vector.tensor_scalar(cosb[:], cosb[:], 12582912.0, None, ALU.add))
                chain(nc.vector.tensor_scalar(cosb[:], cosb[:], 12582912.0, None, ALU.subtract))
                chain(nc.vector.scalar_tensor_tensor(dst[:], cosb[:], -c1, sinb[:], ALU.mult, ALU.add))
                chain(nc.vector.scalar_tensor_tensor(dst[:], cosb[:], -c2, dst[:], ALU.mult, ALU.add))
                chain(nc.vector.scalar_tensor_tensor(dst[:], cosb[:], -c3, dst[:], ALU.mult, ALU.add))
                if shift:
                    chain(nc.vector.tensor_scalar(dst[:], dst[:], float(np.pi / 2), None, ALU.add))
                chain(nc.vector.tensor_scalar(dst[:], dst[:], 3.1415925, -3.1415925, ALU.min, ALU.max))
                nc.vector.memset(stat[:, 62:63], 0.0).then_inc(s_ang, 1)
            dve.wait_ge(s_lam, 16)
            for n in range(2):
                if n:
                    dve.wait_ge(s_lam1, n)
                nc.vector.tensor_tensor_reduce(lamp[:], lam[:, 2 * n, :], lam[:, 2 * n + 1, :], 1.0, 0.0, ALU.mult, ALU.add,
                                               stat[:, 16 + n:17 + n]).then_inc(s_lam1, 1)
            dve.wait_ge(s_lex, 1)
            chain(nc.vector.tensor_tensor(stat[:, 20:21], stat[:, 19:20], stat[:, 18:19], ALU.subtract))
            chain(nc.vector.tensor_scalar(stat[:, 21:22], stat[:, 20:21], -LAM_INIT, None, ALU.add))
            dve.wait_ge(s_trig, 1)
            chain(nc.vector.tensor_scalar(sinb[:], sinb[:], con("sign"), None, ALU.mult))

        @block.tensor
        def _(pe):
            pe.wait_ge(s_cst, 16)
            pe.wait_ge(s_xn, NT)
            for k in range(KT):
                for t in range(NT):
                    last = nc.tensor.transpose(bank(k, t * P, t * P + P), xn[:, t, k * P:(k + 1) * P], ident)
                if k == 0:
                    pe.sem_inc(s_prod, 2)
                last.then_inc(s_xt, 1)
            pe.wait_ge(s_hl, KT)

            def tile(n, i, u):
                pe.wait_ge(s_wlo, n + 3)
                for k in range(KT):
                    pairs = ((w_hi, h_hi), (w_hi, h_lo), (w_lo, h_hi))
                    for m, (w, h) in enumerate(pairs):
                        last = nc.tensor.matmul(bank(u), w[:, u, k, :], h[:, k, :], start=k == 0 and m == 0,
                                                stop=k == KT - 1 and m == 2)
                last.then_inc(s_prod, 1)

            for u in range(2):
                tile(u, 0, u)
            with pe.Fori(1, IN_TILES // 2) as i:
                for u in range(2):
                    pe.wait_ge(s_out, i * 2 + (u - 1))
                    tile(i * 2 + u, i, u)


MIX_PE = (["lora_w", "lora_a", "kk_sum", "lora_g", "v_turn", "rope_swap", "mb0", "mk0", "t_kappa", "mb1", "x_turn0", "mk1",
           "t_beta", "x_turn1", "bonus", "t_khat"]
          + [n for lv in range(5) for n in [f"t{lv}_0", f"o{lv - 1}" if lv else "t_v"] + [f"t{lv}_1"] + [f"score{lv}"] * (lv < NT)
             + [f"x{lv}_0", f"x{lv}_1"] + [f"a_turn{lv}"] * (lv < NT)]
          + ["akv", "o_turn", "wu0", "wu1", "q", "chunk"] + [f"z{c}" for c in range(1, 7)] + ["y", "y_turn"])
MIX_ACT = (["sig_w", "v_copy", "kk_sq", "sig_a", "kk_norm", "gate", "exps", "v_major", "e_kappa", "x_major0", "e_beta",
            "x_major1", "e_khat", "e_v"]
           + [f"{a}{i}" for i in range(NT) for a in ("exp", "a_major", "o_copy")]
           + ["o_sd", "e_akv", "e_wu0", "e_wu1", "y_sd"])
MIX_DVE = (["shift_k", "mix_k", "kk0", "shift_r", "shift_v", "mix_", "lsum", "lprev", "qc", "kc", "kk_max", "kk_inv", "kk",
            "kappa", "b", "beta", "am", "kmod", "qs", "ks", "rhat", "khat", "rk", "q", "k"]
           + [f"{a}{h}" for h in range(2) for a in ("emb", "x1a", "x1b", "emk")] + ["bon"]
           + [n for lv in range(5) for n in [f"et{lv}_0", f"et{lv}_1"] + [f"masked{lv}", f"max{lv}"] * (lv < NT) + [f"ex{lv}_0"]
              + [f"{a}{lv}" for a in ("rl", "nl", "p2", "a")] * (lv < NT) + [f"ex{lv}_1"]]
           + ["o_rs", "o_n", "o_out", "eg", "eh", "e_q"] + [f"z{c}" for c in range(1, 8)]
           + ["y_sum", "y_mean", "y_c", "y_sq", "y_var", "y_rs", "y_n", "ot1", "ot2", "ot3"])


def mix(nc, d, sb, sem, st, g, con, ident, psum, bank):
    cols, stat, pall, cosb, sinb, o_t = (g[k] for k in ("cols", "stat", "pall", "cosb", "sinb", "o_t"))
    PE = Steps(sem("mix_tensor_steps"), MIX_PE)
    AC = Steps(sem("mix_scalar_steps"), MIX_ACT)
    DV = Steps(sem("mix_vector_steps"), MIX_DVE)
    s_lora, s_set, s_set2, s_gp = sem("lora_loaded"), sem("mix_set"), sem("mix_set2"), sem("mix_zeroed")
    s_par = sem("pair_params_loaded")
    wa = sb(st, "wa", [P, S])
    sg = sb(st, "sg", [P, S])
    par = sb(st, "par", [P, NPAR])
    lj = sb(st, "lj", [P, 2, P])
    rkv = sb(st, "rkv", [P, 3, S])
    w3 = sb(st, "w3", [P, 3, S])
    r_, k_, v_ = rkv[:, 0, :], rkv[:, 1, :], rkv[:, 2, :]
    lsum, lprev, kk = w3[:, 0, :], w3[:, 1, :], w3[:, 2, :]
    sg_w = sb(st, "sg_w", [P, S])
    gate = sb(st, "gate", [P, S])
    aa = sb(st, "aa", [P, S])
    pe_ = sb(st, "p_end", [P, S])
    pi_ = sb(st, "p_inv", [P, S])
    pp_ = sb(st, "p_prev", [P, S])
    sq = sb(st, "sq", [P, S])
    beta = sb(st, "beta", [P, S])
    khat = sb(st, "khat", [P, S])
    kr = sb(st, "kr", [P, NT, 2, P])
    ab = sb(st, "ab", [P, 2, NT, 2, P])
    ak = sb(st, "ak", [P, 2, NT, 2, P])
    xx = sb(st, "xx", [P, 2, NT, 2, P])
    t1 = sb(st, "t1", [P, 2, NT, P])
    bn = sb(st, "bn", [P, NT, P])
    kh = sb(st, "kh", [P, NT, P])
    vt = sb(st, "vt", [P, NT, P])
    rh = sb(st, "rh", [P, 2, NT, P])
    wu = sb(st, "wu", [P, 2, NT, P])
    gt = sb(st, "gt", [P, NCH, P])
    zz = sb(st, "zz", [P, NCH, CH])
    hp = t1[:, 0].rearrange("p t c -> p (t c)").rearrange("p (n k) -> p n k", k=CH)
    qt = t1[:, 1]
    yc, ysq, yn = pe_, pi_, pp_
    vf = sb(st, "vf", [P, S])
    vm = sb(st, "vm", [P, NT, P])
    qr = sb(st, "qr", [P, S])
    kro = sb(st, "kro", [P, S])
    sc = sb(st, "sc", [P, 2, S])
    am, at_ = beta, khat
    on = vf
    ast = sb(st, "ast", [P, 48])
    pg = pall[:, 0:24, :].rearrange("p (g j) t -> p g j t", j=HEADS)

    def tile_of(group, j, shift=1):
        return pg[:, group, bass.ds(j, 1), shift:shift + S].rearrange("p a s -> p (a s)")

    block = st.enter_context(nc.Block())

    @block.sync
    def _(sp):
        base = KT + 2
        with sp.Fori(0, HEADS) as j:
            sp.wait_ge(PE.sem, PE.before(j, "lora_g"))
            sp.dma_start(lj[:, 0, :], d["w2a2"][:, bass.ds(j * P, P)]).then_inc(s_lora, 16)
            sp.dma_start(lj[:, 1, :], d["g2"][:, bass.ds(j * P, P)]).then_inc(s_lora, 16)
            sp.wait_ge(DV.sem, DV.before(j, "ot1"))
            sp.dma_start(par[:], d["cols"][:, bass.ds(j * NPAR + base, NPAR)]).then_inc(s_par, 16)

    @block.gpsimd
    def _(pool):
        nc.gpsimd.memset(gt[:], 0.0)
        nc.gpsimd.memset(zz[:, 0, :], 0.0).then_inc(s_gp, 1)
        pool.wait_ge(s_gp, 1)

    @block.scalar
    def _(act):
        act.wait_ge(s_set, 2)
        act.sem_inc(AC.sem, AC.ahead() - 1)
        nc.scalar.activation(wa[0:64], sq[0:64], ACT.Tanh)
        nc.scalar.activation(wa[64:128], sq[64:128], ACT.Copy)
        nc.scalar.activation(sg[:], aa[:], ACT.Sigmoid).then_inc(AC.sem, 1)
        with act.Fori(0, HEADS) as j:
            act.wait_ge(s_par, j * 16 + 16)
            act.wait_ge(PE.sem, PE.reached(j, "lora_w"))
            nc.scalar.activation(sg_w[:], bank(4), ACT.Sigmoid, bias=par[:, 3:4]).then_inc(AC.sem, AC.step("sig_w"))
            nc.scalar.activation(vf[:], tile_of(2, j), ACT.Copy).then_inc(AC.sem, AC.step("v_copy"))
            act.wait_ge(DV.sem, DV.reached(j, "kk0"))
            nc.scalar.activation(sq[:], kk, ACT.Square).then_inc(AC.sem, AC.step("kk_sq"))
            act.wait_ge(PE.sem, PE.reached(j, "lora_a"))
            nc.scalar.activation(aa[:], bank(5), ACT.Sigmoid, bias=par[:, 4:5]).then_inc(AC.sem, AC.step("sig_a"))
            act.wait_ge(PE.sem, PE.reached(j, "kk_sum"))
            nc.scalar.activation(sq[:], bank(7), ACT.Sqrt).then_inc(AC.sem, AC.step("kk_norm"))
            act.wait_ge(PE.sem, PE.reached(j, "lora_g"))
            nc.scalar.activation(gate[:], bank(6), ACT.Copy).then_inc(AC.sem, AC.step("gate"))
            act.wait_ge(DV.sem, DV.reached(j, "lprev"))
            nc.scalar.activation(pe_[:], lsum, ACT.Exp, scale=-E_HALF)
            nc.scalar.activation(pi_[:], lsum, ACT.Exp, scale=E_HALF)
            nc.scalar.activation(pp_[:], lprev, ACT.Exp, scale=-E_HALF).then_inc(AC.sem, AC.step("exps"))
            act.wait_ge(PE.sem, PE.reached(j, "v_turn"))
            nc.scalar.activation(vm[:].rearrange("p a b -> p (a b)"), bank(2), ACT.Copy).then_inc(AC.sem, AC.step("v_major"))

            def x_major(h):
                act.wait_ge(PE.sem, PE.reached(j, f"x_turn{h}"))
                nc.scalar.activation(xx[:, h, :, 0, :], bank(4 + h).rearrange("p (t c) -> p t c", c=P), ACT.Copy).then_inc(
                    AC.sem, AC.step(f"x_major{h}"))

            act.wait_ge(PE.sem, PE.reached(j, "t_kappa"))
            for h in range(2):
                last = nc.scalar.activation(rh[:, h, :, 0:64], bank(6).rearrange("p (t h c) -> p t h c", h=2, c=64)[:, :, h, :], ACT.Copy)
            last.then_inc(AC.sem, AC.step("e_kappa"))
            x_major(0)
            act.wait_ge(PE.sem, PE.reached(j, "t_beta"))
            nc.scalar.activation(bn[:].rearrange("p a b -> p (a b)"), bank(7), ACT.Copy, scale=-1.0).then_inc(AC.sem, AC.step("e_beta"))
            x_major(1)
            act.wait_ge(PE.sem, PE.reached(j, "t_khat"))
            nc.scalar.activation(kh[:].rearrange("p a b -> p (a b)"), bank(6), ACT.Copy).then_inc(AC.sem, AC.step("e_khat"))
            act.wait_ge(PE.sem, PE.reached(j, "t_v"))
            nc.scalar.activation(vt[:].rearrange("p a b -> p (a b)"), bank(6), ACT.Copy).then_inc(AC.sem, AC.step("e_v"))
            for i in range(NT):
                n = (i + 1) * P
                act.wait_ge(DV.sem, DV.reached(j, f"max{i}"))
                for c in range(2):
                    last = nc.scalar.activation(sc[:, c, 0:n], sc[:, c, 0:n], ACT.Exp, bias=ast[:, 2 * i + c:2 * i + c + 1],
                                                accum_out=ast[:, 8 + 2 * i + c:9 + 2 * i + c])
                last.then_inc(AC.sem, AC.step(f"exp{i}"))
                act.wait_ge(PE.sem, PE.reached(j, f"a_turn{i}"))
                nc.scalar.activation(at_[:, 0:n], bank(6, 0, n), ACT.Copy).then_inc(AC.sem, AC.step(f"a_major{i}"))
                act.wait_ge(PE.sem, PE.reached(j, f"o{i}"))
                nc.scalar.activation(on[:, i * P:(i + 1) * P], bank(7, 0, P), ACT.Copy)
                nc.scalar.activation(sc[:, 0, 0:P], bank(7, 0, P), ACT.Square,
                                     accum_out=ast[:, 24 + i:25 + i]).then_inc(AC.sem, AC.step(f"o_copy{i}"))
            act.wait_ge(AC.sem, AC.reached(j, f"o_copy{NT - 1}"))
            nc.scalar.activation(ast[:, 28:32], ast[:, 24:28], ACT.Sqrt, bias=con("eps"), scale=1.0 / P).then_inc(AC.sem, AC.step("o_sd"))
            act.wait_ge(PE.sem, PE.reached(j, "akv"))
            nc.scalar.activation(rh[:, :, :, 64:128].rearrange("p h t c -> p (h t) c"),
                                 bank(4).rearrange("p (u c) -> p u c", c=64), ACT.Copy).then_inc(AC.sem, AC.step("e_akv"))
            for h in range(2):
                act.wait_ge(PE.sem, PE.reached(j, f"wu{h}"))
                nc.scalar.activation(wu[:, h].rearrange("p t c -> p (t c)"), bank(5 * (1 - h)), ACT.Copy).then_inc(AC.sem, AC.step(f"e_wu{h}"))
            act.wait_ge(DV.sem, DV.reached(j, "y_var"))
            nc.scalar.activation(ast[:, 40:48], ast[:, 32:40], ACT.Sqrt, bias=con("gn_eps"), scale=1.0 / CH).then_inc(AC.sem, AC.step("y_sd"))

    @block.vector
    def _(dve):
        for n, dst in ((0, sq), (1, aa)):
            t = 24 + n
            nc.vector.tensor_tensor(w3[:, n, :], pall[:, t, 0:S], pall[:, t, 1:S + 1], ALU.subtract).then_inc(s_set2, 1)
            dve.wait_ge(s_set2, n + 1)
            nc.vector.scalar_tensor_tensor(dst[:], w3[:, n, :], cols[:, KT + n:KT + n + 1], pall[:, t, 1:S + 1],
                                           ALU.mult, ALU.add).then_inc(s_set, 1)
        dve.wait_ge(s_set, 2)
        dve.sem_inc(DV.sem, DV.ahead() - 1)
        nc.vector.memset(ast[:, 0:1], 0.0).then_inc(DV.sem, 1)
        with dve.Fori(0, HEADS) as j:
            dve.wait_ge(DV.sem, DV.before(j, "ot3"))

            def own(name):
                dve.wait_ge(DV.sem, DV.reached(j, name))

            def masked(i):
                n = (i + 1) * P
                dve.wait_ge(PE.sem, PE.reached(j, f"score{i}"))
                mask = con("causal", (NT - 1 - i) * P, S)
                nc.vector.scalar_tensor_tensor(sc[:, :, 0:n], psum[:, 6:8, 0:n], 0.125,
                                               mask.rearrange("p (a n) -> p a n", a=1).to_broadcast([P, 2, n]),
                                               ALU.mult, ALU.add).then_inc(DV.sem, DV.step(f"masked{i}"))
                own(f"masked{i}")
                nc.vector.tensor_reduce(ast[:, 2 * i:2 * i + 2], sc[:, :, 0:n], AX.X, ALU.max, negate=True).then_inc(
                    DV.sem, DV.step(f"max{i}"))

            def weights(i):
                n = (i + 1) * P
                dve.wait_ge(AC.sem, AC.reached(j, f"exp{i}"))
                nc.vector.reciprocal(ast[:, 16:18], ast[:, 8 + 2 * i:10 + 2 * i]).then_inc(DV.sem, DV.step(f"rl{i}"))
                own(f"rl{i}")
                nc.vector.tensor_tensor(ast[:, 18:19], ast[:, 17:18], stat[:, 21:22], ALU.mult).then_inc(DV.sem, DV.step(f"nl{i}"))
                own(f"nl{i}")
                nc.vector.tensor_scalar(sc[:, 1, 0:n], sc[:, 1, 0:n], ast[:, 18:19], None, ALU.mult).then_inc(DV.sem, DV.step(f"p2{i}"))
                own(f"p2{i}")
                dve.wait_ge(PE.sem, PE.reached(j, f"a_turn{i - 1}" if i else "t_khat"))
                nc.vector.scalar_tensor_tensor(am[:, 0:n], sc[:, 0, 0:n], ast[:, 16:17], sc[:, 1, 0:n], ALU.mult,
                                               ALU.add).then_inc(DV.sem, DV.step(f"a{i}"))

            def shift(n, name, dst):
                nc.vector.tensor_tensor(dst, tile_of(3 + n, j, 0), tile_of(3 + n, j), ALU.subtract).then_inc(DV.sem, DV.step(name))

            def mix_in(n, diff):
                return nc.vector.scalar_tensor_tensor(rkv[:, n, :], diff, par[:, n:n + 1], tile_of(3 + n, j), ALU.mult, ALU.add)

            shift(1, "shift_k", w3[:, 1, :])
            own("shift_k")
            dve.wait_ge(s_par, j * 16 + 16)
            mix_in(1, w3[:, 1, :]).then_inc(DV.sem, DV.step("mix_k"))
            own("mix_k")
            nc.vector.tensor_scalar(kk, k_, par[:, 5:6], None, ALU.mult).then_inc(DV.sem, DV.step("kk0"))
            shift(0, "shift_r", w3[:, 0, :])
            shift(2, "shift_v", beta[:])
            own("shift_v")
            mix_in(0, w3[:, 0, :])
            mix_in(2, beta[:]).then_inc(DV.sem, DV.step("mix_"))
            own("mix_")
            dve.wait_ge(AC.sem, AC.reached(j, "sig_w"))
            nc.vector.tensor_tensor_scan(lsum, con("reset"), sg_w[:], 0.0, ALU.mult, ALU.add).then_inc(DV.sem, DV.step("lsum"))
            own("lsum")
            nc.vector.tensor_tensor(lprev, lsum, sg_w[:], ALU.subtract).then_inc(DV.sem, DV.step("lprev"))
            rope = (("q", 0, qr), ("k", 1, kro))
            for a, group, dst in rope:
                nc.vector.tensor_tensor(dst[:], tile_of(group, j), cosb[:], ALU.mult).then_inc(DV.sem, DV.step(a + "c"))
            dve.wait_ge(AC.sem, AC.reached(j, "kk_norm"))
            nc.vector.tensor_scalar(sq[:], sq[:], 1e-12, None, ALU.max).then_inc(DV.sem, DV.step("kk_max"))
            own("kk_max")
            nc.vector.reciprocal(sq[:], sq[:]).then_inc(DV.sem, DV.step("kk_inv"))
            own("kk_inv")
            nc.vector.tensor_tensor(kk, kk, sq[:], ALU.mult).then_inc(DV.sem, DV.step("kk"))
            own("kk")

            def tiles(a):
                return a.rearrange("p (t c) -> p t c", c=P)

            dve.wait_ge(AC.sem, AC.reached(j, "exps"))
            nc.vector.tensor_tensor(kr[:, :, 0, :], tiles(kk), tiles(pp_[:]), ALU.mult).then_inc(DV.sem, DV.step("kappa"))
            nc.vector.tensor_tensor(sq[:], kk, aa[:], ALU.mult).then_inc(DV.sem, DV.step("b"))
            own("b")
            nc.vector.tensor_tensor(beta[:], sq[:], pi_[:], ALU.mult).then_inc(DV.sem, DV.step("beta"))
            nc.vector.tensor_scalar(aa[:], aa[:], 1.0, par[:, 6:7], ALU.subtract, ALU.mult).then_inc(DV.sem, DV.step("am"))
            own("am")
            nc.vector.scalar_tensor_tensor(k_, aa[:], 1.0, k_, ALU.add, ALU.mult).then_inc(DV.sem, DV.step("kmod"))
            dve.wait_ge(PE.sem, PE.reached(j, "rope_swap"))
            for a, group, dst in rope:
                nc.vector.tensor_tensor(sc[:, group, :], bank(group), sinb[:], ALU.mult).then_inc(DV.sem, DV.step(a + "s"))
            nc.vector.tensor_tensor(kr[:, :, 1, :], tiles(r_), tiles(pe_[:]), ALU.mult).then_inc(DV.sem, DV.step("rhat"))
            own("kmod")
            nc.vector.tensor_tensor(khat[:], k_, pi_[:], ALU.mult).then_inc(DV.sem, DV.step("khat"))
            nc.vector.scalar_tensor_tensor(r_, r_, par[:, 7:8], k_, ALU.mult, ALU.mult).then_inc(DV.sem, DV.step("rk"))
            own("ks")
            for a, group, dst in rope:
                nc.vector.tensor_tensor(dst[:], dst[:], sc[:, group, :], ALU.add).then_inc(DV.sem, DV.step(a))
            for h in range(2):
                def mask_products(a, b0, dst, msk):
                    dve.wait_ge(PE.sem, PE.reached(j, f"m{a}{h}"))
                    nc.vector.tensor_tensor(dst[:, h].rearrange("p t a c -> p t (a c)"),
                                            psum[:, b0:b0 + 2, :].rearrange("p b (t c) -> p (b t) c", c=2 * P),
                                            con(msk).rearrange("p (a n) -> p a n", a=1).to_broadcast([P, NT, 2 * P]),
                                            ALU.mult).then_inc(DV.sem, DV.step(f"em{a}{h}"))

                mask_products("b", 0, ab, "mask_b")
                own(f"emb{h}")
                nc.vector.tensor_tensor(t1[:, h], ab[:, h, :, 0, :],
                                        con("level1").rearrange("p (a n) -> p a n", a=1).to_broadcast([P, NT, P]),
                                        ALU.mult).then_inc(DV.sem, DV.step(f"x1a{h}"))
                own(f"x1a{h}")
                nc.vector.tensor_tensor(xx[:, h, :, 1, :], ident.rearrange("p (a n) -> p a n", a=1).to_broadcast([P, NT, P]),
                                        t1[:, h], ALU.subtract).then_inc(DV.sem, DV.step(f"x1b{h}"))
                mask_products("k", 2, ak, "mask_k")
            dve.wait_ge(PE.sem, PE.reached(j, "bonus"))
            nc.vector.tensor_tensor(r_, bank(7), v_, ALU.mult).then_inc(DV.sem, DV.step("bon"))
            for lv in range(5):
                for h in range(2):
                    dve.wait_ge(PE.sem, PE.reached(j, f"t{lv}_{h}"))
                    nc.vector.tensor_tensor(t1[:, h], bank(4 + h).rearrange("p (t c) -> p t c", c=P),
                                            con("levels", lv * P, lv * P + P).rearrange("p (a n) -> p a n", a=1).to_broadcast([P, NT, P]),
                                            ALU.mult).then_inc(DV.sem, DV.step(f"et{lv}_{h}"))
                if lv < NT:
                    masked(lv)
                for h in range(2):
                    if h and lv < NT:
                        weights(lv)
                    dve.wait_ge(PE.sem, PE.reached(j, f"x{lv}_{h}"))
                    src = psum[:, 2 * h:2 * h + 2, :].rearrange("p b (t a c) -> p (b t) a c", a=2, c=P)
                    if lv < 4:
                        nc.vector.tensor_tensor(xx[:, h], xx[:, h], src, ALU.subtract).then_inc(DV.sem, DV.step(f"ex{lv}_{h}"))
                    else:
                        nc.vector.tensor_tensor(xx[:, h, :, 1, :], xx[:, h, :, 1, :], src[:, :, 1, :], ALU.subtract).then_inc(
                            DV.sem, DV.step(f"ex{lv}_{h}"))
            dve.wait_ge(AC.sem, AC.reached(j, "o_sd"))
            nc.vector.reciprocal(ast[:, 20:24], ast[:, 28:32]).then_inc(DV.sem, DV.step("o_rs"))
            own("o_rs")
            for i in range(NT):
                last = nc.vector.tensor_scalar(on[:, i * P:(i + 1) * P], on[:, i * P:(i + 1) * P], ast[:, 20 + i:21 + i],
                                               1.0 - LAM_INIT, ALU.mult, ALU.mult)
            last.then_inc(DV.sem, DV.step("o_n"))
            dve.wait_ge(PE.sem, PE.reached(j, "o_turn"))
            nc.vector.tensor_scalar(o_t[:, bass.ds(j, 1), :].rearrange("p a s -> p (a s)"), bank(6),
                                    cols[:, KT + 2 + HEADS * NPAR:KT + 3 + HEADS * NPAR], None, ALU.mult).then_inc(DV.sem, DV.step("o_out"))
            dve.wait_ge(s_gp, 1)
            dve.wait_ge(PE.sem, PE.reached(j, "chunk"))
            for h in range(2):
                rows = slice(64 * h, 64 * h + 64)
                last = nc.vector.tensor_tensor(
                    gt[rows, :, 64 * h:64 * h + 64].rearrange("p (t c) k -> p c t k", c=2),
                    psum[rows, 0:2, 0:256].rearrange("p c (t k) -> p c t k", k=64),
                    con("stack")[rows].rearrange("p (a b k) -> p a b k", a=1, b=1).to_broadcast([64, 2, NT, 64]), ALU.add)
            last.then_inc(DV.sem, DV.step("eg"))
            decay_end = pe_[:].rearrange("p (t c k) -> p c t k", c=2, k=64)[:, :, :, 63:64]
            nc.vector.tensor_tensor(hp[:].rearrange("p (t c) k -> p c t k", c=2),
                                    psum[:, 0:2, 256:512].rearrange("p c (t k) -> p c t k", k=64),
                                    decay_end.to_broadcast([P, 2, NT, 64]), ALU.mult).then_inc(DV.sem, DV.step("eh"))
            dve.wait_ge(PE.sem, PE.reached(j, "q"))
            nc.vector.tensor_tensor(qt[:], bank(3).rearrange("p (t c) -> p t c", c=P), kr[:, :, 1, :], ALU.add).then_inc(
                DV.sem, DV.step("e_q"))
            own("eh")
            nc.vector.tensor_copy(zz[:, 1, :], hp[:, 0, :]).then_inc(DV.sem, DV.step("z1"))
            for c in range(1, 7):
                dve.wait_ge(PE.sem, PE.reached(j, f"z{c}"))
                nc.vector.scalar_tensor_tensor(zz[:, c + 1, :], bank(2, c * 64, c * 64 + 64), pe_[:, 64 * c + 63:64 * c + 64],
                                               hp[:, c, :], ALU.mult, ALU.add).then_inc(DV.sem, DV.step(f"z{c + 1}"))
            own("z7")
            dve.wait_ge(PE.sem, PE.reached(j, "y"))
            yb = psum[:, 4:6, 0:256].rearrange("p h (t v) -> p h t v", v=64)
            y4 = yc[:].rearrange("p (h t v) -> p h t v", h=2, v=64)
            nc.vector.tensor_reduce(ast[:, 32:40], yb, AX.X, ALU.add).then_inc(DV.sem, DV.step("y_sum"))
            own("y_sum")
            nc.vector.tensor_scalar(ast[:, 40:48], ast[:, 32:40], -1.0 / CH, None, ALU.mult).then_inc(DV.sem, DV.step("y_mean"))
            own("y_mean")

            def per_head(a):
                return a.rearrange("p (h t v) -> p h t v", h=2, v=1).to_broadcast([P, 2, NT, 64])

            nc.vector.tensor_tensor(y4, yb, per_head(ast[:, 40:48]), ALU.add).then_inc(DV.sem, DV.step("y_c"))
            own("y_c")
            nc.vector.tensor_tensor(ysq[:], yc[:], yc[:], ALU.mult).then_inc(DV.sem, DV.step("y_sq"))
            own("y_sq")
            nc.vector.tensor_reduce(ast[:, 32:40], ysq[:].rearrange("p (u v) -> p u v", v=64), AX.X, ALU.add).then_inc(
                DV.sem, DV.step("y_var"))
            dve.wait_ge(AC.sem, AC.reached(j, "y_sd"))
            nc.vector.reciprocal(ast[:, 32:40], ast[:, 40:48]).then_inc(DV.sem, DV.step("y_rs"))
            own("y_rs")
            nc.vector.tensor_tensor(yn[:].rearrange("p (t h v) -> p h t v", h=2, v=64), y4, per_head(ast[:, 32:40]),
                                    ALU.mult).then_inc(DV.sem, DV.step("y_n"))
            dve.wait_ge(PE.sem, PE.reached(j, "y_turn"))
            nc.vector.tensor_scalar(kk, bank(7), par[:, 8:9], par[:, 9:10], ALU.mult, ALU.add).then_inc(DV.sem, DV.step("ot1"))
            own("ot1")
            nc.vector.tensor_tensor(kk, kk, r_, ALU.add).then_inc(DV.sem, DV.step("ot2"))
            own("ot2")
            nc.vector.tensor_tensor(o_t[:, bass.ds(j + HEADS, 1), :].rearrange("p a s -> p (a s)"), kk, gate[:], ALU.mult).then_inc(
                DV.sem, DV.step("ot3"))

    @block.tensor
    def _(pe):
        pe.wait_ge(AC.sem, AC.ahead())
        pe.sem_inc(PE.sem, PE.ahead())
        with pe.Fori(0, HEADS) as j:
            pe.wait_ge(s_lora, j * 32 + 32)

            def dv(name):
                pe.wait_ge(DV.sem, DV.reached(j, name))

            def ac(name):
                pe.wait_ge(AC.sem, AC.reached(j, name))

            def scores(i):
                n = (i + 1) * P
                for c in range(2):
                    rows = slice(64 * c, 64 * c + 64)
                    last = nc.tensor.matmul(bank(6 + c, 0, n), qr[rows, i * P:(i + 1) * P], kro[rows, 0:n], start=True, stop=True)
                last.then_inc(PE.sem, PE.step(f"score{i}"))

            def turn_weights(i):
                dv(f"a{i}")
                for b in range(i + 1):
                    last = nc.tensor.transpose(bank(6, b * P, b * P + P), am[:, b * P:(b + 1) * P], ident)
                last.then_inc(PE.sem, PE.step(f"a_turn{i}"))

            def output(i):
                ac(f"a_major{i}")
                for b in range(i + 1):
                    last = nc.tensor.matmul(bank(7, 0, P), at_[:, b * P:(b + 1) * P], vm[:, b, :], start=b == 0, stop=b == i)
                last.then_inc(PE.sem, PE.step(f"o{i}"))

            nc.tensor.matmul(bank(4), lj[0:64, 0, :], wa[0:64, :], start=True, stop=True).then_inc(PE.sem, PE.step("lora_w"))
            nc.tensor.matmul(bank(5), lj[64:128, 0, :], wa[64:128, :], start=True, stop=True).then_inc(PE.sem, PE.step("lora_a"))
            ac("kk_sq")
            nc.tensor.matmul(bank(7), con("heads"), sq[:], start=True, stop=True).then_inc(PE.sem, PE.step("kk_sum"))
            nc.tensor.matmul(bank(6), lj[:, 1, :], sg[:], start=True, stop=True).then_inc(PE.sem, PE.step("lora_g"))

            def turned(name, b, src):
                for t in range(NT):
                    last = nc.tensor.transpose(bank(b, t * P, t * P + P), src(t), ident)
                last.then_inc(PE.sem, PE.step(name))

            def cross(a, b0, src, h):
                rows = slice(64 * h, 64 * h + 64)
                for t in range(NT):
                    c0 = (t % 2) * 2 * P
                    last = nc.tensor.matmul(bank(b0 + t // 2, c0, c0 + 2 * P), src[rows, t * P:(t + 1) * P],
                                            kr[rows, t, :, :].rearrange("p a c -> p (a c)"), start=True, stop=True)
                last.then_inc(PE.sem, PE.step(f"m{a}{h}"))

            ac("v_copy")
            turned("v_turn", 2, lambda t: vf[:, t * P:(t + 1) * P])
            dv("kk")
            nc.tensor.matmul(bank(0), con("swap"), tile_of(0, j), start=True, stop=True)
            nc.tensor.matmul(bank(1), con("swap"), tile_of(1, j), start=True, stop=True).then_inc(PE.sem, PE.step("rope_swap"))
            dv("rhat")
            cross("b", 0, beta, 0)
            dv("khat")
            ac("v_major")
            cross("k", 2, khat, 0)
            turned("t_kappa", 6, lambda t: kr[:, t, 0, :])
            dv("emb0")
            cross("b", 0, beta, 1)
            dv("x1b0")
            turned("x_turn0", 4, lambda t: xx[:, 0, t, 1, :])
            dv("emk0")
            cross("k", 2, khat, 1)
            turned("t_beta", 7, lambda t: beta[:, t * P:(t + 1) * P])
            dv("x1b1")
            turned("x_turn1", 5, lambda t: xx[:, 1, t, 1, :])
            ac("e_beta")
            nc.tensor.matmul(bank(7), con("heads"), r_, start=True, stop=True).then_inc(PE.sem, PE.step("bonus"))
            turned("t_khat", 6, lambda t: khat[:, t * P:(t + 1) * P])
            for lv in range(5):
                for h in range(2):
                    if lv == 0:
                        ac(f"x_major{h}")
                    else:
                        dv(f"ex{lv - 1}_{h}")
                    for t in range(NT):
                        last = nc.tensor.matmul(bank(4 + h, t * P, t * P + P), ab[:, h, t, 0, :], xx[:, h, t, 0, :], start=True, stop=True)
                    last.then_inc(PE.sem, PE.step(f"t{lv}_{h}"))
                    if lv and not h:
                        output(lv - 1)
                    elif not h:
                        ac("e_khat")
                        turned("t_v", 6, lambda t: v_[:, t * P:(t + 1) * P])
                if lv < NT:
                    if not lv:
                        dv("bon")
                    ac(f"o_copy{lv - 1}" if lv else "e_v")
                    scores(lv)
                for h in range(2):
                    dv(f"et{lv}_{h}")
                    for t in range(NT):
                        b, c0 = 2 * h + t // 2, (t % 2) * 2 * P
                        if lv < 4:
                            nc.tensor.matmul(bank(b, c0, c0 + P), xx[:, h, t, 1, :], t1[:, h, t, :], start=True, stop=True)
                        last = nc.tensor.matmul(bank(b, c0 + P, c0 + 2 * P), t1[:, h, t, :], xx[:, h, t, 1, :], start=True, stop=True)
                    last.then_inc(PE.sem, PE.step(f"x{lv}_{h}"))
                if lv < NT:
                    turn_weights(lv)
            dv("ex4_1")
            for h in range(2):
                for t in range(NT):
                    u = h * NT + t
                    last = nc.tensor.matmul(bank(4, u * 64, u * 64 + 64), ak[:, h, t, 0, :], vt[:, t, 64 * h:64 * h + 64], start=True, stop=True)
            last.then_inc(PE.sem, PE.step("akv"))
            dv("o_n")
            for t in range(NT):
                last = nc.tensor.transpose(bank(6, t * P, t * P + P), on[:, t * P:(t + 1) * P], ident)
            last.then_inc(PE.sem, PE.step("o_turn"))
            ac("e_akv")
            for h in range(2):
                for t in range(NT):
                    last = nc.tensor.matmul(bank(5 * (1 - h), t * P, t * P + P), xx[:, h, t, 1, :], rh[:, h, t, :], start=True, stop=True)
                last.then_inc(PE.sem, PE.step(f"wu{h}"))
            ac("e_wu1")
            for h in range(2):
                for t in range(NT):
                    last = nc.tensor.matmul(bank(3, t * P, t * P + P, slice(64 * h, 64 * h + 64)), wu[:, h, t, 0:64], ab[:, h, t, 1, :],
                                            start=True, stop=True)
            last.then_inc(PE.sem, PE.step("q"))
            for c in range(2):
                tok = slice(64 * c, 64 * c + 64)
                for h in range(2):
                    hs, rows = slice(64 * h, 64 * h + 64), slice(64 * h, 64 * h + 64)
                    for t in range(NT):
                        nc.tensor.matmul(bank(c, t * 64, t * 64 + 64, rows), wu[tok, h, t, 0:64], bn[tok, t, hs], start=True, stop=True)
                        o = bank(c, 256 + t * 64, 320 + t * 64, rows)
                        nc.tensor.matmul(o, kh[tok, t, hs], vt[tok, t, hs], start=True, stop=False)
                        last = nc.tensor.matmul(o, bn[tok, t, hs], wu[tok, h, t, 64:128], start=False, stop=True)
            last.then_inc(PE.sem, PE.step("chunk"))

            def y_within(u):
                h, t = u // NT, u % NT
                o = bank(4 + h, t * 64, t * 64 + 64)
                nc.tensor.matmul(o, ak[:, h, t, 1, :], vt[:, t, 64 * h:64 * h + 64], start=t == 0, stop=False)
                nc.tensor.matmul(o, ab[:, h, t, 1, :], wu[:, h, t, 64:128], start=False, stop=False)

            y_within(0)
            y_within(1)
            for c in range(1, 7):
                dv(f"z{c}")
                nc.tensor.matmul(bank(2, c * 64, c * 64 + 64), gt[:, c, :], zz[:, c, :], start=True, stop=True).then_inc(
                    PE.sem, PE.step(f"z{c}"))
                if c < 6:
                    y_within(c + 1)
            dv("z7")
            y_within(7)
            for h in range(2):
                rows = slice(64 * h, 64 * h + 64)
                for t in range(NT):
                    for c in range(2):
                        tok = slice(64 * c, 64 * c + 64)
                        last = nc.tensor.matmul(bank(4 + h, t * 64, t * 64 + 64, tok), qt[rows, t, tok], zz[rows, 2 * t + c, :],
                                                start=False, stop=t == NT - 1)
            last.then_inc(PE.sem, PE.step("y"))
            dv("y_n")
            for t in range(NT):
                last = nc.tensor.transpose(bank(7, t * P, t * P + P), yn[:, t * P:(t + 1) * P], ident)
            last.then_inc(PE.sem, PE.step("y_turn"))


def output_and_route(nc, d, sb, sem, st, g, con, ident, psum, bank):
    x, stat, o_t, rank, info, flags = (g[k] for k in ("x", "stat", "o_t", "rank", "info", "flags"))
    s_w = [sem(f"w_out_loaded{k}") for k in range(KT)]
    s_rw, s_fw, s_oh, s_ol = sem("router_loaded"), sem("ffn_norm_loaded"), sem("o_hi"), sem("o_lo")
    s_wh, s_wl, s_acc, s_x2, s_ss = sem("w_out_hi"), sem("w_out_lo"), sem("out_projected"), sem("x2_ready"), sem("x2_squared")
    s_sd, s_rs, s_h2, s_store = sem("x2_deviation"), sem("x2_rstd"), sem("h2_ready"), sem("h2_stored")
    s_turn, s_h2t, s_log, s_rt = sem("h2_turned"), sem("h2t_ready"), sem("logits_ready"), sem("route_steps")
    s_exp, s_mask, s_rank = sem("gate_exp"), sem("choice_mask"), sem("ranks_ready")
    wo = sb(st, "wo_raw", [P, KT, D])
    wh = sb(st, "wo_hi", [P, KT, D], F32R)
    wl = sb(st, "wo_lo", [P, KT, D], F32R)
    oh = sb(st, "o_hi_sb", [P, KT, S], F32R)
    ol = sb(st, "o_lo_sb", [P, KT, S], F32R)
    h2 = wo[:, 0:4, :]
    h2t = wo[:, 4:8, :].rearrange("p a (b s) -> p (a b) s", s=S)
    fw = sb(st, "fw", [P, D])
    rw = sb(st, "rw", [P, KT, EXPERTS])
    rb = sb(st, "rb", [1, EXPERTS])
    lg = sb(st, "lg", [P, NT, EXPERTS])
    top8 = sb(st, "top8", [P, NT, 8])
    idx8 = sb(st, "idx8", [P, NT, 8], U32)
    idxf = sb(st, "idxf", [P, NT, 8])
    one = sb(st, "one_hot", [P, 4, NT, EXPERTS])
    mask = sb(st, "mask", [P, NT, EXPERTS])
    which = sb(st, "which", [P, NT, EXPERTS])
    eg = sb(st, "eg", [P, NT, EXPERTS])
    r1 = sb(st, "r1", [P, 32])
    w_v = d["w_out"][0].rearrange("(k p) n -> p k n", p=P)
    block = st.enter_context(nc.Block())

    def flat(t):
        return psum[:, 2 * t:2 * t + 2, :].rearrange("p b n -> p (b n)")

    @block.sync
    def _(sp):
        for k in range(KT):
            sp.dma_start(wo[:, k, :], w_v[:, k, :]).then_inc(s_w[k], 16)
        for t in range(NT):
            sp.wait_ge(s_h2, t + 1)
            sp.dma_start(g["h2_dram"][t * P:(t + 1) * P, :], h2[:, t, :]).then_inc(s_store, 16)
        sp.wait_ge(s_store, 16 * NT)

    @block.gpsimd
    def _(pool):
        nc.gpsimd.dma_start(fw[:], d["ffn_norm_w"].to_broadcast([P, D])).then_inc(s_fw, 16)
        nc.gpsimd.dma_start(rw[:], d["router_w"][0].rearrange("(k p) e -> p k e", p=P)).then_inc(s_rw, 16)
        nc.gpsimd.dma_start(rb[:], d["router_b"]).then_inc(s_rw, 16)
        pool.wait_ge(s_fw, 16)

    @block.scalar
    def _(act):
        nc.scalar.activation(oh[:], o_t[:], ACT.Copy).then_inc(s_oh, 1)
        for k in range(KT):
            act.wait_ge(s_w[k], 16)
            nc.scalar.activation(wh[:, k, :], wo[:, k, :], ACT.Copy).then_inc(s_wh, 1)
        for t in range(NT):
            act.wait_ge(s_wl, KT)
            act.wait_ge(s_x2, t + 1)
            last = nc.scalar.activation(h2[:, t, :], x[:, t, :], ACT.Square, accum_out=stat[:, 24 + t:25 + t])
        last.then_inc(s_ss, 1)
        act.wait_ge(s_ss, 1)
        nc.scalar.activation(stat[:, 28:32], stat[:, 24:28], ACT.Sqrt, bias=con("eps"), scale=1.0 / D).then_inc(s_sd, 1)
        for t in range(NT):
            act.wait_ge(s_turn, t + 1)
            nc.scalar.activation(h2t[:, :, t * P:(t + 1) * P], flat(t).rearrange("p (k c) -> p k c", c=P), ACT.Copy).then_inc(s_h2t, 1)
        act.wait_ge(s_rt, 9)
        for t in range(NT):
            last = nc.scalar.activation(eg[:, t, :], lg[:, t, :], ACT.Exp, bias=r1[:, t:t + 1])
        last.then_inc(s_exp, 1)

    @block.vector
    def _(dve):
        dve.wait_ge(s_oh, 1)
        nc.vector.tensor_tensor(ol[:], o_t[:], oh[:].bitcast(F32), ALU.subtract).then_inc(s_ol, 1)
        for k in range(KT):
            dve.wait_ge(s_wh, k + 1)
            nc.vector.tensor_tensor(wl[:, k, :], wo[:, k, :], wh[:, k, :].bitcast(F32), ALU.subtract).then_inc(s_wl, 1)
        for t in range(NT):
            dve.wait_ge(s_acc, t + 1)
            nc.vector.tensor_tensor(x[:, t, :], flat(t), x[:, t, :], ALU.add).then_inc(s_x2, 1)
        nc.vector.memset(info[:], 0.0)
        nc.vector.memset(rank[:], -1e6)
        dve.wait_ge(s_sd, 1)
        nc.vector.reciprocal(stat[:, 32:36], stat[:, 28:32]).then_inc(s_rs, 1)
        dve.wait_ge(s_rs, 1)
        dve.wait_ge(s_fw, 16)
        for t in range(NT):
            nc.vector.scalar_tensor_tensor(h2[:, t, :], x[:, t, :], stat[:, 32 + t:33 + t], fw[:], ALU.mult, ALU.mult).then_inc(s_h2, 1)
        n = 0

        def chain(ins):
            nonlocal n
            n += 1
            ins.then_inc(s_rt, 1)
            dve.wait_ge(s_rt, n)

        dve.wait_ge(s_log, 1)
        chain(nc.vector.tensor_copy(lg[:], bank(0, 0, NT * EXPERTS).rearrange("p (t e) -> p t e", e=EXPERTS)))
        for t in range(NT):
            nc.vector.max(top8[:, t, :], lg[:, t, :]).then_inc(s_rt, 1)
        n += NT
        dve.wait_ge(s_rt, n)
        for t in range(NT - 1):
            nc.vector.max_index(idx8[:, t, :], top8[:, t, :], lg[:, t, :]).then_inc(s_rt, 1)
        n += NT - 1
        nc.vector.max_index(idx8[:, NT - 1, :], top8[:, NT - 1, :], lg[:, NT - 1, :])
        chain(nc.vector.tensor_scalar(r1[:, 0:4], top8[:, :, 0], -1.0, None, ALU.mult))
        chain(nc.vector.tensor_copy(idxf[:], idx8[:]))
        for j in range(4):
            last = nc.vector.tensor_tensor(one[:, j], con("experts").rearrange("p (a e) -> p a e", a=1).to_broadcast([P, NT, EXPERTS]),
                                           idxf[:, :, j:j + 1].to_broadcast([P, NT, EXPERTS]), ALU.is_equal)
        chain(last)
        chain(nc.vector.tensor_tensor(mask[:], one[:, 0], one[:, 1], ALU.add))
        chain(nc.vector.tensor_tensor(mask[:], mask[:], one[:, 2], ALU.add))
        chain(nc.vector.tensor_tensor(mask[:], mask[:], one[:, 3], ALU.add))
        nc.vector.memset(r1[:, 31:32], 0.0).then_inc(s_mask, 1)
        chain(nc.vector.scalar_tensor_tensor(which[:], one[:, 2], 2.0, one[:, 1], ALU.mult, ALU.add))
        chain(nc.vector.scalar_tensor_tensor(which[:], one[:, 3], 3.0, which[:], ALU.mult, ALU.add))
        dve.wait_ge(s_exp, 1)
        chain(nc.vector.tensor_tensor(eg[:], eg[:], mask[:], ALU.mult))
        chain(nc.vector.tensor_reduce(r1[:, 4:8], eg[:], AX.X, ALU.add))
        chain(nc.vector.reciprocal(r1[:, 8:12], r1[:, 4:8]))
        nc.vector.tensor_tensor(info[:, :, 0:EXPERTS, 2], eg[:], r1[:, 8:12].rearrange("p (t a) -> p t a", a=1).to_broadcast([P, NT, EXPERTS]),
                                ALU.mult)
        chain(nc.vector.tensor_scalar(r1[:, 12:16], con("token"), 4.0, -BIG, ALU.mult, ALU.add))
        nc.vector.tensor_tensor(info[:, :, 0:EXPERTS, 1], which[:], r1[:, 12:16].rearrange("p (t a) -> p t a", a=1).to_broadcast([P, NT, EXPERTS]),
                                ALU.add)
        chain(nc.vector.tensor_scalar(r1[:, 16:20], con("token"), -BIG, None, ALU.add))
        nc.vector.tensor_copy(info[:, :, 0:EXPERTS, 0], r1[:, 16:20].rearrange("p (t a) -> p t a", a=1).to_broadcast([P, NT, EXPERTS]))
        chain(nc.vector.tensor_scalar(which[:], mask[:], 1e6, -1e6, ALU.mult, ALU.add))
        dve.wait_ge(s_rank, 1)
        nc.vector.tensor_tensor(rank[:, :, 0:EXPERTS], which[:], bank(1, 0, NT * EXPERTS).rearrange("p (t e) -> p t e", e=EXPERTS), ALU.add)
        chain(nc.vector.tensor_reduce(r1[:, 20:21], bank(1, NT * EXPERTS, (NT + 1) * EXPERTS), AX.X, ALU.max))
        for r in range(ROUNDS):
            last = nc.vector.tensor_scalar(flags[:, r:r + 1], r1[:, 20:21], float(P * r) if r else -1.0, None, ALU.is_gt)
        chain(last)

    @block.tensor
    def _(pe):
        pe.wait_ge(s_ol, 1)
        for k in range(KT):
            pe.wait_ge(s_wl, k + 1)
            for t in range(NT):
                for c in range(2):
                    for m, (o, w) in enumerate(((oh, wh), (oh, wl), (ol, wh))):
                        last = nc.tensor.matmul(bank(2 * t + c), o[:, k, t * P:(t + 1) * P], w[:, k, c * 512:(c + 1) * 512],
                                                start=k == 0 and m == 0, stop=k == KT - 1 and m == 2)
                if k == KT - 1:
                    last.then_inc(s_acc, 1)
        for t in range(NT):
            pe.wait_ge(s_h2, t + 1)
            for k in range(KT):
                last = nc.tensor.transpose(bank(2 * t + k // 4, (k % 4) * P, (k % 4) * P + P), h2[:, t, k * P:(k + 1) * P], ident)
            last.then_inc(s_turn, 1)
        pe.wait_ge(s_h2t, NT)
        pe.wait_ge(s_rw, 32)
        for t in range(NT):
            o = bank(0, t * EXPERTS, (t + 1) * EXPERTS)
            for k in range(KT):
                nc.tensor.matmul(o, h2t[:, k, t * P:(t + 1) * P], rw[:, k, :], start=k == 0, stop=False)
            last = nc.tensor.matmul(o, con("ones")[0:1, :], rb[:], start=False, stop=True)
        last.then_inc(s_log, 1)
        pe.wait_ge(s_mask, 1)
        for t in range(NT):
            o = bank(1, t * EXPERTS, (t + 1) * EXPERTS)
            for u in range(t):
                nc.tensor.matmul(o, con("ones"), mask[:, u, :], start=u == 0, stop=False)
            nc.tensor.matmul(o, con("before"), mask[:, t, :], start=t == 0, stop=True)
        for u in range(NT):
            last = nc.tensor.matmul(bank(1, NT * EXPERTS, (NT + 1) * EXPERTS), con("ones"), mask[:, u, :], start=u == 0, stop=u == NT - 1)
        last.then_inc(s_rank, 1)


def experts(nc, d, sb, sem, st, g, con, ident, psum, bank):
    rank, info, flags = g["rank"], g["info"], g["flags"]
    raw = sb(st, "w_pieces", [P, RAW, 2, D])
    hi = sb(st, "w_pieces_hi", [P, RING, 2, D], F32R)
    lo = sb(st, "w_pieces_lo", [P, RING, 2, D], F32R)
    xg = sb(st, "xg", [P, D])
    xh = sb(st, "xh", [P, KT, P], F32R)
    xl = sb(st, "xl", [P, KT, P], F32R)
    ah = sb(st, "ah", [P, KT, P], F32R)
    al = sb(st, "al", [P, KT, P], F32R)
    gg = sb(st, "gg", [P, 512])
    uu = sb(st, "uu", [P, 512])
    sg = sb(st, "sig", [P, 512])
    av = sb(st, "av", [P, 512])
    ys = sb(st, "ys", [P, D])
    sel = sb(st, "sel", [P, NT, P])
    pick = sb(st, "pick_e", [P, P], F32R)
    bias = sb(st, "bias", [P, 3 * D], F32R)
    next_i = sb(st, "next_i", [P, 2], I32)
    next_g = sb(st, "next_g", [P, 1])
    this_i = sb(st, "this_i", [P, 1], I32)
    this_g = sb(st, "this_g", [P, 1])
    s_raw = [sem(f"piece_loaded{p}") for p in range(PIECES)]
    s_hi, s_lo, s_used = sem("piece_hi"), sem("piece_lo"), sem("piece_used")
    s_bl, s_bh, s_bias, s_z = sem("bias_loaded"), sem("bias_hi"), sem("bias_split"), sem("zeroed")
    s_sel, s_imm, s_idx, s_copy, s_pick = sem("selected"), sem("index_summed"), sem("index_ready"), sem("index_moved"), sem("bias_row_picked")
    s_gath, s_tx, s_xh, s_xl = sem("rows_gathered"), sem("rows_turned"), sem("x_hi"), sem("x_lo")
    s_g, s_u, s_sig, s_act = sem("gate_clipped"), sem("up_steps"), sem("gate_sigmoid"), sem("act_ready")
    s_ta, s_ah, s_al, s_y, s_scat = sem("act_turned"), sem("act_hi"), sem("act_lo"), sem("y_ready"), sem("rows_scattered")
    s_round, s_stored, s_part = sem("round_moved"), sem("rows_stored"), sem("dma_about_to_start")
    block = st.enter_context(nc.Block())

    def rounds(eng, run):
        with eng.Fori(0, ROUNDS) as r:
            flag = eng.value_load(flags[0:1, bass.ds(r, 1)])
            with eng.If(flag == 1):
                run(r)

    @block.sync
    def _(sp):
        for rows in (slice(0, 32), slice(32, 64)):
            for w, c0, n in (("mlp1_b", 0, 2 * D), ("mlp2_b", 2 * D, D)):
                sp.dma_start(raw[rows].rearrange("p a b n -> p (a b n)")[:, c0:c0 + n], d[w][0]).then_inc(s_bl, 16)
        sp.wait_ge(s_bias, 1)

        def run(r):
            with sp.Fori(0, EXPERTS) as e:
                for p in range(PIECES):
                    sp.wait_ge(s_lo, (r * EXPERTS + e) * PIECES + (p + 1))
                    half, k = p // 4, p % 4
                    src = (d["mlp1_w"][0][bass.ds(e, 1), k * 256:(k + 1) * 256, half * D:(half + 1) * D] if half < 2
                           else d["mlp2_w"][0][bass.ds(e, 1), k * 256:(k + 1) * 256, :])
                    sp.dma_start(raw[:, p % RAW], src.rearrange("e (r p) n -> p (e r) n", p=P)).then_inc(s_raw[p], 16)

        rounds(sp, run)

    @block.gpsimd
    def _(pool):
        nc.gpsimd.memset(xg[:], 0.0).then_inc(s_z, 1)
        pool.wait_ge(s_z, 1)
        nc.gpsimd.memset(bias[64:128, :].bitcast(F32), 0.0).then_inc(s_z, 1)
        pool.wait_ge(s_z, 2)
        pool.sem_inc(s_stored, 1)

        def part_waits():
            pool.sem_inc(s_part, 1)

        def gather(m):
            pool.wait_ge(s_idx, m + 1)
            pool.wait_ge(s_tx, m * 2 + 1)
            part_waits()
            nc.gpsimd.indirect_dma_start(xg[:], None, g["h2_dram"], bass.IndirectOffsetOnAxis(next_i[:, 0:1], 0),
                                         bounds_check=S - 1, oob_is_err=False).then_inc(s_gath, 16)

        def scatter(turn):
            pool.wait_ge(s_copy, turn + 1)
            pool.wait_ge(s_y, turn + 2)
            part_waits()
            nc.gpsimd.indirect_dma_start(g["y_dram"], bass.IndirectOffsetOnAxis(this_i[:, 0:1], 0), ys[:], None,
                                         bounds_check=4 * S - 1, oob_is_err=False).then_inc(s_scat, 16)
            pool.wait_ge(s_scat, turn * 16 + 16)
            pool.sem_inc(s_stored, 1)

        def run(r):
            gather(r * TURNS)
            gather(r * TURNS + 1)
            with pool.Fori(1, EXPERTS) as e:
                scatter(r * EXPERTS + (e - 1))
                gather(r * TURNS + (e + 1))
            scatter(r * EXPERTS + (EXPERTS - 1))

        rounds(pool, run)

    @block.scalar
    def _(act):
        act.wait_ge(s_bl, 64)
        flat = raw[:].rearrange("p a b n -> p (a b n)")
        nc.scalar.activation(bias[0:32, :], flat[0:32, 0:3 * D], ACT.Copy)
        nc.scalar.activation(hi[:].rearrange("p a b n -> p (a b n)")[32:64, 0:3 * D], flat[32:64, 0:3 * D], ACT.Copy).then_inc(s_bh, 1)
        act.wait_ge(s_bias, 1)
        act.sem_inc(s_y, 1)

        def split(turn, p):
            act.wait_ge(s_raw[p], turn * 16 + 16)
            act.wait_ge(s_used, turn * PIECES + (p + 1))
            nc.scalar.activation(hi[:, p % RING], raw[:, p % RAW], ACT.Copy).then_inc(s_hi, 1)

        def x_hi(m, q):
            act.wait_ge(s_tx, m * 2 + (q + 2))
            nc.scalar.activation(xh[:, 4 * q:4 * q + 4, :].rearrange("p a b -> p (a b)"), bank(7), ACT.Copy).then_inc(s_xh, 1)

        def sigmoid(turn, h):
            act.wait_ge(s_g, turn * 2 + (h + 1))
            nc.scalar.activation(sg[:], gg[:], ACT.Sigmoid, scale=1.702).then_inc(s_sig, 1)

        def a_hi(turn, h):
            act.wait_ge(s_ta, turn * 2 + (h + 2))
            nc.scalar.activation(ah[:, 4 * h:4 * h + 4, :].rearrange("p a b -> p (a b)"), bank(6), ACT.Copy).then_inc(s_ah, 1)

        def y_out(turn):
            act.wait_ge(s_used, turn * PIECES + (PIECES + RING))
            act.wait_ge(s_copy, turn + 1)
            act.wait_ge(s_stored, turn + 1)
            nc.scalar.activation(ys[:], psum[:, 4:6, :].rearrange("p b n -> p (b n)"), ACT.Copy, scale=this_g[:, 0:1]).then_inc(s_y, 1)

        def body(r, e, first):
            turn = r * EXPERTS + e
            for p in range(PIECES):
                split(turn, p)
                if p == 1 and not first:
                    y_out(r * EXPERTS + (e - 1))
                if p == 6:
                    sigmoid(turn, 0)
                if p == 7:
                    a_hi(turn, 0)
                if p == 8:
                    x_hi(r * TURNS + (e + 1), 0)
                if p == 9:
                    sigmoid(turn, 1)
                if p == 10:
                    a_hi(turn, 1)
                    x_hi(r * TURNS + (e + 1), 1)

        def run(r):
            for q in range(2):
                x_hi(r * TURNS, q)
            body(r, 0, True)
            with act.Fori(1, EXPERTS) as e:
                body(r, e, False)
            y_out(r * EXPERTS + (EXPERTS - 1))

        rounds(act, run)

    @block.vector
    def _(dve):
        dve.wait_ge(s_bh, 1)
        hi_flat, raw_flat = (a[:].rearrange("p a b n -> p (a b n)") for a in (hi, raw))
        nc.vector.tensor_tensor(bias[32:64, :], raw_flat[32:64, 0:3 * D], hi_flat[32:64, 0:3 * D].bitcast(F32), ALU.subtract).then_inc(s_bias, 1)
        dve.wait_ge(s_bias, 1)
        dve.sem_inc(s_lo, RAW)
        dve.sem_inc(s_round, 1)
        dve.sem_inc(s_xl, 1)
        dve.sem_inc(s_act, 1)
        dve.sem_inc(s_al, 1)

        def split(turn, p):
            dve.wait_ge(s_hi, turn * PIECES + (p + 1))
            nc.vector.tensor_tensor(lo[:, p % RING], raw[:, p % RAW], hi[:, p % RING].bitcast(F32), ALU.subtract).then_inc(s_lo, 1)

        def select(m, e):
            dve.wait_ge(s_imm, m + 1)
            nc.vector.tensor_tensor(sel[:], con("slot").rearrange("p (a n) -> p a n", a=1).to_broadcast([P, NT, P]),
                                    rank[:, :, bass.ds(e, 1)].to_broadcast([P, NT, P]), ALU.is_equal).then_inc(s_sel, 1)

        def indices(m):
            dve.wait_ge(s_imm, m + 2)
            dve.wait_ge(s_tx, m * 2 + 1)
            nc.vector.tensor_scalar(next_i[:], bank(4, 0, 2), BIG, None, ALU.add)
            nc.vector.tensor_copy(next_g[:], bank(4, 2, 3)).then_inc(s_idx, 1)

        def move_indices(turn, m):
            dve.wait_ge(s_stored, turn + 1)
            dve.wait_ge(s_idx, m + 1)
            nc.vector.tensor_copy(this_i[:], next_i[:, 1:2])
            nc.vector.tensor_copy(this_g[:], next_g[:]).then_inc(s_copy, 1)

        def pick_bias(e, used):
            dve.wait_ge(s_used, used)
            nc.vector.tensor_copy(pick[:], con("pick")[:, bass.ds(e, 1)].to_broadcast([P, P])).then_inc(s_pick, 1)

        def x_lo(m, q):
            dve.wait_ge(s_xh, m * 2 + (q + 1))
            x4 = xh[:, 4 * q:4 * q + 4, :].rearrange("p a b -> p (a b)")
            nc.vector.tensor_tensor(xl[:, 4 * q:4 * q + 4, :].rearrange("p a b -> p (a b)"), bank(7), x4.bitcast(F32),
                                    ALU.subtract).then_inc(s_xl, 1)

        def a_lo(turn, h):
            dve.wait_ge(s_ah, turn * 2 + (h + 1))
            a4 = ah[:, 4 * h:4 * h + 4, :].rearrange("p a b -> p (a b)")
            nc.vector.tensor_tensor(al[:, 4 * h:4 * h + 4, :].rearrange("p a b -> p (a b)"), bank(6), a4.bitcast(F32),
                                    ALU.subtract).then_inc(s_al, 1)

        def swiglu(turn, h):
            dve.wait_ge(s_used, turn * PIECES + (4 * h + 4 + RING))
            pair = psum[:, 2 * h:2 * h + 2, :].rearrange("p b (n two) -> p (b n) two", two=2)
            nc.vector.tensor_scalar(gg[:], pair[:, :, 0], 7.0, None, ALU.min).then_inc(s_g, 1)
            nc.vector.tensor_scalar(uu[:], pair[:, :, 1], 7.0, -7.0, ALU.min, ALU.max).then_inc(s_u, 1)
            dve.wait_ge(s_g, turn * 2 + (h + 1))
            dve.wait_ge(s_u, turn * 4 + (2 * h + 1))
            nc.vector.scalar_tensor_tensor(uu[:], uu[:], 1.0, gg[:], ALU.add, ALU.mult).then_inc(s_u, 1)
            dve.wait_ge(s_u, turn * 4 + (2 * h + 2))
            dve.wait_ge(s_sig, turn * 2 + (h + 1))
            dve.wait_ge(s_ta, turn * 2 + (h + 1))
            nc.vector.tensor_tensor(av[:], uu[:], sg[:], ALU.mult).then_inc(s_act, 1)

        def body(r, e):
            turn = r * EXPERTS + e
            m = r * TURNS + (e + 1)
            for p in range(PIECES):
                split(turn, p)
                if p == 1:
                    select(m, e + 1)
                if p == 4:
                    move_indices(turn, r * TURNS + e)
                    dve.wait_ge(s_copy, turn + 1)
                    indices(m)
                if p == 5:
                    swiglu(turn, 0)
                if p == 7:
                    a_lo(turn, 0)
                if p == 8:
                    swiglu(turn, 1)
                    x_lo(m, 0)
                if p == 10:
                    a_lo(turn, 1)
                    x_lo(m, 1)
                    pick_bias(e + 1, turn * PIECES + (9 + RING))

        def run(r):
            dve.wait_ge(s_round, r + 1)
            select(r * TURNS, 0)
            indices(r * TURNS)
            pick_bias(0, r * (EXPERTS * PIECES) + RING)
            for q in range(2):
                x_lo(r * TURNS, q)
            body(r, 0)
            with dve.Fori(1, EXPERTS) as e:
                body(r, e)
            nc.vector.tensor_scalar(rank[:], rank[:], float(-P), None, ALU.add).then_inc(s_round, 1)

        rounds(dve, run)

    @block.tensor
    def _(pe):
        pe.wait_ge(s_z, 2)
        pe.wait_ge(s_bias, 1)
        pe.sem_inc(s_used, RING)
        pe.sem_inc(s_imm, 1)
        pe.sem_inc(s_tx, 1)
        pe.sem_inc(s_ta, 1)

        def index_sum(m, e, turn):
            pe.wait_ge(s_sel, m + 1)
            pe.wait_ge(s_y, turn + 1)
            for t in range(NT):
                last = nc.tensor.matmul(bank(4, 0, 4), sel[:, t, :], info[:, t, bass.ds(e, 1), :].rearrange("p a c -> p (a c)"),
                                        start=t == 0, stop=t == NT - 1)
            last.then_inc(s_imm, 1)

        def turn_x(m, q):
            if q == 0:
                pe.wait_ge(s_gath, m * 16 + 16)
            pe.wait_ge(s_xl, m * 2 + (q + 1))
            for k in range(4):
                last = nc.tensor.transpose(bank(7, k * P, k * P + P), xg[:, (4 * q + k) * P:(4 * q + k + 1) * P], ident)
            last.then_inc(s_tx, 1)

        def turn_a(turn, h):
            pe.wait_ge(s_act, turn * 2 + (h + 2))
            pe.wait_ge(s_al, turn * 2 + (h + 1))
            for k in range(4):
                last = nc.tensor.transpose(bank(6, k * P, k * P + P), av[:, k * P:(k + 1) * P], ident)
            last.then_inc(s_ta, 1)

        def piece(turn, p, ops, b0, k0, first, last_piece):
            if first:
                for c in range(2):
                    nc.tensor.matmul(bank(b0 + c), pick[:], bias[:, (b0 + c) * 512:(b0 + c + 1) * 512], start=True, stop=False)
            pe.wait_ge(s_lo, turn * PIECES + (p + 1 + RAW))
            for r2 in range(2):
                for c in range(2):
                    w = [a[:, p % RING, r2, c * 512:(c + 1) * 512] for a in (hi, lo)]
                    a = [o[:, k0 + r2, :] for o in ops]
                    nc.tensor.matmul(bank(b0 + c), a[0], w[0], start=False, stop=False)
                    nc.tensor.matmul(bank(b0 + c), a[0], w[1], start=False, stop=False)
                    last = nc.tensor.matmul(bank(b0 + c), a[1], w[0], start=False, stop=last_piece and r2 == 1)
            last.then_inc(s_used, 1)

        def body(r, e):
            turn = r * EXPERTS + e
            m = r * TURNS + (e + 1)
            pe.wait_ge(s_xl, m * 2 + 1)
            pe.wait_ge(s_pick, m)
            pe.wait_ge(s_act, turn * 2 + 1)
            for p in range(8):
                piece(turn, p, (xh, xl), 2 * (p // 4), 2 * (p % 4), p % 4 == 0, p % 4 == 3)
                if p == 1:
                    index_sum(m, e + 1, turn)
                if p == 5:
                    turn_a(turn, 0)
            turn_x(m, 0)
            pe.wait_ge(s_al, turn * 2 + 2)
            pe.wait_ge(s_idx, m + 1)
            piece(turn, 8, (ah, al), 4, 0, True, False)
            turn_a(turn, 1)
            turn_x(m, 1)
            piece(turn, 9, (ah, al), 4, 2, False, False)
            pe.wait_ge(s_al, turn * 2 + 3)
            piece(turn, 10, (ah, al), 4, 4, False, False)
            piece(turn, 11, (ah, al), 4, 6, False, True)

        def run(r):
            index_sum(r * TURNS, 0, r * EXPERTS)
            turn_x(r * TURNS, 0)
            turn_x(r * TURNS, 1)
            body(r, 0)
            with pe.Fori(1, EXPERTS) as e:
                body(r, e)

        rounds(pe, run)


def combine(nc, d, sb, sem, st, g, con, out):
    x, stat, y_dram = g["x"], g["stat"], g["y_dram"]
    y4 = sb(st, "y4", [P, NT, 4, D])
    sqr = sb(st, "sqr", [P, D])
    fw = sb(st, "final_w", [P, D])
    s_y = [sem(f"y_loaded{t}") for t in range(NT)]
    s_fw, s_add, s_ss, s_sd, s_rs, s_o, s_out = (sem(n) for n in ("final_w_loaded", "rows_added", "x3_squared", "x3_deviation",
                                                                  "x3_rstd", "out_ready", "out_stored"))
    block = st.enter_context(nc.Block())

    @block.sync
    def _(sp):
        for t in range(NT):
            sp.dma_start(y4[:, t], y_dram[t * 4 * P:(t + 1) * 4 * P, :].rearrange("(p j) n -> p j n", j=4)).then_inc(s_y[t], 16)
        for t in range(NT):
            sp.wait_ge(s_o, t + 1)
            sp.dma_start(out[0, t * P:(t + 1) * P, :], x[:, t, :]).then_inc(s_out, 16)
        sp.wait_ge(s_out, 16 * NT)

    @block.gpsimd
    def _(pool):
        nc.gpsimd.dma_start(fw[:], d["final_norm_w"].to_broadcast([P, D])).then_inc(s_fw, 16)

    @block.scalar
    def _(act):
        for t in range(NT):
            act.wait_ge(s_add, 4 * t + 4)
            nc.scalar.activation(sqr[:], x[:, t, :], ACT.Square, accum_out=stat[:, 40 + t:41 + t]).then_inc(s_ss, 1)
            act.wait_ge(s_ss, t + 1)
            nc.scalar.activation(stat[:, 44 + t:45 + t], stat[:, 40 + t:41 + t], ACT.Sqrt, bias=con("eps"), scale=1.0 / D).then_inc(s_sd, 1)

    @block.vector
    def _(dve):
        dve.wait_ge(s_fw, 16)

        def finish(t):
            dve.wait_ge(s_sd, t + 1)
            nc.vector.reciprocal(stat[:, 48 + t:49 + t], stat[:, 44 + t:45 + t]).then_inc(s_rs, 1)
            dve.wait_ge(s_rs, t + 1)
            nc.vector.scalar_tensor_tensor(x[:, t, :], x[:, t, :], stat[:, 48 + t:49 + t], fw[:], ALU.mult, ALU.mult).then_inc(s_o, 1)

        for t in range(NT):
            dve.wait_ge(s_y[t], 16)
            for j in range(4):
                if j:
                    dve.wait_ge(s_add, 4 * t + j)
                nc.vector.tensor_tensor(x[:, t, :], x[:, t, :], y4[:, t, j, :], ALU.add).then_inc(s_add, 1)
            if t:
                finish(t - 1)
        finish(NT - 1)


def kernel(x, positions, attn_norm_w, w_in, shift_mu, lambda_q1, lambda_k1, lambda_q2, lambda_k2, subln_w, rw_w0, rw_w2,
           rw_a0, rw_a2, rw_g2, rw_k_k, rw_k_a, rw_r_k, rw_lnx_w, rw_lnx_b, w_out, ffn_norm_w, router_w, router_b,
           mlp1_w, mlp1_b, mlp2_w, mlp2_b, final_norm_w):
    import concourse.bacc as bacc
    from concourse.bass_utils import run_bass_kernel_spmd as run

    def col(a):
        return np.asarray(a).reshape(-1, P).T

    mu = col(shift_mu)
    per_pair = [mu[:, 0:4], mu[:, 4:8], mu[:, 8:12]] + [col(a) for a in (rw_w0, rw_a0, rw_k_k, rw_k_a, rw_r_k, rw_lnx_w, rw_lnx_b)]
    pairs = np.stack(per_pair, 2).reshape(P, HEADS * NPAR)
    tables, _ = constant_tables()
    arrays = {
        "x": x, "positions": positions, "w_in": w_in, "w_out": w_out, "router_w": router_w, "router_b": router_b,
        "mlp1_w": mlp1_w, "mlp1_b": mlp1_b, "mlp2_w": mlp2_w, "mlp2_b": mlp2_b, "ffn_norm_w": ffn_norm_w,
        "final_norm_w": np.asarray(final_norm_w).reshape(1, D),
        "cols": np.concatenate([col(attn_norm_w), mu[:, 12:14], pairs, col(subln_w)], 1),
        "lam": np.concatenate([np.asarray(a) for a in (lambda_q1, lambda_k1, lambda_q2, lambda_k2)], 1),
        "w2a2": np.concatenate([np.asarray(rw_w2)[0], np.asarray(rw_a2)[0]], 0), "g2": np.asarray(rw_g2)[0],
        "cst": tables,
    }
    nc = bacc.Bacc("TRN2", target_bir_lowering=False, num_devices=1)
    feed, d = {}, {}
    for name, a in arrays.items():
        a = np.ascontiguousarray(a)
        feed[f"in_{name}"] = a
        d[name] = nc.dram_tensor(f"in_{name}", a.shape, mybir.dt.from_np(a.dtype), kind="ExternalInput").ap()
    out = nc.dram_tensor("out_0", (1, S, D), F32, kind="ExternalOutput").ap()
    build_program(nc, d, out)
    return run(nc, [feed], core_ids=[0]).results[0]["out_0"]
```

```python
from contextlib import ExitStack

import numpy as np

import concourse.bass as bass
from concourse import mybir

F32 = mybir.dt.float32
F32R = mybir.dt.float32r
I32 = mybir.dt.int32
U32 = mybir.dt.uint32
ALU = mybir.AluOpType
ACT = mybir.ActivationFunctionType
AX = mybir.AxisListType

P = 128
D = 1024
S = 512
NT = S // P
KT = D // P
IN_TILES = 26
HEADS = 4
CH = 64
NCH = S // CH
LEVELS = (2, 4, 8, 16, 32)
NORM_EPS = 1e-5
GN_EPS = 64e-5
LAM_INIT = 0.8 - 0.6 * 1.0
E_HALF = float(np.exp(-0.5))
EXPERTS = 32
TURNS = EXPERTS + 1
PIECES = 12
RAW = 6
RING = 4
ROUNDS = S // P
BIG = float(1 << 20)
NPAR = 10
NEG = -1e30


def constant_tables():
    p = np.arange(P)[:, None]
    c = np.arange(P)[None, :]
    same = p // CH == c // CH
    m1 = (same & (p < c)).astype(np.float32)
    m2 = (same & (p <= c)).astype(np.float32)
    level = [((p // (2 * b) == c // (2 * b)) & ((p // b) % 2 == 1) & ((c // b) % 2 == 0)) for b in LEVELS]
    t = np.arange(S)[None, :]
    inv = (np.float32(10000.0) ** (-np.arange(0, 64, 2, dtype=np.float32) / np.float32(64))).astype(np.float32)
    parts = {
        "ident": p == c,
        "mask_b": np.concatenate([m1, -m2], 1),
        "mask_k": np.concatenate([m1, m2], 1),
        "level1": (p // 2 == c // 2) & (p % 2 == 0) & (c % 2 == 1),
        "levels": np.concatenate(level, 1),
        "stack": p % CH == np.arange(CH)[None, :],
        "heads": same,
        "swap": p == (c ^ 32),
        "causal": np.where(np.arange(S)[None, :] - 3 * P > p, NEG, 0.0),
        "reset": np.broadcast_to(t % CH != 0, (P, S)),
        "before": p < c,
        "ones": np.ones((P, P)),
        "slot": np.broadcast_to(c, (P, P)),
        "token": np.arange(NT)[None, :] * P + p,
        "experts": np.broadcast_to(np.arange(EXPERTS)[None, :], (P, EXPERTS)),
        "pick": ((p % EXPERTS) == np.arange(TURNS)[None, :]) & (p < 2 * EXPERTS),
        "inv": inv[np.arange(P) % 32][:, None],
        "sign": np.where(np.arange(P)[:, None] % 64 < 32, -1.0, 1.0),
        "eps": np.full((P, 1), NORM_EPS),
        "gn_eps": np.full((P, 1), GN_EPS),
    }
    at, out, n = {}, [], 0
    for name, a in parts.items():
        a = np.asarray(a, np.float32)
        at[name] = (n, n + a.shape[1])
        n += a.shape[1]
        out.append(a)
    return np.ascontiguousarray(np.concatenate(out, 1)), at


class Steps:

    def __init__(self, sem, names):
        self.sem, self.names, self.next = sem, list(names), 0

    def step(self, name):
        assert self.names[self.next] == name, (self.names[self.next], name)
        self.next += 1
        return 1

    def reached(self, j, name):
        return j * len(self.names) + (len(self.names) + self.names.index(name) + 2)

    def before(self, j, name):
        return j * len(self.names) + (self.names.index(name) + 2)

    def ahead(self):
        return len(self.names) + 1


def build_program(nc, d, out):
    _, at = constant_tables()
    with ExitStack() as top:
        def sb(stack, name, shape, dt=F32):
            return stack.enter_context(nc.sbuf_tensor(name, shape, dt))

        def sem(name):
            return top.enter_context(nc.semaphore(name))

        psum = top.enter_context(nc.psum_tensor("psum", [P, 8, 512], F32))
        cst = sb(top, "cst", [P, d["cst"].shape[1]])
        cols = sb(top, "cols", [P, d["cols"].shape[1]])
        x = sb(top, "x", [P, NT, D])
        stat = sb(top, "stat", [P, 64])

        def con(name, a=0, b=None):
            lo, hi = at[name]
            return cst[:, lo + a:(lo + b if b is not None else hi)]

        ident = con("ident")

        def bank(n, a=0, b=512, rows=slice(0, P)):
            return psum[rows, n, a:b]

        h2_dram = nc.dram_tensor("h2_rows", (S, D), F32, kind="Internal").ap()
        y_dram = nc.dram_tensor("expert_rows", (4 * S, D), F32, kind="Internal").ap()
        rank = sb(top, "rank", [P, NT, TURNS])
        info = sb(top, "info", [P, NT, TURNS, 4])
        flags = sb(top, "flags", [P, ROUNDS], I32)

        o_t = sb(top, "o_t", [P, 2 * HEADS, S])
        with ExitStack() as st:
            pall = sb(st, "pall", [P, IN_TILES, S + 1])
            cosb = sb(st, "cosb", [P, S])
            sinb = sb(st, "sinb", [P, S])
            g = dict(cst=cst, cols=cols, x=x, stat=stat, pall=pall, cosb=cosb, sinb=sinb, o_t=o_t)
            project(nc, d, sb, sem, g, con, ident, psum, bank)
            mix(nc, d, sb, sem, st, g, con, ident, psum, bank)
        with ExitStack() as late:
            raw = sb(late, "w_pieces", [P, RAW, 2, D])
            bias = sb(late, "bias", [P, 3 * D], F32R)
            s_raw = [sem(f"piece_loaded{p}") for p in range(PIECES)]
            g = dict(x=x, stat=stat, o_t=o_t, rank=rank, info=info, flags=flags, h2_dram=h2_dram, y_dram=y_dram,
                     raw=raw, bias=bias, s_raw=s_raw)
            with ExitStack() as st:
                output_and_route(nc, d, sb, sem, st, g, con, ident, psum, bank)
            with ExitStack() as st:
                experts(nc, d, sb, sem, st, g, con, ident, psum, bank)
        with ExitStack() as st:
            combine(nc, d, sb, sem, st, dict(x=x, stat=stat, y_dram=y_dram), con, out)


def project(nc, d, sb, sem, g, con, ident, psum, bank):
    cst, cols, x, stat, pall, cosb, sinb = (g[k] for k in ("cst", "cols", "x", "stat", "pall", "cosb", "sinb"))
    s_cst, s_cols, s_lam, s_pos = sem("cst_loaded"), sem("cols_loaded"), sem("lam_loaded"), sem("pos_loaded")
    s_x = [sem(f"x_loaded{t}") for t in range(NT)]
    s_w = [sem(f"w_in_loaded{u}") for u in range(2)]
    s_sq, s_sd, s_rstd, s_xn = sem("x_squared"), sem("x_deviation"), sem("x_rstd"), sem("x_normed")
    s_xt, s_hh, s_hl = sem("x_turned"), sem("h_hi"), sem("h_lo")
    s_whi, s_wlo, s_prod, s_out = sem("w_hi"), sem("w_lo"), sem("projected"), sem("p_copied")
    s_zero, s_rope, s_lam1, s_ang = sem("p_zeroed"), sem("rope_steps"), sem("lam_steps"), sem("angles_done")
    s_trig, s_lex = sem("trig_done"), sem("lam_exp")
    with ExitStack() as st:
        xn = sb(st, "xn", [P, NT, D])
        h_hi = sb(st, "h_hi_sb", [P, KT, S], F32R)
        h_lo = sb(st, "h_lo_sb", [P, KT, S], F32R)
        w_raw = sb(st, "w_raw", [P, 2, KT, P])
        w_hi = sb(st, "w_hi_sb", [P, 2, KT, P], F32R)
        w_lo = sb(st, "w_lo_sb", [P, 2, KT, P], F32R)
        posi = sb(st, "posi", [P, S], I32)
        ang = sb(st, "ang", [P, S])
        turns = sb(st, "turns", [P, S])
        taken = sb(st, "taken", [P, S])
        lam = sb(st, "lam", [P, 4, 64])
        lamp = sb(st, "lamp", [P, 64])
        w_v = d["w_in"][0].rearrange("(k p) n -> p k n", p=P)
        x_v = d["x"][0].rearrange("(t p) c -> p t c", p=P)
        block = st.enter_context(nc.Block())

        @block.sync
        def _(sp):
            for t in range(NT):
                sp.dma_start(x[:, t, :], x_v[:, t, :]).then_inc(s_x[t], 16)
            sp.dma_start(cst[:], d["cst"]).then_inc(s_cst, 16)
            with sp.Fori(0, IN_TILES // 2) as i:
                for u in range(2):
                    sp.wait_ge(s_wlo, i * 2 + (u + 1))
                    sp.dma_start(w_raw[:, u], w_v[:, :, bass.ds(i * 256 + u * P, P)]).then_inc(s_w[u], 16)

        @block.gpsimd
        def _(pool):
            nc.gpsimd.dma_start(cols[:], d["cols"]).then_inc(s_cols, 16)
            nc.gpsimd.dma_start(posi[:], d["positions"].to_broadcast([P, S])).then_inc(s_pos, 16)
            nc.gpsimd.dma_start(lam[:].rearrange("p a b -> p (a b)"), d["lam"].to_broadcast([P, 256])).then_inc(s_lam, 16)
            nc.gpsimd.memset(pall[:, :, 0:1], 0.0).then_inc(s_zero, 1)
            pool.wait_ge(s_zero, 1)
            pool.wait_ge(s_cst, 16)
            pool.wait_ge(s_pos, 16)
            step = 0

            def chain(ins):
                nonlocal step
                step += 1
                ins.then_inc(s_rope, 1)
                pool.wait_ge(s_rope, step)

            two_pi = 2 * np.pi
            c1 = 6.28125
            c2 = float(np.float32(two_pi - c1) - np.float32(two_pi - c1) % np.float32(2.0 ** -20))
            c3 = float(two_pi - c1 - c2)
            chain(nc.gpsimd.tensor_copy(cosb[:], posi[:]))
            chain(nc.gpsimd.tensor_scalar(sinb[:], cosb[:], con("inv"), None, ALU.mult))
            for dst, shift in ((ang, 0.25), (turns, 0.0)):
                chain(nc.gpsimd.tensor_scalar(cosb[:], sinb[:], float(1 / two_pi), shift, ALU.mult, ALU.add))
                chain(nc.gpsimd.tensor_scalar(cosb[:], cosb[:], 12582912.0, None, ALU.add))
                chain(nc.gpsimd.tensor_scalar(cosb[:], cosb[:], 12582912.0, None, ALU.subtract))
                for c, angle in ((c1, sinb), (c2, dst), (c3, dst)):
                    chain(nc.gpsimd.tensor_scalar(taken[:], cosb[:], -c, None, ALU.mult))
                    chain(nc.gpsimd.tensor_tensor(dst[:], taken[:], angle[:], ALU.add))
                if shift:
                    chain(nc.gpsimd.tensor_scalar(dst[:], dst[:], float(np.pi / 2), None, ALU.add))
                chain(nc.gpsimd.tensor_scalar(dst[:], dst[:], 3.1415925, -3.1415925, ALU.min, ALU.max))
                pool.sem_inc(s_ang, 1)

        @block.scalar
        def _(act):
            for t in range(NT):
                act.wait_ge(s_x[t], 16)
                last = nc.scalar.activation(xn[:, t, :], x[:, t, :], ACT.Square, accum_out=stat[:, t:t + 1])
            last.then_inc(s_sq, 1)
            act.wait_ge(s_sq, 1)
            act.wait_ge(s_wlo, 2)
            nc.scalar.activation(stat[:, 4:8], stat[:, 0:4], ACT.Sqrt, bias=stat[:, 63:64], scale=1.0 / D).then_inc(s_sd, 1)
            act.wait_ge(s_cols, 16)

            def split(i, u):
                act.wait_ge(s_w[u], i * 16 + 16)
                act.wait_ge(s_prod, i * 2 + (u + 1))
                nc.scalar.activation(w_hi[:, u], w_raw[:, u], ACT.Copy).then_inc(s_whi, 1)

            def copy_out(n, u):
                act.wait_ge(s_prod, n + 3)
                nc.scalar.activation(pall[:, bass.ds(n, 1), 1:S + 1].rearrange("p a s -> p (a s)"), bank(u), ACT.Copy).then_inc(s_out, 1)

            split(0, 0)
            split(0, 1)
            for k in range(KT):
                act.wait_ge(s_xt, k + 1)
                nc.scalar.activation(h_hi[:, k, :], bank(k), ACT.Copy, scale=cols[:, k:k + 1]).then_inc(s_hh, 1)
            with act.Fori(1, IN_TILES // 2 - 1) as i:
                for u in range(2):
                    split(i, u)
                    copy_out(i * 2 + (u - 2), u)
            act.wait_ge(s_ang, 2)
            nc.scalar.activation(cosb[:], ang[:], ACT.Sin)
            nc.scalar.activation(sinb[:], turns[:], ACT.Sin).then_inc(s_trig, 1)
            act.wait_ge(s_lam1, 2)
            nc.scalar.activation(stat[:, 18:20], stat[:, 16:18], ACT.Exp).then_inc(s_lex, 1)
            for u in range(2):
                split(IN_TILES // 2 - 1, u)
                copy_out(IN_TILES - 4 + u, u)
            for u in range(2):
                copy_out(IN_TILES - 2 + u, u)

        @block.vector
        def _(dve):
            nc.vector.memset(stat[:, 63:64], NORM_EPS).then_inc(s_wlo, 2)
            dve.wait_ge(s_sd, 1)
            nc.vector.reciprocal(stat[:, 8:12], stat[:, 4:8]).then_inc(s_rstd, 1)
            dve.wait_ge(s_rstd, 1)
            for t in range(NT):
                nc.vector.tensor_scalar(xn[:, t, :], x[:, t, :], stat[:, 8 + t:9 + t], None, ALU.mult).then_inc(s_xn, 1)

            def split(i, u):
                dve.wait_ge(s_whi, i * 2 + (u + 1))
                nc.vector.tensor_tensor(w_lo[:, u], w_raw[:, u], w_hi[:, u].bitcast(F32), ALU.subtract).then_inc(s_wlo, 1)

            split(0, 0)
            split(0, 1)
            for k in range(KT):
                dve.wait_ge(s_hh, k + 1)
                nc.vector.scalar_tensor_tensor(h_lo[:, k, :], bank(k), cols[:, k:k + 1], h_hi[:, k, :].bitcast(F32),
                                               ALU.mult, ALU.subtract).then_inc(s_hl, 1)
            dve.wait_ge(s_lam, 16)
            for n in range(2):
                if n:
                    dve.wait_ge(s_lam1, n)
                nc.vector.tensor_tensor_reduce(lamp[:], lam[:, 2 * n, :], lam[:, 2 * n + 1, :], 1.0, 0.0, ALU.mult, ALU.add,
                                               stat[:, 16 + n:17 + n]).then_inc(s_lam1, 1)
            with dve.Fori(1, IN_TILES // 2) as i:
                for u in range(2):
                    split(i, u)
            dve.wait_ge(s_lex, 1)
            nc.vector.tensor_tensor(stat[:, 20:21], stat[:, 19:20], stat[:, 18:19], ALU.subtract).then_inc(s_lam1, 1)
            dve.wait_ge(s_lam1, 3)
            nc.vector.tensor_scalar(stat[:, 21:22], stat[:, 20:21], -LAM_INIT, None, ALU.add)
            dve.wait_ge(s_trig, 1)
            nc.vector.tensor_scalar(sinb[:], sinb[:], con("sign"), None, ALU.mult).then_inc(s_lam1, 1)
            dve.wait_ge(s_lam1, 4)

        @block.tensor
        def _(pe):
            pe.wait_ge(s_cst, 16)
            pe.wait_ge(s_xn, NT)
            for k in range(KT):
                for t in range(NT):
                    last = nc.tensor.transpose(bank(k, t * P, t * P + P), xn[:, t, k * P:(k + 1) * P], ident)
                if k == 0:
                    pe.sem_inc(s_prod, 2)
                last.then_inc(s_xt, 1)

            def tile(n, i, u, first=False):
                pe.wait_ge(s_wlo, n + 3)
                for k in range(KT):
                    if first:
                        pe.wait_ge(s_hl, k + 1)
                    pairs = ((w_hi, h_hi), (w_hi, h_lo), (w_lo, h_hi))
                    for m, (w, h) in enumerate(pairs):
                        last = nc.tensor.matmul(bank(u), w[:, u, k, :], h[:, k, :], start=k == 0 and m == 0,
                                                stop=k == KT - 1 and m == 2)
                last.then_inc(s_prod, 1)

            pe.wait_ge(s_hl, 2)
            for u in range(2):
                tile(u, 0, u, u == 0)
            with pe.Fori(1, IN_TILES // 2) as i:
                for u in range(2):
                    pe.wait_ge(s_out, i * 2 + (u - 1))
                    tile(i * 2 + u, i, u)


MIX_PE = (["lora_w", "lora_a", "kk_sum", "lora_g", "v_turn", "rope_swap", "mb0", "mk0", "t_kappa", "mb1", "x_turn0", "mk1",
           "t_beta", "x_turn1", "bonus", "t_khat"]
          + [n for lv in range(5) for n in [f"t{lv}_0", f"t{lv}_1"] + ([f"x{lv}_0", f"a_turn{lv - 1}", f"x{lv}_1", f"o{lv - 1}"] if lv
             else ["t_v", f"x{lv}_0", f"x{lv}_1"]) + [f"score{lv}"] * (lv < NT)]
          + ["akv", "o_turn", "wu0", "wu1", "q", "chunk"] + [f"z{c}" for c in range(1, 7)] + ["y", "y_turn"])
MIX_ACT = (["sig_w", "v_copy", "kk_sq", "sig_a", "kk_norm", "gate", "exps", "v_major", "e_kappa", "x_major0", "e_beta",
            "x_major1", "e_khat", "e_v"]
           + [f"{a}{i}" for i in range(NT) for a in ("exp", "a_major", "o_copy")]
           + ["o_sd", "e_akv", "e_wu0", "e_wu1", "y_sd"])
MIX_DVE = (["shift_k", "mix_k", "kk0", "shift_r", "shift_v", "mix_", "lsum", "lprev", "qc", "kc", "kk_max", "kk_inv", "kk",
            "kappa", "b", "beta", "am", "kmod", "qs", "ks", "rhat", "khat", "rk", "q", "k"]
           + [f"{a}{h}" for h in range(2) for a in ("emb", "x1a", "x1b", "emk")] + ["bon"]
           + [n for lv in range(5) for n in [f"et{lv}_0", f"et{lv}_1"] + [f"{a}{lv - 1}" for a in ("rl", "nl", "p2", "a")] * (lv > 0)
              + [f"ex{lv}_0", f"ex{lv}_1"] + [f"masked{lv}", f"max{lv}"] * (lv < NT)]
           + ["o_rs", "o_n", "o_out", "eg", "eh", "e_q"] + [f"z{c}" for c in range(1, 8)]
           + ["y_sum", "y_mean", "y_c", "y_sq", "y_var", "y_rs", "y_n", "ot1", "ot2", "ot3"])


def mix(nc, d, sb, sem, st, g, con, ident, psum, bank):
    cols, stat, pall, cosb, sinb, o_t = (g[k] for k in ("cols", "stat", "pall", "cosb", "sinb", "o_t"))
    PE = Steps(sem("mix_tensor_steps"), MIX_PE)
    AC = Steps(sem("mix_scalar_steps"), MIX_ACT)
    DV = Steps(sem("mix_vector_steps"), MIX_DVE)
    s_lora, s_set, s_set2, s_gp = sem("lora_loaded"), sem("mix_set"), sem("mix_set2"), sem("mix_zeroed")
    s_par = sem("pair_params_loaded")
    wa = sb(st, "wa", [P, S])
    sg = sb(st, "sg", [P, S])
    par = sb(st, "par", [P, NPAR])
    lj = sb(st, "lj", [P, 2, P])
    rkv = sb(st, "rkv", [P, 3, S])
    w3 = sb(st, "w3", [P, 3, S])
    r_, k_, v_ = rkv[:, 0, :], rkv[:, 1, :], rkv[:, 2, :]
    lsum, lprev, kk = w3[:, 0, :], w3[:, 1, :], w3[:, 2, :]
    sg_w = sb(st, "sg_w", [P, S])
    gate = sb(st, "gate", [P, S])
    aa = sb(st, "aa", [P, S])
    pe_ = sb(st, "p_end", [P, S])
    pi_ = sb(st, "p_inv", [P, S])
    pp_ = sb(st, "p_prev", [P, S])
    sq = sb(st, "sq", [P, S])
    beta = sb(st, "beta", [P, S])
    khat = sb(st, "khat", [P, S])
    kr = sb(st, "kr", [P, NT, 2, P])
    ab = sb(st, "ab", [P, 2, NT, 2, P])
    ak = sb(st, "ak", [P, 2, NT, 2, P])
    xx = sb(st, "xx", [P, 2, NT, 2, P])
    t1 = sb(st, "t1", [P, 2, NT, P])
    bn = sb(st, "bn", [P, NT, P])
    kh = sb(st, "kh", [P, NT, P])
    vt = sb(st, "vt", [P, NT, P])
    rh = sb(st, "rh", [P, 2, NT, P])
    wu = sb(st, "wu", [P, 2, NT, P])
    gt = sb(st, "gt", [P, NCH, P])
    zz = sb(st, "zz", [P, NCH, CH])
    hp = t1[:, 0].rearrange("p t c -> p (t c)").rearrange("p (n k) -> p n k", k=CH)
    qt = t1[:, 1]
    yc, ysq, yn = pe_, pi_, pp_
    vf = sb(st, "vf", [P, S])
    vm = sb(st, "vm", [P, NT, P])
    qr = sb(st, "qr", [P, S])
    kro = sb(st, "kro", [P, S])
    sc = sb(st, "sc", [P, 2, S])
    am, at_ = beta, khat
    on = vf
    ast = sb(st, "ast", [P, 48])
    pg = pall[:, 0:24, :].rearrange("p (g j) t -> p g j t", j=HEADS)

    def tile_of(group, j, shift=1):
        return pg[:, group, bass.ds(j, 1), shift:shift + S].rearrange("p a s -> p (a s)")

    block = st.enter_context(nc.Block())

    @block.sync
    def _(sp):
        base = KT + 2
        with sp.Fori(0, HEADS) as j:
            sp.wait_ge(PE.sem, PE.before(j, "lora_g"))
            sp.dma_start(lj[:, 0, :], d["w2a2"][:, bass.ds(j * P, P)]).then_inc(s_lora, 16)
            sp.dma_start(lj[:, 1, :], d["g2"][:, bass.ds(j * P, P)]).then_inc(s_lora, 16)
            sp.wait_ge(DV.sem, DV.before(j, "ot1"))
            sp.dma_start(par[:], d["cols"][:, bass.ds(j * NPAR + base, NPAR)]).then_inc(s_par, 16)

    @block.gpsimd
    def _(pool):
        nc.gpsimd.memset(gt[:], 0.0)
        nc.gpsimd.memset(zz[:, 0, :], 0.0).then_inc(s_gp, 1)
        pool.wait_ge(s_gp, 1)

    @block.scalar
    def _(act):
        act.wait_ge(s_set, 2)
        act.sem_inc(AC.sem, AC.ahead() - 1)
        nc.scalar.activation(wa[0:64], sq[0:64], ACT.Tanh)
        nc.scalar.activation(wa[64:128], sq[64:128], ACT.Copy)
        nc.scalar.activation(sg[:], aa[:], ACT.Sigmoid).then_inc(AC.sem, 1)
        with act.Fori(0, HEADS) as j:
            act.wait_ge(s_par, j * 16 + 16)
            act.wait_ge(PE.sem, PE.reached(j, "lora_w"))
            nc.scalar.activation(sg_w[:], bank(4), ACT.Sigmoid, bias=par[:, 3:4]).then_inc(AC.sem, AC.step("sig_w"))
            nc.scalar.activation(vf[:], tile_of(2, j), ACT.Copy).then_inc(AC.sem, AC.step("v_copy"))
            act.wait_ge(DV.sem, DV.reached(j, "kk0"))
            nc.scalar.activation(sq[:], kk, ACT.Square).then_inc(AC.sem, AC.step("kk_sq"))
            act.wait_ge(PE.sem, PE.reached(j, "lora_a"))
            nc.scalar.activation(aa[:], bank(5), ACT.Sigmoid, bias=par[:, 4:5]).then_inc(AC.sem, AC.step("sig_a"))
            act.wait_ge(PE.sem, PE.reached(j, "kk_sum"))
            nc.scalar.activation(sq[:], bank(7), ACT.Sqrt).then_inc(AC.sem, AC.step("kk_norm"))
            act.wait_ge(PE.sem, PE.reached(j, "lora_g"))
            nc.scalar.activation(gate[:], bank(6), ACT.Copy).then_inc(AC.sem, AC.step("gate"))
            act.wait_ge(DV.sem, DV.reached(j, "lprev"))
            nc.scalar.activation(pe_[:], lsum, ACT.Exp, scale=-E_HALF)
            nc.scalar.activation(pi_[:], lsum, ACT.Exp, scale=E_HALF)
            nc.scalar.activation(pp_[:], lprev, ACT.Exp, scale=-E_HALF).then_inc(AC.sem, AC.step("exps"))
            act.wait_ge(PE.sem, PE.reached(j, "v_turn"))
            nc.scalar.activation(vm[:].rearrange("p a b -> p (a b)"), bank(2), ACT.Copy).then_inc(AC.sem, AC.step("v_major"))

            def x_major(h):
                act.wait_ge(PE.sem, PE.reached(j, f"x_turn{h}"))
                nc.scalar.activation(xx[:, h, :, 0, :], bank(4 + h).rearrange("p (t c) -> p t c", c=P), ACT.Copy).then_inc(
                    AC.sem, AC.step(f"x_major{h}"))

            act.wait_ge(PE.sem, PE.reached(j, "t_kappa"))
            for h in range(2):
                last = nc.scalar.activation(rh[:, h, :, 0:64], bank(6).rearrange("p (t h c) -> p t h c", h=2, c=64)[:, :, h, :], ACT.Copy)
            last.then_inc(AC.sem, AC.step("e_kappa"))
            x_major(0)
            act.wait_ge(PE.sem, PE.reached(j, "t_beta"))
            nc.scalar.activation(bn[:].rearrange("p a b -> p (a b)"), bank(7), ACT.Copy, scale=-1.0).then_inc(AC.sem, AC.step("e_beta"))
            x_major(1)
            act.wait_ge(PE.sem, PE.reached(j, "t_khat"))
            nc.scalar.activation(kh[:].rearrange("p a b -> p (a b)"), bank(6), ACT.Copy).then_inc(AC.sem, AC.step("e_khat"))
            act.wait_ge(PE.sem, PE.reached(j, "t_v"))
            nc.scalar.activation(vt[:].rearrange("p a b -> p (a b)"), bank(6), ACT.Copy).then_inc(AC.sem, AC.step("e_v"))
            for i in range(NT):
                n = (i + 1) * P
                act.wait_ge(DV.sem, DV.reached(j, f"max{i}"))
                for c in range(2):
                    last = nc.scalar.activation(sc[:, c, 0:n], sc[:, c, 0:n], ACT.Exp, bias=ast[:, 2 * i + c:2 * i + c + 1],
                                                accum_out=ast[:, 8 + 2 * i + c:9 + 2 * i + c])
                last.then_inc(AC.sem, AC.step(f"exp{i}"))
                act.wait_ge(PE.sem, PE.reached(j, f"a_turn{i}"))
                nc.scalar.activation(at_[:, 0:n], bank(6, 0, n), ACT.Copy).then_inc(AC.sem, AC.step(f"a_major{i}"))
                act.wait_ge(PE.sem, PE.reached(j, f"o{i}"))
                nc.scalar.activation(on[:, i * P:(i + 1) * P], bank(7, 0, P), ACT.Copy)
                nc.scalar.activation(sc[:, 0, 0:P], bank(7, 0, P), ACT.Square,
                                     accum_out=ast[:, 24 + i:25 + i]).then_inc(AC.sem, AC.step(f"o_copy{i}"))
            act.wait_ge(AC.sem, AC.reached(j, f"o_copy{NT - 1}"))
            nc.scalar.activation(ast[:, 28:32], ast[:, 24:28], ACT.Sqrt, bias=con("eps"), scale=1.0 / P).then_inc(AC.sem, AC.step("o_sd"))
            act.wait_ge(PE.sem, PE.reached(j, "akv"))
            nc.scalar.activation(rh[:, :, :, 64:128].rearrange("p h t c -> p (h t) c"),
                                 bank(4).rearrange("p (u c) -> p u c", c=64), ACT.Copy).then_inc(AC.sem, AC.step("e_akv"))
            for h in range(2):
                act.wait_ge(PE.sem, PE.reached(j, f"wu{h}"))
                nc.scalar.activation(wu[:, h].rearrange("p t c -> p (t c)"), bank(5 * (1 - h)), ACT.Copy).then_inc(AC.sem, AC.step(f"e_wu{h}"))
            act.wait_ge(DV.sem, DV.reached(j, "y_var"))
            nc.scalar.activation(ast[:, 40:48], ast[:, 32:40], ACT.Sqrt, bias=con("gn_eps"), scale=1.0 / CH).then_inc(AC.sem, AC.step("y_sd"))

    @block.vector
    def _(dve):
        for n, dst in ((0, sq), (1, aa)):
            t = 24 + n
            nc.vector.tensor_tensor(w3[:, n, :], pall[:, t, 0:S], pall[:, t, 1:S + 1], ALU.subtract).then_inc(s_set2, 1)
            dve.wait_ge(s_set2, n + 1)
            nc.vector.scalar_tensor_tensor(dst[:], w3[:, n, :], cols[:, KT + n:KT + n + 1], pall[:, t, 1:S + 1],
                                           ALU.mult, ALU.add).then_inc(s_set, 1)
        dve.wait_ge(s_set, 2)
        dve.sem_inc(DV.sem, DV.ahead() - 1)
        nc.vector.memset(ast[:, 0:1], 0.0).then_inc(DV.sem, 1)
        with dve.Fori(0, HEADS) as j:
            dve.wait_ge(DV.sem, DV.before(j, "ot3"))

            def own(name):
                dve.wait_ge(DV.sem, DV.reached(j, name))

            def masked(i):
                n = (i + 1) * P
                dve.wait_ge(PE.sem, PE.reached(j, f"score{i}"))
                mask = con("causal", (NT - 1 - i) * P, S)
                nc.vector.scalar_tensor_tensor(sc[:, :, 0:n], psum[:, 6:8, 0:n], 0.125,
                                               mask.rearrange("p (a n) -> p a n", a=1).to_broadcast([P, 2, n]),
                                               ALU.mult, ALU.add).then_inc(DV.sem, DV.step(f"masked{i}"))
                own(f"masked{i}")
                nc.vector.tensor_reduce(ast[:, 2 * i:2 * i + 2], sc[:, :, 0:n], AX.X, ALU.max, negate=True).then_inc(
                    DV.sem, DV.step(f"max{i}"))

            def weights(i):
                n = (i + 1) * P
                dve.wait_ge(AC.sem, AC.reached(j, f"exp{i}"))
                nc.vector.reciprocal(ast[:, 16:18], ast[:, 8 + 2 * i:10 + 2 * i]).then_inc(DV.sem, DV.step(f"rl{i}"))
                own(f"rl{i}")
                nc.vector.tensor_tensor(ast[:, 18:19], ast[:, 17:18], stat[:, 21:22], ALU.mult).then_inc(DV.sem, DV.step(f"nl{i}"))
                own(f"nl{i}")
                nc.vector.tensor_scalar(sc[:, 1, 0:n], sc[:, 1, 0:n], ast[:, 18:19], None, ALU.mult).then_inc(DV.sem, DV.step(f"p2{i}"))
                own(f"p2{i}")
                dve.wait_ge(PE.sem, PE.reached(j, f"a_turn{i - 1}" if i else "t_khat"))
                nc.vector.scalar_tensor_tensor(am[:, 0:n], sc[:, 0, 0:n], ast[:, 16:17], sc[:, 1, 0:n], ALU.mult,
                                               ALU.add).then_inc(DV.sem, DV.step(f"a{i}"))

            def shift(n, name, dst):
                nc.vector.tensor_tensor(dst, tile_of(3 + n, j, 0), tile_of(3 + n, j), ALU.subtract).then_inc(DV.sem, DV.step(name))

            def mix_in(n, diff):
                return nc.vector.scalar_tensor_tensor(rkv[:, n, :], diff, par[:, n:n + 1], tile_of(3 + n, j), ALU.mult, ALU.add)

            shift(1, "shift_k", w3[:, 1, :])
            own("shift_k")
            dve.wait_ge(s_par, j * 16 + 16)
            mix_in(1, w3[:, 1, :]).then_inc(DV.sem, DV.step("mix_k"))
            own("mix_k")
            nc.vector.tensor_scalar(kk, k_, par[:, 5:6], None, ALU.mult).then_inc(DV.sem, DV.step("kk0"))
            shift(0, "shift_r", w3[:, 0, :])
            shift(2, "shift_v", beta[:])
            own("shift_v")
            mix_in(0, w3[:, 0, :])
            mix_in(2, beta[:]).then_inc(DV.sem, DV.step("mix_"))
            own("mix_")
            dve.wait_ge(AC.sem, AC.reached(j, "sig_w"))
            nc.vector.tensor_tensor_scan(lsum, con("reset"), sg_w[:], 0.0, ALU.mult, ALU.add).then_inc(DV.sem, DV.step("lsum"))
            own("lsum")
            nc.vector.tensor_tensor(lprev, lsum, sg_w[:], ALU.subtract).then_inc(DV.sem, DV.step("lprev"))
            rope = (("q", 0, qr), ("k", 1, kro))
            for a, group, dst in rope:
                nc.vector.tensor_tensor(dst[:], tile_of(group, j), cosb[:], ALU.mult).then_inc(DV.sem, DV.step(a + "c"))
            dve.wait_ge(AC.sem, AC.reached(j, "kk_norm"))
            nc.vector.tensor_scalar(sq[:], sq[:], 1e-12, None, ALU.max).then_inc(DV.sem, DV.step("kk_max"))
            own("kk_max")
            nc.vector.reciprocal(sq[:], sq[:]).then_inc(DV.sem, DV.step("kk_inv"))
            own("kk_inv")
            nc.vector.tensor_tensor(kk, kk, sq[:], ALU.mult).then_inc(DV.sem, DV.step("kk"))
            own("kk")

            def tiles(a):
                return a.rearrange("p (t c) -> p t c", c=P)

            dve.wait_ge(AC.sem, AC.reached(j, "exps"))
            nc.vector.tensor_tensor(kr[:, :, 0, :], tiles(kk), tiles(pp_[:]), ALU.mult).then_inc(DV.sem, DV.step("kappa"))
            nc.vector.tensor_tensor(sq[:], kk, aa[:], ALU.mult).then_inc(DV.sem, DV.step("b"))
            own("b")
            nc.vector.tensor_tensor(beta[:], sq[:], pi_[:], ALU.mult).then_inc(DV.sem, DV.step("beta"))
            nc.vector.tensor_scalar(aa[:], aa[:], 1.0, par[:, 6:7], ALU.subtract, ALU.mult).then_inc(DV.sem, DV.step("am"))
            own("am")
            nc.vector.scalar_tensor_tensor(k_, aa[:], 1.0, k_, ALU.add, ALU.mult).then_inc(DV.sem, DV.step("kmod"))
            dve.wait_ge(PE.sem, PE.reached(j, "rope_swap"))
            for a, group, dst in rope:
                nc.vector.tensor_tensor(sc[:, group, :], bank(group), sinb[:], ALU.mult).then_inc(DV.sem, DV.step(a + "s"))
            nc.vector.tensor_tensor(kr[:, :, 1, :], tiles(r_), tiles(pe_[:]), ALU.mult).then_inc(DV.sem, DV.step("rhat"))
            own("kmod")
            nc.vector.tensor_tensor(khat[:], k_, pi_[:], ALU.mult).then_inc(DV.sem, DV.step("khat"))
            nc.vector.scalar_tensor_tensor(r_, r_, par[:, 7:8], k_, ALU.mult, ALU.mult).then_inc(DV.sem, DV.step("rk"))
            own("ks")
            for a, group, dst in rope:
                nc.vector.tensor_tensor(dst[:], dst[:], sc[:, group, :], ALU.add).then_inc(DV.sem, DV.step(a))
            for h in range(2):
                def mask_products(a, b0, dst, msk):
                    dve.wait_ge(PE.sem, PE.reached(j, f"m{a}{h}"))
                    nc.vector.tensor_tensor(dst[:, h].rearrange("p t a c -> p t (a c)"),
                                            psum[:, b0:b0 + 2, :].rearrange("p b (t c) -> p (b t) c", c=2 * P),
                                            con(msk).rearrange("p (a n) -> p a n", a=1).to_broadcast([P, NT, 2 * P]),
                                            ALU.mult).then_inc(DV.sem, DV.step(f"em{a}{h}"))

                mask_products("b", 0, ab, "mask_b")
                own(f"emb{h}")
                nc.vector.tensor_tensor(t1[:, h], ab[:, h, :, 0, :],
                                        con("level1").rearrange("p (a n) -> p a n", a=1).to_broadcast([P, NT, P]),
                                        ALU.mult).then_inc(DV.sem, DV.step(f"x1a{h}"))
                own(f"x1a{h}")
                nc.vector.tensor_tensor(xx[:, h, :, 1, :], ident.rearrange("p (a n) -> p a n", a=1).to_broadcast([P, NT, P]),
                                        t1[:, h], ALU.subtract).then_inc(DV.sem, DV.step(f"x1b{h}"))
                mask_products("k", 2, ak, "mask_k")
            dve.wait_ge(PE.sem, PE.reached(j, "bonus"))
            nc.vector.tensor_tensor(r_, bank(7), v_, ALU.mult).then_inc(DV.sem, DV.step("bon"))
            for lv in range(5):
                for h in range(2):
                    dve.wait_ge(PE.sem, PE.reached(j, f"t{lv}_{h}"))
                    nc.vector.tensor_tensor(t1[:, h], bank(4 + h).rearrange("p (t c) -> p t c", c=P),
                                            con("levels", lv * P, lv * P + P).rearrange("p (a n) -> p a n", a=1).to_broadcast([P, NT, P]),
                                            ALU.mult).then_inc(DV.sem, DV.step(f"et{lv}_{h}"))
                if lv:
                    weights(lv - 1)
                for h in range(2):
                    dve.wait_ge(PE.sem, PE.reached(j, f"x{lv}_{h}"))
                    src = psum[:, 2 * h:2 * h + 2, :].rearrange("p b (t a c) -> p (b t) a c", a=2, c=P)
                    if lv < 4:
                        nc.vector.tensor_tensor(xx[:, h], xx[:, h], src, ALU.subtract).then_inc(DV.sem, DV.step(f"ex{lv}_{h}"))
                    else:
                        nc.vector.tensor_tensor(xx[:, h, :, 1, :], xx[:, h, :, 1, :], src[:, :, 1, :], ALU.subtract).then_inc(
                            DV.sem, DV.step(f"ex{lv}_{h}"))
                if lv < NT:
                    masked(lv)
            dve.wait_ge(AC.sem, AC.reached(j, "o_sd"))
            nc.vector.reciprocal(ast[:, 20:24], ast[:, 28:32]).then_inc(DV.sem, DV.step("o_rs"))
            own("o_rs")
            for i in range(NT):
                last = nc.vector.tensor_scalar(on[:, i * P:(i + 1) * P], on[:, i * P:(i + 1) * P], ast[:, 20 + i:21 + i],
                                               1.0 - LAM_INIT, ALU.mult, ALU.mult)
            last.then_inc(DV.sem, DV.step("o_n"))
            dve.wait_ge(PE.sem, PE.reached(j, "o_turn"))
            nc.vector.tensor_scalar(o_t[:, bass.ds(j, 1), :].rearrange("p a s -> p (a s)"), bank(6),
                                    cols[:, KT + 2 + HEADS * NPAR:KT + 3 + HEADS * NPAR], None, ALU.mult).then_inc(DV.sem, DV.step("o_out"))
            dve.wait_ge(s_gp, 1)
            dve.wait_ge(PE.sem, PE.reached(j, "chunk"))
            for h in range(2):
                rows = slice(64 * h, 64 * h + 64)
                last = nc.vector.tensor_tensor(
                    gt[rows, :, 64 * h:64 * h + 64].rearrange("p (t c) k -> p c t k", c=2),
                    psum[rows, 0:2, 0:256].rearrange("p c (t k) -> p c t k", k=64),
                    con("stack")[rows].rearrange("p (a b k) -> p a b k", a=1, b=1).to_broadcast([64, 2, NT, 64]), ALU.add)
            last.then_inc(DV.sem, DV.step("eg"))
            decay_end = pe_[:].rearrange("p (t c k) -> p c t k", c=2, k=64)[:, :, :, 63:64]
            nc.vector.tensor_tensor(hp[:].rearrange("p (t c) k -> p c t k", c=2),
                                    psum[:, 0:2, 256:512].rearrange("p c (t k) -> p c t k", k=64),
                                    decay_end.to_broadcast([P, 2, NT, 64]), ALU.mult).then_inc(DV.sem, DV.step("eh"))
            dve.wait_ge(PE.sem, PE.reached(j, "q"))
            nc.vector.tensor_tensor(qt[:], bank(3).rearrange("p (t c) -> p t c", c=P), kr[:, :, 1, :], ALU.add).then_inc(
                DV.sem, DV.step("e_q"))
            own("eh")
            nc.vector.tensor_copy(zz[:, 1, :], hp[:, 0, :]).then_inc(DV.sem, DV.step("z1"))
            for c in range(1, 7):
                dve.wait_ge(PE.sem, PE.reached(j, f"z{c}"))
                nc.vector.scalar_tensor_tensor(zz[:, c + 1, :], bank(2, c * 64, c * 64 + 64), pe_[:, 64 * c + 63:64 * c + 64],
                                               hp[:, c, :], ALU.mult, ALU.add).then_inc(DV.sem, DV.step(f"z{c + 1}"))
            own("z7")
            dve.wait_ge(PE.sem, PE.reached(j, "y"))
            yb = psum[:, 4:6, 0:256].rearrange("p h (t v) -> p h t v", v=64)
            y4 = yc[:].rearrange("p (h t v) -> p h t v", h=2, v=64)
            nc.vector.tensor_reduce(ast[:, 32:40], yb, AX.X, ALU.add).then_inc(DV.sem, DV.step("y_sum"))
            own("y_sum")
            nc.vector.tensor_scalar(ast[:, 40:48], ast[:, 32:40], -1.0 / CH, None, ALU.mult).then_inc(DV.sem, DV.step("y_mean"))
            own("y_mean")

            def per_head(a):
                return a.rearrange("p (h t v) -> p h t v", h=2, v=1).to_broadcast([P, 2, NT, 64])

            nc.vector.tensor_tensor(y4, yb, per_head(ast[:, 40:48]), ALU.add).then_inc(DV.sem, DV.step("y_c"))
            own("y_c")
            nc.vector.tensor_tensor(ysq[:], yc[:], yc[:], ALU.mult).then_inc(DV.sem, DV.step("y_sq"))
            own("y_sq")
            nc.vector.tensor_reduce(ast[:, 32:40], ysq[:].rearrange("p (u v) -> p u v", v=64), AX.X, ALU.add).then_inc(
                DV.sem, DV.step("y_var"))
            dve.wait_ge(AC.sem, AC.reached(j, "y_sd"))
            nc.vector.reciprocal(ast[:, 32:40], ast[:, 40:48]).then_inc(DV.sem, DV.step("y_rs"))
            own("y_rs")
            nc.vector.tensor_tensor(yn[:].rearrange("p (t h v) -> p h t v", h=2, v=64), y4, per_head(ast[:, 32:40]),
                                    ALU.mult).then_inc(DV.sem, DV.step("y_n"))
            dve.wait_ge(PE.sem, PE.reached(j, "y_turn"))
            nc.vector.tensor_scalar(kk, bank(7), par[:, 8:9], par[:, 9:10], ALU.mult, ALU.add).then_inc(DV.sem, DV.step("ot1"))
            own("ot1")
            nc.vector.tensor_tensor(kk, kk, r_, ALU.add).then_inc(DV.sem, DV.step("ot2"))
            own("ot2")
            nc.vector.tensor_tensor(o_t[:, bass.ds(j + HEADS, 1), :].rearrange("p a s -> p (a s)"), kk, gate[:], ALU.mult).then_inc(
                DV.sem, DV.step("ot3"))

    @block.tensor
    def _(pe):
        pe.wait_ge(AC.sem, AC.ahead())
        pe.sem_inc(PE.sem, PE.ahead())
        with pe.Fori(0, HEADS) as j:
            pe.wait_ge(s_lora, j * 32 + 32)

            def dv(name):
                pe.wait_ge(DV.sem, DV.reached(j, name))

            def ac(name):
                pe.wait_ge(AC.sem, AC.reached(j, name))

            def scores(i):
                n = (i + 1) * P
                for c in range(2):
                    rows = slice(64 * c, 64 * c + 64)
                    last = nc.tensor.matmul(bank(6 + c, 0, n), qr[rows, i * P:(i + 1) * P], kro[rows, 0:n], start=True, stop=True)
                last.then_inc(PE.sem, PE.step(f"score{i}"))

            def turn_weights(i):
                dv(f"a{i}")
                for b in range(i + 1):
                    last = nc.tensor.transpose(bank(6, b * P, b * P + P), am[:, b * P:(b + 1) * P], ident)
                last.then_inc(PE.sem, PE.step(f"a_turn{i}"))

            def output(i):
                ac(f"a_major{i}")
                for b in range(i + 1):
                    last = nc.tensor.matmul(bank(7, 0, P), at_[:, b * P:(b + 1) * P], vm[:, b, :], start=b == 0, stop=b == i)
                last.then_inc(PE.sem, PE.step(f"o{i}"))

            nc.tensor.matmul(bank(4), lj[0:64, 0, :], wa[0:64, :], start=True, stop=True).then_inc(PE.sem, PE.step("lora_w"))
            nc.tensor.matmul(bank(5), lj[64:128, 0, :], wa[64:128, :], start=True, stop=True).then_inc(PE.sem, PE.step("lora_a"))
            ac("kk_sq")
            nc.tensor.matmul(bank(7), con("heads"), sq[:], start=True, stop=True).then_inc(PE.sem, PE.step("kk_sum"))
            nc.tensor.matmul(bank(6), lj[:, 1, :], sg[:], start=True, stop=True).then_inc(PE.sem, PE.step("lora_g"))

            def turned(name, b, src):
                for t in range(NT):
                    last = nc.tensor.transpose(bank(b, t * P, t * P + P), src(t), ident)
                last.then_inc(PE.sem, PE.step(name))

            def cross(a, b0, src, h):
                rows = slice(64 * h, 64 * h + 64)
                for t in range(NT):
                    c0 = (t % 2) * 2 * P
                    last = nc.tensor.matmul(bank(b0 + t // 2, c0, c0 + 2 * P), src[rows, t * P:(t + 1) * P],
                                            kr[rows, t, :, :].rearrange("p a c -> p (a c)"), start=True, stop=True)
                last.then_inc(PE.sem, PE.step(f"m{a}{h}"))

            ac("v_copy")
            turned("v_turn", 2, lambda t: vf[:, t * P:(t + 1) * P])
            dv("kk")
            nc.tensor.matmul(bank(0), con("swap"), tile_of(0, j), start=True, stop=True)
            nc.tensor.matmul(bank(1), con("swap"), tile_of(1, j), start=True, stop=True).then_inc(PE.sem, PE.step("rope_swap"))
            dv("rhat")
            cross("b", 0, beta, 0)
            dv("khat")
            ac("v_major")
            cross("k", 2, khat, 0)
            turned("t_kappa", 6, lambda t: kr[:, t, 0, :])
            dv("emb0")
            cross("b", 0, beta, 1)
            dv("x1b0")
            turned("x_turn0", 4, lambda t: xx[:, 0, t, 1, :])
            dv("emk0")
            cross("k", 2, khat, 1)
            turned("t_beta", 7, lambda t: beta[:, t * P:(t + 1) * P])
            dv("x1b1")
            turned("x_turn1", 5, lambda t: xx[:, 1, t, 1, :])
            ac("e_beta")
            nc.tensor.matmul(bank(7), con("heads"), r_, start=True, stop=True).then_inc(PE.sem, PE.step("bonus"))
            turned("t_khat", 6, lambda t: khat[:, t * P:(t + 1) * P])
            for lv in range(5):
                for h in range(2):
                    if lv == 0:
                        ac(f"x_major{h}")
                    else:
                        dv(f"ex{lv - 1}_{h}")
                    for t in range(NT):
                        last = nc.tensor.matmul(bank(4 + h, t * P, t * P + P), ab[:, h, t, 0, :], xx[:, h, t, 0, :], start=True, stop=True)
                    last.then_inc(PE.sem, PE.step(f"t{lv}_{h}"))
                if not lv:
                    ac("e_khat")
                    turned("t_v", 6, lambda t: v_[:, t * P:(t + 1) * P])
                for h in range(2):
                    dv(f"et{lv}_{h}")
                    for t in range(NT):
                        b, c0 = 2 * h + t // 2, (t % 2) * 2 * P
                        if lv < 4:
                            nc.tensor.matmul(bank(b, c0, c0 + P), xx[:, h, t, 1, :], t1[:, h, t, :], start=True, stop=True)
                        last = nc.tensor.matmul(bank(b, c0 + P, c0 + 2 * P), t1[:, h, t, :], xx[:, h, t, 1, :], start=True, stop=True)
                    last.then_inc(PE.sem, PE.step(f"x{lv}_{h}"))
                    if lv:
                        (output if h else turn_weights)(lv - 1)
                if lv < NT:
                    if not lv:
                        dv("bon")
                    ac(f"o_copy{lv - 1}" if lv else "e_v")
                    scores(lv)
            dv("ex4_1")
            for h in range(2):
                for t in range(NT):
                    u = h * NT + t
                    last = nc.tensor.matmul(bank(4, u * 64, u * 64 + 64), ak[:, h, t, 0, :], vt[:, t, 64 * h:64 * h + 64], start=True, stop=True)
            last.then_inc(PE.sem, PE.step("akv"))
            dv("o_n")
            for t in range(NT):
                last = nc.tensor.transpose(bank(6, t * P, t * P + P), on[:, t * P:(t + 1) * P], ident)
            last.then_inc(PE.sem, PE.step("o_turn"))
            ac("e_akv")
            for h in range(2):
                for t in range(NT):
                    last = nc.tensor.matmul(bank(5 * (1 - h), t * P, t * P + P), xx[:, h, t, 1, :], rh[:, h, t, :], start=True, stop=True)
                last.then_inc(PE.sem, PE.step(f"wu{h}"))
            ac("e_wu1")
            for h in range(2):
                for t in range(NT):
                    last = nc.tensor.matmul(bank(3, t * P, t * P + P, slice(64 * h, 64 * h + 64)), wu[:, h, t, 0:64], ab[:, h, t, 1, :],
                                            start=True, stop=True)
            last.then_inc(PE.sem, PE.step("q"))
            for c in range(2):
                tok = slice(64 * c, 64 * c + 64)
                for h in range(2):
                    hs, rows = slice(64 * h, 64 * h + 64), slice(64 * h, 64 * h + 64)
                    for t in range(NT):
                        nc.tensor.matmul(bank(c, t * 64, t * 64 + 64, rows), wu[tok, h, t, 0:64], bn[tok, t, hs], start=True, stop=True)
                        o = bank(c, 256 + t * 64, 320 + t * 64, rows)
                        nc.tensor.matmul(o, kh[tok, t, hs], vt[tok, t, hs], start=True, stop=False)
                        last = nc.tensor.matmul(o, bn[tok, t, hs], wu[tok, h, t, 64:128], start=False, stop=True)
            last.then_inc(PE.sem, PE.step("chunk"))

            def y_within(u):
                h, t = u // NT, u % NT
                o = bank(4 + h, t * 64, t * 64 + 64)
                nc.tensor.matmul(o, ak[:, h, t, 1, :], vt[:, t, 64 * h:64 * h + 64], start=t == 0, stop=False)
                nc.tensor.matmul(o, ab[:, h, t, 1, :], wu[:, h, t, 64:128], start=False, stop=False)

            y_within(0)
            y_within(1)
            for c in range(1, 7):
                dv(f"z{c}")
                nc.tensor.matmul(bank(2, c * 64, c * 64 + 64), gt[:, c, :], zz[:, c, :], start=True, stop=True).then_inc(
                    PE.sem, PE.step(f"z{c}"))
                if c < 6:
                    y_within(c + 1)
            dv("z7")
            y_within(7)
            for h in range(2):
                rows = slice(64 * h, 64 * h + 64)
                for t in range(NT):
                    for c in range(2):
                        tok = slice(64 * c, 64 * c + 64)
                        last = nc.tensor.matmul(bank(4 + h, t * 64, t * 64 + 64, tok), qt[rows, t, tok], zz[rows, 2 * t + c, :],
                                                start=False, stop=t == NT - 1)
            last.then_inc(PE.sem, PE.step("y"))
            dv("y_n")
            for t in range(NT):
                last = nc.tensor.transpose(bank(7, t * P, t * P + P), yn[:, t * P:(t + 1) * P], ident)
            last.then_inc(PE.sem, PE.step("y_turn"))


def piece_source(d, e, p):
    half, k = p // 4, p % 4
    src = (d["mlp1_w"][0][bass.ds(e, 1), k * 256:(k + 1) * 256, half * D:(half + 1) * D] if half < 2
           else d["mlp2_w"][0][bass.ds(e, 1), k * 256:(k + 1) * 256, :])
    return src.rearrange("e (r p) n -> p (e r) n", p=P)


def output_and_route(nc, d, sb, sem, st, g, con, ident, psum, bank):
    x, stat, o_t, rank, info, flags, raw, bias = (g[k] for k in ("x", "stat", "o_t", "rank", "info", "flags", "raw", "bias"))
    s_w = [sem(f"w_out_loaded{k}") for k in range(KT)]
    s_rw, s_fw, s_oh, s_ol = sem("router_loaded"), sem("ffn_norm_loaded"), sem("o_hi"), sem("o_lo")
    s_wh, s_wl, s_acc, s_x2, s_ss = sem("w_out_hi"), sem("w_out_lo"), sem("out_projected"), sem("x2_ready"), sem("x2_squared")
    s_sd, s_rs, s_h2, s_store = sem("x2_deviation"), sem("x2_rstd"), sem("h2_ready"), sem("h2_stored")
    s_turn, s_h2t, s_log, s_rt = sem("h2_turned"), sem("h2t_ready"), sem("logits_ready"), sem("route_steps")
    s_exp, s_mask, s_rank, s_lgt = sem("gate_exp"), sem("choice_mask"), sem("ranks_ready"), sem("logits_copied")
    s_bl, s_bh, s_bias, s_z = sem("bias_loaded"), sem("bias_hi"), sem("bias_split"), sem("bias_zeroed")
    raw_flat = raw[:].rearrange("p a b n -> p (a b n)")
    bias_raw = raw_flat[:, 0:3 * D]
    fw = raw_flat[:, 3 * D:4 * D]
    wo = raw_flat[:, 4 * D:(4 + KT) * D].rearrange("p (k n) -> p k n", n=D)
    wh = sb(st, "wo_hi", [P, KT, D], F32R)
    wl = sb(st, "wo_lo", [P, KT, D], F32R)
    oh = sb(st, "o_hi_sb", [P, KT, S], F32R)
    ol = sb(st, "o_lo_sb", [P, KT, S], F32R)
    h2 = wo[:, 0:4, :]
    h2t = wo[:, 4:8, :].rearrange("p a (b s) -> p (a b) s", s=S)
    rw = sb(st, "rw", [P, KT, EXPERTS])
    rb = sb(st, "rb", [EXPERTS, 1])
    idx8 = sb(st, "idx8", [P, NT, 8], U32)
    r1 = sb(st, "r1", [P, 32])
    table = o_t[:].rearrange("p k s -> p (k s)")
    at = 0

    def carve(rows, *dims):
        nonlocal at
        n = int(np.prod(dims))
        at += n
        names = "abc"[:len(dims)]
        return table[0:rows, at - n:at].rearrange(f"p ({' '.join(names)}) -> p {' '.join(names)}",
                                                  **dict(zip(names[1:], dims[1:])))

    lgt = carve(EXPERTS, S)
    lg = carve(P, NT, EXPERTS)
    top8 = carve(P, NT, 8)
    idxf = carve(P, NT, 8)
    one = carve(P, 4, NT, EXPERTS)
    mask = carve(P, NT, EXPERTS)
    which = carve(P, NT, EXPERTS)
    eg = carve(P, NT, EXPERTS)
    w_v = d["w_out"][0].rearrange("(k p) n -> p k n", p=P)
    block = st.enter_context(nc.Block())

    def flat(t):
        return psum[:, 2 * t:2 * t + 2, :].rearrange("p b n -> p (b n)")

    @block.sync
    def _(sp):
        for k in range(KT):
            sp.dma_start(wo[:, k, :], w_v[:, k, :]).then_inc(s_w[k], 16)
        for rows in (slice(0, 32), slice(32, 64)):
            for w, c0, n in (("mlp1_b", 0, 2 * D), ("mlp2_b", 2 * D, D)):
                sp.dma_start(bias_raw[rows, c0:c0 + n], d[w][0]).then_inc(s_bl, 16)
        sp.wait_ge(s_bias, 1)
        sp.wait_ge(s_store, 16 * NT)
        sp.wait_ge(s_turn, NT)
        sp.wait_ge(s_log, 1)
        for p in range(RAW):
            sp.dma_start(raw[:, p], piece_source(d, 0, p)).then_inc(g["s_raw"][p], 16)

    @block.gpsimd
    def _(pool):
        nc.gpsimd.memset(bias[64:128, :].bitcast(F32), 0.0).then_inc(s_z, 1)
        nc.gpsimd.dma_start(fw[:], d["ffn_norm_w"].to_broadcast([P, D])).then_inc(s_fw, 16)
        nc.gpsimd.dma_start(rw[:], d["router_w"][0].rearrange("(k p) e -> p k e", p=P)).then_inc(s_rw, 16)
        nc.gpsimd.dma_start(rb[:], d["router_b"].rearrange("a e -> e a")).then_inc(s_rw, 16)
        for t in range(NT):
            pool.wait_ge(s_h2, t + 1)
            nc.gpsimd.dma_start(g["h2_dram"][t * P:(t + 1) * P, :], h2[:, t, :]).then_inc(s_store, 16)
        pool.wait_ge(s_store, 16 * NT)
        pool.wait_ge(s_z, 1)

    @block.scalar
    def _(act):
        for k in range(KT):
            nc.scalar.activation(oh[:, k, :], o_t[:, k, :], ACT.Copy).then_inc(s_oh, 1)
            act.wait_ge(s_w[k], 16)
            nc.scalar.activation(wh[:, k, :], wo[:, k, :], ACT.Copy).then_inc(s_wh, 1)
        act.wait_ge(s_bl, 64)
        nc.scalar.activation(bias[0:64, :], bias_raw[0:64, :], ACT.Copy).then_inc(s_bh, 1)
        act.wait_ge(s_wl, KT)

        def deviation(t):
            act.wait_ge(s_x2, t + 1)
            nc.scalar.activation(h2[:, t, :], x[:, t, :], ACT.Square, accum_out=stat[:, 24 + t:25 + t]).then_inc(s_ss, 1)
            act.wait_ge(s_ss, t + 1)
            nc.scalar.activation(stat[:, 28 + t:29 + t], stat[:, 24 + t:25 + t], ACT.Sqrt, bias=con("eps"), scale=1.0 / D).then_inc(s_sd, 1)

        def turned(t):
            act.wait_ge(s_turn, t + 1)
            nc.scalar.activation(h2t[:, :, t * P:(t + 1) * P], flat(t).rearrange("p (k c) -> p k c", c=P), ACT.Copy).then_inc(s_h2t, 1)

        deviation(0)
        deviation(1)
        turned(0)
        turned(1)
        for t in (2, 3):
            deviation(t)
            turned(t)
        act.wait_ge(s_rt, 9)
        for t in range(NT):
            last = nc.scalar.activation(eg[:, t, :], lg[:, t, :], ACT.Exp, bias=r1[:, t:t + 1])
        last.then_inc(s_exp, 1)

    @block.vector
    def _(dve):
        nc.vector.memset(info[:], 0.0)
        nc.vector.memset(rank[:], -1e6)
        for k in range(KT):
            dve.wait_ge(s_oh, k + 1)
            nc.vector.tensor_tensor(ol[:, k, :], o_t[:, k, :], oh[:, k, :].bitcast(F32), ALU.subtract).then_inc(s_ol, 1)
            dve.wait_ge(s_wh, k + 1)
            nc.vector.tensor_tensor(wl[:, k, :], wo[:, k, :], wh[:, k, :].bitcast(F32), ALU.subtract).then_inc(s_wl, 1)
        dve.wait_ge(s_bh, 1)
        nc.vector.tensor_tensor(bias[32:64, :], bias_raw[32:64, :], bias[32:64, :].bitcast(F32), ALU.subtract).then_inc(s_bias, 1)
        dve.wait_ge(s_fw, 16)
        for t in range(NT):
            dve.wait_ge(s_acc, t + 1)
            nc.vector.tensor_tensor(x[:, t, :], flat(t), x[:, t, :], ALU.add).then_inc(s_x2, 1)
            dve.wait_ge(s_sd, t + 1)
            nc.vector.reciprocal(stat[:, 32 + t:33 + t], stat[:, 28 + t:29 + t]).then_inc(s_rs, 1)
            dve.wait_ge(s_rs, t + 1)
            nc.vector.scalar_tensor_tensor(h2[:, t, :], x[:, t, :], stat[:, 32 + t:33 + t], fw[:], ALU.mult, ALU.mult).then_inc(s_h2, 1)
        n = 0

        def chain(ins):
            nonlocal n
            n += 1
            ins.then_inc(s_rt, 1)
            dve.wait_ge(s_rt, n)

        dve.wait_ge(s_rw, 32)
        dve.wait_ge(s_log, 1)
        nc.vector.tensor_scalar(lgt[:], bank(0, rows=slice(0, EXPERTS)), rb[:, 0:1], None, ALU.add).then_inc(s_lgt, 1)
        dve.wait_ge(s_log, 2)
        chain(nc.vector.tensor_copy(lg[:], bank(3, 0, NT * EXPERTS).rearrange("p (t e) -> p t e", e=EXPERTS)))
        for t in range(NT):
            nc.vector.max(top8[:, t, :], lg[:, t, :]).then_inc(s_rt, 1)
        n += NT
        dve.wait_ge(s_rt, n)
        for t in range(NT - 1):
            nc.vector.max_index(idx8[:, t, :], top8[:, t, :], lg[:, t, :]).then_inc(s_rt, 1)
        n += NT - 1
        nc.vector.max_index(idx8[:, NT - 1, :], top8[:, NT - 1, :], lg[:, NT - 1, :])
        chain(nc.vector.tensor_scalar(r1[:, 0:4], top8[:, :, 0], -1.0, None, ALU.mult))
        chain(nc.vector.tensor_copy(idxf[:], idx8[:]))
        for j in range(4):
            last = nc.vector.tensor_tensor(one[:, j], con("experts").rearrange("p (a e) -> p a e", a=1).to_broadcast([P, NT, EXPERTS]),
                                           idxf[:, :, j:j + 1].to_broadcast([P, NT, EXPERTS]), ALU.is_equal)
        chain(last)
        chain(nc.vector.tensor_tensor(mask[:], one[:, 0], one[:, 1], ALU.add))
        chain(nc.vector.tensor_tensor(mask[:], mask[:], one[:, 2], ALU.add))
        chain(nc.vector.tensor_tensor(mask[:], mask[:], one[:, 3], ALU.add))
        nc.vector.memset(r1[:, 31:32], 0.0).then_inc(s_mask, 1)
        chain(nc.vector.scalar_tensor_tensor(which[:], one[:, 2], 2.0, one[:, 1], ALU.mult, ALU.add))
        chain(nc.vector.scalar_tensor_tensor(which[:], one[:, 3], 3.0, which[:], ALU.mult, ALU.add))
        dve.wait_ge(s_exp, 1)
        chain(nc.vector.tensor_tensor(eg[:], eg[:], mask[:], ALU.mult))
        chain(nc.vector.tensor_reduce(r1[:, 4:8], eg[:], AX.X, ALU.add))
        chain(nc.vector.reciprocal(r1[:, 8:12], r1[:, 4:8]))
        nc.vector.tensor_tensor(info[:, :, 0:EXPERTS, 2], eg[:], r1[:, 8:12].rearrange("p (t a) -> p t a", a=1).to_broadcast([P, NT, EXPERTS]),
                                ALU.mult)
        chain(nc.vector.tensor_scalar(r1[:, 12:16], con("token"), 4.0, -BIG, ALU.mult, ALU.add))
        nc.vector.tensor_tensor(info[:, :, 0:EXPERTS, 1], which[:], r1[:, 12:16].rearrange("p (t a) -> p t a", a=1).to_broadcast([P, NT, EXPERTS]),
                                ALU.add)
        chain(nc.vector.tensor_scalar(r1[:, 16:20], con("token"), -BIG, None, ALU.add))
        nc.vector.tensor_copy(info[:, :, 0:EXPERTS, 0], r1[:, 16:20].rearrange("p (t a) -> p t a", a=1).to_broadcast([P, NT, EXPERTS]))
        chain(nc.vector.tensor_scalar(which[:], mask[:], 1e6, -1e6, ALU.mult, ALU.add))
        dve.wait_ge(s_rank, 1)
        nc.vector.tensor_tensor(rank[:, :, 0:EXPERTS], which[:], bank(1, 0, NT * EXPERTS).rearrange("p (t e) -> p t e", e=EXPERTS), ALU.add)
        chain(nc.vector.tensor_reduce(r1[:, 20:21], bank(1, NT * EXPERTS, (NT + 1) * EXPERTS), AX.X, ALU.max))
        for r in range(ROUNDS):
            last = nc.vector.tensor_scalar(flags[:, r:r + 1], r1[:, 20:21], float(P * r) if r else -1.0, None, ALU.is_gt)
        chain(last)

    @block.tensor
    def _(pe):

        def project_out(tiles, k):
            for t in tiles:
                for c in range(2):
                    for m, (o, w) in enumerate(((oh, wh), (oh, wl), (ol, wh))):
                        last = nc.tensor.matmul(bank(2 * t + c), o[:, k, t * P:(t + 1) * P], w[:, k, c * 512:(c + 1) * 512],
                                                start=k == 0 and m == 0, stop=k == KT - 1 and m == 2)
                if k == KT - 1:
                    last.then_inc(s_acc, 1)

        def turn(t):
            pe.wait_ge(s_h2, t + 1)
            for k in range(KT):
                last = nc.tensor.transpose(bank(2 * t + k // 4, (k % 4) * P, (k % 4) * P + P), h2[:, t, k * P:(k + 1) * P], ident)
            last.then_inc(s_turn, 1)

        def logits(t):
            pe.wait_ge(s_h2t, t + 1)
            for k in range(KT):
                last = nc.tensor.matmul(bank(0, t * P, t * P + P, slice(0, EXPERTS)), rw[:, k, :], h2t[:, k, t * P:(t + 1) * P],
                                        start=k == 0, stop=k == KT - 1)
            return last

        for k in range(KT):
            pe.wait_ge(s_ol, k + 1)
            pe.wait_ge(s_wl, k + 1)
            project_out((0, 1), k)
        for k in range(KT):
            project_out((2,), k)
        turn(0)
        turn(1)
        for k in range(KT):
            project_out((3,), k)
        pe.wait_ge(s_rw, 32)
        logits(0)
        logits(1)
        for t in (2, 3):
            turn(t)
            last = logits(t)
        last.then_inc(s_log, 1)
        pe.wait_ge(s_lgt, 1)
        for t in range(NT):
            last = nc.tensor.transpose(bank(3, t * EXPERTS, (t + 1) * EXPERTS), lgt[:, t * P:(t + 1) * P], ident[0:EXPERTS, 0:EXPERTS])
        last.then_inc(s_log, 1)
        pe.wait_ge(s_mask, 1)
        for t in range(NT):
            o = bank(1, t * EXPERTS, (t + 1) * EXPERTS)
            for u in range(t):
                nc.tensor.matmul(o, con("ones"), mask[:, u, :], start=u == 0, stop=False)
            nc.tensor.matmul(o, con("before"), mask[:, t, :], start=t == 0, stop=True)
        for u in range(NT):
            last = nc.tensor.matmul(bank(1, NT * EXPERTS, (NT + 1) * EXPERTS), con("ones"), mask[:, u, :], start=u == 0, stop=u == NT - 1)
        last.then_inc(s_rank, 1)


def experts(nc, d, sb, sem, st, g, con, ident, psum, bank):
    rank, info, flags, raw, bias, s_raw = (g[k] for k in ("rank", "info", "flags", "raw", "bias", "s_raw"))
    hi = sb(st, "w_pieces_hi", [P, RING, 2, D], F32R)
    lo = sb(st, "w_pieces_lo", [P, RING, 2, D], F32R)
    xg = sb(st, "xg", [P, D])
    xh = sb(st, "xh", [P, KT, P], F32R)
    xl = sb(st, "xl", [P, KT, P], F32R)
    ah = sb(st, "ah", [P, KT, P], F32R)
    al = sb(st, "al", [P, KT, P], F32R)
    gg = sb(st, "gg", [P, 512])
    uu = sb(st, "uu", [P, 512])
    sg = sb(st, "sig", [P, 512])
    av = sb(st, "av", [P, 512])
    ys = sb(st, "ys", [P, D])
    sel = sb(st, "sel", [P, NT, P])
    pick = sb(st, "pick_e", [P, P], F32R)
    next_i = sb(st, "next_i", [P, 2], I32)
    next_g = sb(st, "next_g", [P, 1])
    this_i = sb(st, "this_i", [P, 1], I32)
    this_g = sb(st, "this_g", [P, 1])
    s_hi, s_lo, s_used = sem("piece_hi"), sem("piece_lo"), sem("piece_used")
    s_z = sem("rows_zeroed")
    s_sel, s_imm, s_idx, s_copy, s_pick = sem("selected"), sem("index_summed"), sem("index_ready"), sem("index_moved"), sem("bias_row_picked")
    s_gath, s_tx, s_xh, s_xl = sem("rows_gathered"), sem("rows_turned"), sem("x_hi"), sem("x_lo")
    s_g, s_u, s_sig, s_act = sem("gate_clipped"), sem("up_steps"), sem("gate_sigmoid"), sem("act_ready")
    s_ta, s_ah, s_al, s_y, s_scat = sem("act_turned"), sem("act_hi"), sem("act_lo"), sem("y_ready"), sem("rows_scattered")
    s_round, s_stored, s_part = sem("round_moved"), sem("rows_stored"), sem("dma_about_to_start")
    block = st.enter_context(nc.Block())

    def rounds(eng, run):
        with eng.Fori(0, ROUNDS) as r:
            flag = eng.value_load(flags[0:1, bass.ds(r, 1)])
            with eng.If(flag == 1):
                run(r)

    @block.sync
    def _(sp):
        def load(r, e, p):
            sp.wait_ge(s_lo, (r * EXPERTS + e) * PIECES + (p + 1))
            sp.dma_start(raw[:, p % RAW], piece_source(d, e, p)).then_inc(s_raw[p], 16)

        def rest(r):
            with sp.Fori(0, EXPERTS - 1) as e:
                for p in range(RAW, PIECES):
                    load(r, e, p)
                for p in range(RAW):
                    load(r, e + 1, p)
            for p in range(RAW, PIECES):
                load(r, EXPERTS - 1, p)

        rest(0)
        with sp.Fori(1, ROUNDS) as r:
            flag = sp.value_load(flags[0:1, bass.ds(r, 1)])
            with sp.If(flag == 1):
                for p in range(RAW):
                    load(r, 0, p)
                rest(r)

    @block.gpsimd
    def _(pool):
        nc.gpsimd.memset(xg[:], 0.0).then_inc(s_z, 1)
        pool.wait_ge(s_z, 1)
        pool.sem_inc(s_stored, 1)

        def part_waits():
            pool.sem_inc(s_part, 1)

        def gather(m):
            pool.wait_ge(s_idx, m + 1)
            pool.wait_ge(s_tx, m * 2 + 1)
            part_waits()
            nc.gpsimd.indirect_dma_start(xg[:], None, g["h2_dram"], bass.IndirectOffsetOnAxis(next_i[:, 0:1], 0),
                                         bounds_check=S - 1, oob_is_err=False).then_inc(s_gath, 16)

        def scatter(turn):
            pool.wait_ge(s_copy, turn + 1)
            pool.wait_ge(s_y, turn + 2)
            part_waits()
            nc.gpsimd.indirect_dma_start(g["y_dram"], bass.IndirectOffsetOnAxis(this_i[:, 0:1], 0), ys[:], None,
                                         bounds_check=4 * S - 1, oob_is_err=False).then_inc(s_scat, 16)
            pool.wait_ge(s_scat, turn * 16 + 16)
            pool.sem_inc(s_stored, 1)

        def run(r):
            gather(r * TURNS)
            gather(r * TURNS + 1)
            with pool.Fori(1, EXPERTS) as e:
                scatter(r * EXPERTS + (e - 1))
                gather(r * TURNS + (e + 1))
            scatter(r * EXPERTS + (EXPERTS - 1))

        rounds(pool, run)

    @block.scalar
    def _(act):
        act.sem_inc(s_y, 1)

        def split(turn, p):
            act.wait_ge(s_raw[p], turn * 16 + 16)
            act.wait_ge(s_used, turn * PIECES + (p + 1))
            nc.scalar.activation(hi[:, p % RING], raw[:, p % RAW], ACT.Copy).then_inc(s_hi, 1)

        def x_hi(m, q):
            act.wait_ge(s_tx, m * 2 + (q + 2))
            nc.scalar.activation(xh[:, 4 * q:4 * q + 4, :].rearrange("p a b -> p (a b)"), bank(7), ACT.Copy).then_inc(s_xh, 1)

        def sigmoid(turn, h):
            act.wait_ge(s_g, turn * 2 + (h + 1))
            nc.scalar.activation(sg[:], gg[:], ACT.Sigmoid, scale=1.702).then_inc(s_sig, 1)

        def a_hi(turn, h):
            act.wait_ge(s_ta, turn * 2 + (h + 2))
            nc.scalar.activation(ah[:, 4 * h:4 * h + 4, :].rearrange("p a b -> p (a b)"), bank(6), ACT.Copy).then_inc(s_ah, 1)

        def y_out(turn):
            act.wait_ge(s_used, turn * PIECES + (PIECES + RING))
            act.wait_ge(s_copy, turn + 1)
            act.wait_ge(s_stored, turn + 1)
            nc.scalar.activation(ys[:], psum[:, 4:6, :].rearrange("p b n -> p (b n)"), ACT.Copy, scale=this_g[:, 0:1]).then_inc(s_y, 1)

        def body(r, e, first):
            turn = r * EXPERTS + e
            for p in range(PIECES):
                split(turn, p)
                if p == 1 and first:
                    x_hi(r * TURNS, 0)
                    x_hi(r * TURNS, 1)
                elif p == 1:
                    y_out(r * EXPERTS + (e - 1))
                if p == 6:
                    sigmoid(turn, 0)
                if p == 7:
                    a_hi(turn, 0)
                if p == 8:
                    x_hi(r * TURNS + (e + 1), 0)
                if p == 9:
                    sigmoid(turn, 1)
                if p == 10:
                    a_hi(turn, 1)
                    x_hi(r * TURNS + (e + 1), 1)

        def run(r):
            body(r, 0, True)
            with act.Fori(1, EXPERTS) as e:
                body(r, e, False)
            y_out(r * EXPERTS + (EXPERTS - 1))

        rounds(act, run)

    @block.vector
    def _(dve):
        dve.sem_inc(s_lo, RAW)
        dve.sem_inc(s_round, 1)
        dve.sem_inc(s_xl, 1)
        dve.sem_inc(s_act, 1)
        dve.sem_inc(s_al, 1)

        def split(turn, p):
            dve.wait_ge(s_hi, turn * PIECES + (p + 1))
            nc.vector.tensor_tensor(lo[:, p % RING], raw[:, p % RAW], hi[:, p % RING].bitcast(F32), ALU.subtract).then_inc(s_lo, 1)

        def select(m, e):
            dve.wait_ge(s_imm, m + 1)
            nc.vector.tensor_tensor(sel[:], con("slot").rearrange("p (a n) -> p a n", a=1).to_broadcast([P, NT, P]),
                                    rank[:, :, bass.ds(e, 1)].to_broadcast([P, NT, P]), ALU.is_equal).then_inc(s_sel, 1)

        def indices(m):
            dve.wait_ge(s_imm, m + 2)
            dve.wait_ge(s_tx, m * 2 + 1)
            nc.vector.tensor_scalar(next_i[:], bank(4, 0, 2), BIG, None, ALU.add)
            nc.vector.tensor_copy(next_g[:], bank(4, 2, 3)).then_inc(s_idx, 1)

        def move_indices(turn, m):
            dve.wait_ge(s_stored, turn + 1)
            dve.wait_ge(s_idx, m + 1)
            nc.vector.tensor_copy(this_i[:], next_i[:, 1:2])
            nc.vector.tensor_copy(this_g[:], next_g[:]).then_inc(s_copy, 1)

        def pick_bias(e, used):
            dve.wait_ge(s_used, used)
            nc.vector.tensor_copy(pick[:], con("pick")[:, bass.ds(e, 1)].to_broadcast([P, P])).then_inc(s_pick, 1)

        def x_lo(m, q):
            dve.wait_ge(s_xh, m * 2 + (q + 1))
            x4 = xh[:, 4 * q:4 * q + 4, :].rearrange("p a b -> p (a b)")
            nc.vector.tensor_tensor(xl[:, 4 * q:4 * q + 4, :].rearrange("p a b -> p (a b)"), bank(7), x4.bitcast(F32),
                                    ALU.subtract).then_inc(s_xl, 1)

        def a_lo(turn, h):
            dve.wait_ge(s_ah, turn * 2 + (h + 1))
            a4 = ah[:, 4 * h:4 * h + 4, :].rearrange("p a b -> p (a b)")
            nc.vector.tensor_tensor(al[:, 4 * h:4 * h + 4, :].rearrange("p a b -> p (a b)"), bank(6), a4.bitcast(F32),
                                    ALU.subtract).then_inc(s_al, 1)

        def swiglu(turn, h):
            dve.wait_ge(s_used, turn * PIECES + (4 * h + 4 + RING))
            pair = psum[:, 2 * h:2 * h + 2, :].rearrange("p b (n two) -> p (b n) two", two=2)
            nc.vector.tensor_scalar(gg[:], pair[:, :, 0], 7.0, None, ALU.min).then_inc(s_g, 1)
            nc.vector.tensor_scalar(uu[:], pair[:, :, 1], 7.0, -7.0, ALU.min, ALU.max).then_inc(s_u, 1)
            dve.wait_ge(s_g, turn * 2 + (h + 1))
            dve.wait_ge(s_u, turn * 4 + (2 * h + 1))
            nc.vector.scalar_tensor_tensor(uu[:], uu[:], 1.0, gg[:], ALU.add, ALU.mult).then_inc(s_u, 1)
            dve.wait_ge(s_u, turn * 4 + (2 * h + 2))
            dve.wait_ge(s_sig, turn * 2 + (h + 1))
            dve.wait_ge(s_ta, turn * 2 + (h + 1))
            nc.vector.tensor_tensor(av[:], uu[:], sg[:], ALU.mult).then_inc(s_act, 1)

        def body(r, e, first):
            turn = r * EXPERTS + e
            m = r * TURNS + (e + 1)
            for p in range(PIECES):
                split(turn, p)
                if p == 1:
                    if first:
                        x_lo(r * TURNS, 0)
                        x_lo(r * TURNS, 1)
                    select(m, e + 1)
                if p == 4:
                    move_indices(turn, r * TURNS + e)
                    dve.wait_ge(s_copy, turn + 1)
                    indices(m)
                if p == 5:
                    swiglu(turn, 0)
                if p == 7:
                    a_lo(turn, 0)
                if p == 8:
                    swiglu(turn, 1)
                    x_lo(m, 0)
                if p == 10:
                    a_lo(turn, 1)
                    x_lo(m, 1)
                    pick_bias(e + 1, turn * PIECES + (9 + RING))

        def run(r):
            dve.wait_ge(s_round, r + 1)
            select(r * TURNS, 0)
            indices(r * TURNS)
            pick_bias(0, r * (EXPERTS * PIECES) + RING)
            body(r, 0, True)
            with dve.Fori(1, EXPERTS) as e:
                body(r, e, False)
            nc.vector.tensor_scalar(rank[:], rank[:], float(-P), None, ALU.add).then_inc(s_round, 1)

        rounds(dve, run)

    @block.tensor
    def _(pe):
        pe.wait_ge(s_z, 1)
        pe.sem_inc(s_used, RING)
        pe.sem_inc(s_imm, 1)
        pe.sem_inc(s_tx, 1)
        pe.sem_inc(s_ta, 1)

        def index_sum(m, e, turn):
            pe.wait_ge(s_sel, m + 1)
            pe.wait_ge(s_y, turn + 1)
            for t in range(NT):
                last = nc.tensor.matmul(bank(4, 0, 4), sel[:, t, :], info[:, t, bass.ds(e, 1), :].rearrange("p a c -> p (a c)"),
                                        start=t == 0, stop=t == NT - 1)
            last.then_inc(s_imm, 1)

        def turn_x(m, q):
            if q == 0:
                pe.wait_ge(s_gath, m * 16 + 16)
            pe.wait_ge(s_xl, m * 2 + (q + 1))
            for k in range(4):
                last = nc.tensor.transpose(bank(7, k * P, k * P + P), xg[:, (4 * q + k) * P:(4 * q + k + 1) * P], ident)
            last.then_inc(s_tx, 1)

        def turn_a(turn, h):
            pe.wait_ge(s_act, turn * 2 + (h + 2))
            pe.wait_ge(s_al, turn * 2 + (h + 1))
            for k in range(4):
                last = nc.tensor.transpose(bank(6, k * P, k * P + P), av[:, k * P:(k + 1) * P], ident)
            last.then_inc(s_ta, 1)

        def piece(turn, p, ops, b0, k0, first, last_piece):
            if first:
                for c in range(2):
                    nc.tensor.matmul(bank(b0 + c), pick[:], bias[:, (b0 + c) * 512:(b0 + c + 1) * 512], start=True, stop=False)
            pe.wait_ge(s_lo, turn * PIECES + (p + 1 + RAW))
            for r2 in range(2):
                for c in range(2):
                    w = [a[:, p % RING, r2, c * 512:(c + 1) * 512] for a in (hi, lo)]
                    a = [o[:, k0 + r2, :] for o in ops]
                    nc.tensor.matmul(bank(b0 + c), a[0], w[0], start=False, stop=False)
                    nc.tensor.matmul(bank(b0 + c), a[0], w[1], start=False, stop=False)
                    last = nc.tensor.matmul(bank(b0 + c), a[1], w[0], start=False, stop=last_piece and r2 == 1)
            last.then_inc(s_used, 1)

        def body(r, e):
            turn = r * EXPERTS + e
            m = r * TURNS + (e + 1)
            pe.wait_ge(s_xl, m * 2 + 1)
            pe.wait_ge(s_pick, m)
            pe.wait_ge(s_act, turn * 2 + 1)
            for p in range(8):
                piece(turn, p, (xh, xl), 2 * (p // 4), 2 * (p % 4), p % 4 == 0, p % 4 == 3)
                if p == 1:
                    index_sum(m, e + 1, turn)
                if p == 5:
                    turn_a(turn, 0)
            turn_x(m, 0)
            pe.wait_ge(s_al, turn * 2 + 2)
            pe.wait_ge(s_idx, m + 1)
            piece(turn, 8, (ah, al), 4, 0, True, False)
            turn_a(turn, 1)
            turn_x(m, 1)
            piece(turn, 9, (ah, al), 4, 2, False, False)
            pe.wait_ge(s_al, turn * 2 + 3)
            piece(turn, 10, (ah, al), 4, 4, False, False)
            piece(turn, 11, (ah, al), 4, 6, False, True)

        def run(r):
            index_sum(r * TURNS, 0, r * EXPERTS)
            turn_x(r * TURNS, 0)
            turn_x(r * TURNS, 1)
            body(r, 0)
            with pe.Fori(1, EXPERTS) as e:
                body(r, e)

        rounds(pe, run)


def combine(nc, d, sb, sem, st, g, con, out):
    x, stat, y_dram = g["x"], g["stat"], g["y_dram"]
    y4 = sb(st, "y4", [P, NT, 4, D])
    sqr = sb(st, "sqr", [P, D])
    fw = sb(st, "final_w", [P, D])
    s_y = [sem(f"y_loaded{t}") for t in range(NT - 1)]
    s_y_last = [sem(f"y_last_loaded{j}") for j in range(4)]
    s_fw, s_add, s_ss, s_sd, s_rs, s_o, s_out = (sem(n) for n in ("final_w_loaded", "rows_added", "x3_squared", "x3_deviation",
                                                                  "x3_rstd", "out_ready", "out_stored"))
    block = st.enter_context(nc.Block())

    @block.sync
    def _(sp):
        rows = y_dram.rearrange("(t p j) n -> t p j n", p=P, j=4)
        for t in range(NT - 1):
            sp.dma_start(y4[:, t], rows[t]).then_inc(s_y[t], 16)
        for j in range(4):
            sp.dma_start(y4[:, NT - 1, j, :], rows[NT - 1, :, j, :]).then_inc(s_y_last[j], 16)
        for t in range(NT):
            sp.wait_ge(s_o, t + 1)
            sp.dma_start(out[0, t * P:(t + 1) * P, :], x[:, t, :]).then_inc(s_out, 16)
        sp.wait_ge(s_out, 16 * NT)

    @block.gpsimd
    def _(pool):
        nc.gpsimd.dma_start(fw[:], d["final_norm_w"].to_broadcast([P, D])).then_inc(s_fw, 16)

    @block.scalar
    def _(act):
        for t in range(NT):
            act.wait_ge(s_add, 4 * t + 4)
            nc.scalar.activation(sqr[:], x[:, t, :], ACT.Square, accum_out=stat[:, 40 + t:41 + t]).then_inc(s_ss, 1)
            act.wait_ge(s_ss, t + 1)
            nc.scalar.activation(stat[:, 44 + t:45 + t], stat[:, 40 + t:41 + t], ACT.Sqrt, bias=con("eps"), scale=1.0 / D).then_inc(s_sd, 1)

    @block.vector
    def _(dve):
        def finish(t):
            dve.wait_ge(s_sd, t + 1)
            nc.vector.reciprocal(stat[:, 48 + t:49 + t], stat[:, 44 + t:45 + t]).then_inc(s_rs, 1)
            dve.wait_ge(s_rs, t + 1)
            nc.vector.scalar_tensor_tensor(x[:, t, :], x[:, t, :], stat[:, 48 + t:49 + t], fw[:], ALU.mult, ALU.mult).then_inc(s_o, 1)

        for t in range(NT):
            for j in range(4):
                dve.wait_ge(s_y[t] if t < NT - 1 else s_y_last[j], 16)
                if j:
                    dve.wait_ge(s_add, 4 * t + j)
                nc.vector.tensor_tensor(x[:, t, :], x[:, t, :], y4[:, t, j, :], ALU.add).then_inc(s_add, 1)
            if t == 1:
                dve.wait_ge(s_fw, 16)
            if t:
                finish(t - 1)
        finish(NT - 1)


def kernel(x, positions, attn_norm_w, w_in, shift_mu, lambda_q1, lambda_k1, lambda_q2, lambda_k2, subln_w, rw_w0, rw_w2,
           rw_a0, rw_a2, rw_g2, rw_k_k, rw_k_a, rw_r_k, rw_lnx_w, rw_lnx_b, w_out, ffn_norm_w, router_w, router_b,
           mlp1_w, mlp1_b, mlp2_w, mlp2_b, final_norm_w):
    import concourse.bacc as bacc
    from concourse.bass_utils import run_bass_kernel_spmd as run

    def col(a):
        return np.asarray(a).reshape(-1, P).T

    mu = col(shift_mu)
    per_pair = [mu[:, 0:4], mu[:, 4:8], mu[:, 8:12]] + [col(a) for a in (rw_w0, rw_a0, rw_k_k, rw_k_a, rw_r_k, rw_lnx_w, rw_lnx_b)]
    pairs = np.stack(per_pair, 2).reshape(P, HEADS * NPAR)
    tables, _ = constant_tables()
    arrays = {
        "x": x, "positions": positions, "w_in": w_in, "w_out": w_out, "router_w": router_w, "router_b": router_b,
        "mlp1_w": mlp1_w, "mlp1_b": mlp1_b, "mlp2_w": mlp2_w, "mlp2_b": mlp2_b, "ffn_norm_w": ffn_norm_w,
        "final_norm_w": np.asarray(final_norm_w).reshape(1, D),
        "cols": np.concatenate([col(attn_norm_w), mu[:, 12:14], pairs, col(subln_w)], 1),
        "lam": np.concatenate([np.asarray(a) for a in (lambda_q1, lambda_k1, lambda_q2, lambda_k2)], 1),
        "w2a2": np.concatenate([np.asarray(rw_w2)[0], np.asarray(rw_a2)[0]], 0), "g2": np.asarray(rw_g2)[0],
        "cst": tables,
    }
    nc = bacc.Bacc("TRN2", target_bir_lowering=False, num_devices=1)
    feed, d = {}, {}
    for name, a in arrays.items():
        a = np.ascontiguousarray(a)
        feed[f"in_{name}"] = a
        d[name] = nc.dram_tensor(f"in_{name}", a.shape, mybir.dt.from_np(a.dtype), kind="ExternalInput").ap()
    out = nc.dram_tensor("out_0", (1, S, D), F32, kind="ExternalOutput").ap()
    build_program(nc, d, out)
    return run(nc, [feed], core_ids=[0]).results[0]["out_0"]
```
